# Optimizing a Trainium2 kernel written in Bass

```python
import math
import jax, jax.numpy as jnp
from jax import lax
import numpy as np

D_MODEL = 1024
BATCH = 1
SEQ = 256
DEPTH = 2
DEC_BATCH = 8
DEC_SEQ = 8
PAST_LEN = 1024
PAGE_SIZE = 128

HEAD_DIM = 64
N_MIX_HEADS = D_MODEL // HEAD_DIM
A_HEADS = 6
B_HEADS = 5
C_HEADS = N_MIX_HEADS - A_HEADS - B_HEADS
C_DK = 64
C_DV = HEAD_DIM
D_MIX = (A_HEADS + B_HEADS) * HEAD_DIM + C_HEADS * C_DV
D_FF = 2816
MOBA_BLOCK = 256
MOBA_TOPK = 3
MOBA_Q_BLOCK = 16
FOX_Q_BLOCK = 128
HGRN_CHUNK = 64
ROPE_THETA = 10000.0
FOX_BIAS_INIT = 2.0
EPS = 1e-6
NEG_BIG = -1e30
IN_SPLIT_SIZES = (A_HEADS * HEAD_DIM,) * 3 + (B_HEADS * HEAD_DIM,) * 3 + (B_HEADS,) + (C_HEADS * C_DK, C_HEADS * C_DK, C_HEADS * C_DV, C_HEADS * C_DV)
D_IN = sum(IN_SPLIT_SIZES)

kernel_name = 'hymba_moba_fox_hgrn2_macaron_step'

def _rmsnorm(x, g):
    x32 = x.astype(jnp.float32)
    y = x32 * lax.rsqrt(jnp.mean(x32 * x32, axis=-1, keepdims=True) + EPS)
    return (y * g.astype(jnp.float32)).astype(x.dtype)

def _swiglu(h, wg, wu, wd):
    return (jax.nn.silu(h @ wg) * (h @ wu)) @ wd

def _rope(x, pos0):
    T, hd = x.shape[1], x.shape[-1]
    half = hd // 2
    inv = ROPE_THETA ** (-jnp.arange(half, dtype=jnp.float32) * 2.0 / hd)
    ang = (pos0 + jnp.arange(T, dtype=jnp.float32))[:, None] * inv[None, :]
    cos = jnp.cos(ang)[None, :, None, :]
    sin = jnp.sin(ang)[None, :, None, :]
    x32 = x.astype(jnp.float32)
    x1, x2 = x32[..., :half], x32[..., half:]
    return jnp.concatenate([x1 * cos - x2 * sin, x1 * sin + x2 * cos], axis=-1).astype(x.dtype)

def _to_blocks(x, qb):
    B, T, H, d = x.shape
    return x.reshape(B, T // qb, qb, H, d).transpose(1, 0, 3, 2, 4)

def _from_blocks(o):
    n, B, H, qb, d = o.shape
    return o.transpose(1, 0, 3, 2, 4).reshape(B, n * qb, H, d)

def _moba_attend(q, k_all, v_all, pos0):
    B, T, H, hd = q.shape
    L = k_all.shape[1]
    nb = -(-L // MOBA_BLOCK)
    pad = nb * MOBA_BLOCK - L

    def blocks(a):
        a = jnp.pad(a, ((0, 0), (0, pad), (0, 0), (0, 0)))
        return a.reshape(B, nb, MOBA_BLOCK, H, hd).transpose(0, 3, 1, 2, 4)

    kb, vb = blocks(k_all), blocks(v_all)
    kmean = jnp.mean(kb.astype(jnp.float32), axis=3)
    topk = min(MOBA_TOPK, nb)
    qb = math.gcd(T, MOBA_Q_BLOCK)
    b_ix = jnp.arange(B)[:, None, None, None]
    h_ix = jnp.arange(H)[None, :, None, None]
    blk_ix = jnp.arange(nb)
    in_blk = jnp.arange(MOBA_BLOCK)
    scale = hd ** -0.5

    def step(args):
        qc, i = args
        t = pos0 + i * qb + jnp.arange(qb)
        own = t // MOBA_BLOCK
        gate = jnp.einsum('bhqd,bhnd->bhqn', qc.astype(jnp.float32), kmean)
        gate = jnp.where(blk_ix[None, :] < own[:, None], gate, NEG_BIG)
        _, sel = lax.top_k(gate, topk)
        idx = jnp.concatenate([sel.astype(jnp.int32), jnp.broadcast_to(own[None, None, :, None], (B, H, qb, 1)).astype(jnp.int32)], axis=-1)
        valid = jnp.concatenate([sel < own[:, None], jnp.ones((B, H, qb, 1), dtype=bool)], axis=-1)
        ks = kb[b_ix, h_ix, idx]
        vs = vb[b_ix, h_ix, idx]
        kpos = idx[..., None] * MOBA_BLOCK + in_blk
        mask = valid[..., None] & (kpos <= t[None, None, :, None, None])
        s = jnp.einsum('bhqd,bhqnkd->bhqnk', qc, ks).astype(jnp.float32) * scale
        s = jnp.where(mask, s, NEG_BIG)
        p = jax.nn.softmax(s.reshape(B, H, qb, -1), axis=-1).reshape(s.shape)
        return jnp.einsum('bhqnk,bhqnkd->bhqd', p.astype(vs.dtype), vs)

    o = lax.map(step, (_to_blocks(q, qb), jnp.arange(T // qb)))
    return _from_blocks(o)

def _fox_attend(q, k_all, v_all, logf_all, pos0):
    B, T, H, hd = q.shape
    L = k_all.shape[1]
    c = jnp.cumsum(logf_all.astype(jnp.float32), axis=1).transpose(0, 2, 1)
    kh = k_all.transpose(0, 2, 1, 3)
    vh = v_all.transpose(0, 2, 1, 3)
    qb = math.gcd(T, FOX_Q_BLOCK)
    kpos = jnp.arange(L)
    scale = hd ** -0.5

    def step(args):
        qc, i = args
        start = pos0 + i * qb
        t = start + jnp.arange(qb)
        ct = lax.dynamic_slice_in_dim(c, start, qb, axis=2)
        s = jnp.einsum('bhqd,bhkd->bhqk', qc, kh).astype(jnp.float32) * scale + ct[..., None] - c[:, :, None, :]
        s = jnp.where(kpos[None, :] <= t[:, None], s, NEG_BIG)
        p = jax.nn.softmax(s, axis=-1)
        return jnp.einsum('bhqk,bhkd->bhqd', p.astype(vh.dtype), vh)

    o = lax.map(step, (_to_blocks(q, qb), jnp.arange(T // qb)))
    return _from_blocks(o)

def _hgrn2_recurrence(q, k, v, logf, s0):
    T = q.shape[1]
    L = math.gcd(T, HGRN_CHUNK)
    causal = jnp.tril(jnp.ones((L, L), dtype=bool))

    def chunks(a):
        return _to_blocks(a.astype(jnp.float32), L)

    def step(S, inp):
        qc, kc, vc, gc = inp
        cum = jnp.cumsum(gc, axis=2)
        o_inter = jnp.einsum('bhld,bhde->bhle', qc * jnp.exp(cum), S)
        diff = cum[:, :, :, None, :] - cum[:, :, None, :, :]
        decay = jnp.exp(jnp.where(causal[None, None, :, :, None], diff, NEG_BIG))
        A = jnp.einsum('bhtd,bhtsd,bhsd->bhts', qc, decay, kc)
        o = o_inter + jnp.einsum('bhts,bhse->bhte', A, vc)
        last = cum[:, :, -1:, :]
        S_new = jnp.exp(last[:, :, 0, :])[..., None] * S + jnp.einsum('bhsd,bhse->bhde', kc * jnp.exp(last - cum), vc)
        return S_new, o

    S, o = lax.scan(step, s0.astype(jnp.float32), (chunks(q), chunks(k), chunks(v), chunks(logf)))
    return _from_blocks(o), S

def _token_mix(h, w_in, fox_b, lb, hgrn_g, w_out, past):
    B, T, _ = h.shape
    pos0 = 0 if past is None else past[0].shape[1]
    split_at = np.cumsum(IN_SPLIT_SIZES)[:-1].tolist()
    qa, ka, va, qf, kf, vf, ff, qc, fc, ic, gc = jnp.split(h @ w_in, split_at, axis=-1)

    def heads(a, n):
        return a.reshape(B, T, n, -1)

    qa = _rope(heads(qa, A_HEADS), pos0)
    ka = _rope(heads(ka, A_HEADS), pos0)
    va = heads(va, A_HEADS)
    qf, kf, vf = heads(qf, B_HEADS), heads(kf, B_HEADS), heads(vf, B_HEADS)
    logf_f = jax.nn.log_sigmoid(ff.astype(jnp.float32) + fox_b.astype(jnp.float32))
    lb32 = lb.astype(jnp.float32).reshape(C_HEADS, C_DK)
    fc32 = heads(fc, C_HEADS).astype(jnp.float32)
    f_c = lb32 + (1.0 - lb32) * jax.nn.sigmoid(fc32)
    logf_c = jnp.log(f_c)
    kc = (1.0 - lb32) * jax.nn.sigmoid(-fc32)
    qc = jax.nn.silu(heads(qc, C_HEADS).astype(jnp.float32))
    ic = heads(ic, C_HEADS)

    if past is None:
        ka_all, va_all, kf_all, vf_all, lf_all = ka, va, kf, vf, logf_f
        s0 = jnp.zeros((B, C_HEADS, C_DK, C_DV), dtype=jnp.float32)
    else:
        pk_a, pv_a, pk_f, pv_f, plf, s0 = past
        ka_all = jnp.concatenate([pk_a.astype(ka.dtype), ka], axis=1)
        va_all = jnp.concatenate([pv_a.astype(va.dtype), va], axis=1)
        kf_all = jnp.concatenate([pk_f.astype(kf.dtype), kf], axis=1)
        vf_all = jnp.concatenate([pv_f.astype(vf.dtype), vf], axis=1)
        lf_all = jnp.concatenate([plf.astype(jnp.float32), logf_f], axis=1)

    oa = _moba_attend(qa, ka_all, va_all, pos0)
    of = _fox_attend(qf, kf_all, vf_all, lf_all, pos0)
    oc, s_new = _hgrn2_recurrence(qc, kc, ic, logf_c, s0)
    oc = _rmsnorm(oc, hgrn_g) * jax.nn.silu(heads(gc, C_HEADS).astype(jnp.float32))
    o = jnp.concatenate([oa.reshape(B, T, -1), of.reshape(B, T, -1), oc.reshape(B, T, -1).astype(h.dtype)], axis=-1) @ w_out
    new = (ka, va, kf, vf, logf_f.astype(h.dtype), s_new.astype(h.dtype))
    return o, new

def setup_inputs(seed: int = 0) -> dict:
    key = jax.random.key(seed)
    ks = jax.random.split(key, 24)
    nrm = jax.random.normal
    n_pages = PAST_LEN // PAGE_SIZE
    n_pool = (DEC_BATCH * n_pages * 5) // 4
    page_table = jax.random.permutation(ks[8], n_pool)[:DEC_BATCH * n_pages].reshape(DEC_BATCH, n_pages).astype(jnp.int32)
    return {
        'x_prompt': nrm(ks[0], (BATCH, SEQ, D_MODEL), jnp.float32),
        'x_sample': nrm(ks[1], (DEC_BATCH, DEC_SEQ, D_MODEL), jnp.float32),
        'cache_moba_k': nrm(ks[2], (DEPTH, n_pool, PAGE_SIZE, A_HEADS, HEAD_DIM), jnp.float32),
        'cache_moba_v': nrm(ks[3], (DEPTH, n_pool, PAGE_SIZE, A_HEADS, HEAD_DIM), jnp.float32),
        'cache_fox_k': nrm(ks[4], (DEPTH, n_pool, PAGE_SIZE, B_HEADS, HEAD_DIM), jnp.float32),
        'cache_fox_v': nrm(ks[5], (DEPTH, n_pool, PAGE_SIZE, B_HEADS, HEAD_DIM), jnp.float32),
        'cache_fox_logf': jax.nn.log_sigmoid(FOX_BIAS_INIT + nrm(ks[6], (DEPTH, n_pool, PAGE_SIZE, B_HEADS), jnp.float32)),
        'state_hgrn': 0.5 * nrm(ks[7], (DEPTH, DEC_BATCH, C_HEADS, C_DK, C_DV), jnp.float32),
        'page_table': page_table,
        'norm_ffn1_g': 1.0 + 0.02 * nrm(ks[9], (DEPTH, D_MODEL), jnp.float32),
        'ffn1_w_gate': nrm(ks[10], (DEPTH, D_MODEL, D_FF), jnp.float32) * D_MODEL ** -0.5,
        'ffn1_w_up': nrm(ks[11], (DEPTH, D_MODEL, D_FF), jnp.float32) * D_MODEL ** -0.5,
        'ffn1_w_down': nrm(ks[12], (DEPTH, D_FF, D_MODEL), jnp.float32) * D_FF ** -0.5,
        'norm_mix_g': 1.0 + 0.02 * nrm(ks[13], (DEPTH, D_MODEL), jnp.float32),
        'w_in': nrm(ks[14], (DEPTH, D_MODEL, D_IN), jnp.float32) * D_MODEL ** -0.5,
        'fox_f_bias': FOX_BIAS_INIT + 0.1 * nrm(ks[15], (DEPTH, B_HEADS), jnp.float32),
        'hgrn_lb_logits': 0.1 * nrm(ks[16], (DEPTH, C_HEADS * C_DK), jnp.float32),
        'hgrn_norm_g': 1.0 + 0.02 * nrm(ks[17], (DEPTH, C_DV), jnp.float32),
        'w_out': nrm(ks[18], (DEPTH, D_MIX, D_MODEL), jnp.float32) * D_MIX ** -0.5,
        'norm_ffn2_g': 1.0 + 0.02 * nrm(ks[19], (DEPTH, D_MODEL), jnp.float32),
        'ffn2_w_gate': nrm(ks[20], (DEPTH, D_MODEL, D_FF), jnp.float32) * D_MODEL ** -0.5,
        'ffn2_w_up': nrm(ks[21], (DEPTH, D_MODEL, D_FF), jnp.float32) * D_MODEL ** -0.5,
        'ffn2_w_down': nrm(ks[22], (DEPTH, D_FF, D_MODEL), jnp.float32) * D_FF ** -0.5,
        'norm_final_g': 1.0 + 0.02 * nrm(ks[23], (D_MODEL,), jnp.float32),
    }

def reference(x_prompt, x_sample, cache_moba_k, cache_moba_v, cache_fox_k, cache_fox_v, cache_fox_logf, state_hgrn, page_table, norm_ffn1_g, ffn1_w_gate, ffn1_w_up, ffn1_w_down, norm_mix_g, w_in, fox_f_bias, hgrn_lb_logits, hgrn_norm_g, w_out, norm_ffn2_g, ffn2_w_gate, ffn2_w_up, ffn2_w_down, norm_final_g):
    lb_p = jax.nn.softmax(hgrn_lb_logits.astype(jnp.float32), axis=0)
    lower_bounds = jnp.cumsum(lb_p, axis=0) - lb_p[0:1]
    n_seq, n_pages = page_table.shape

    def paged(cache_l):
        rows = cache_l[page_table]
        return rows.reshape((n_seq, n_pages * cache_l.shape[1]) + cache_l.shape[2:])

    def trunk(x, sample):
        new = []
        for l in range(DEPTH):
            x = x + 0.5 * _swiglu(_rmsnorm(x, norm_ffn1_g[l]), ffn1_w_gate[l], ffn1_w_up[l], ffn1_w_down[l])
            past = None
            if sample:
                past = (paged(cache_moba_k[l]), paged(cache_moba_v[l]), paged(cache_fox_k[l]), paged(cache_fox_v[l]), paged(cache_fox_logf[l]), state_hgrn[l])
            o, rows = _token_mix(_rmsnorm(x, norm_mix_g[l]), w_in[l], fox_f_bias[l], lower_bounds[l], hgrn_norm_g[l], w_out[l], past)
            x = x + o
            x = x + 0.5 * _swiglu(_rmsnorm(x, norm_ffn2_g[l]), ffn2_w_gate[l], ffn2_w_up[l], ffn2_w_down[l])
            new.append(rows)
        y = _rmsnorm(x, norm_final_g)
        return y, [jnp.stack(z) for z in zip(*new)]

    y_prompt, (mk_p, mv_p, fk_p, fv_p, fl_p, hs_p) = trunk(x_prompt, False)
    y_sample, (mk_s, mv_s, fk_s, fv_s, fl_s, hs_s) = trunk(x_sample, True)
    return (y_prompt, y_sample, mk_p, mv_p, fk_p, fv_p, fl_p, hs_p, mk_s, mv_s, fk_s, fv_s, fl_s, hs_s)


_drawn_inputs = setup_inputs


def setup_inputs(seed=0):
    import zlib

    import numpy as np

    out = dict(_drawn_inputs(seed))
    spreads = {}
    factors = {'norm_ffn1_g': 4.356,
     'hgrn_norm_g': 34.45,
     'norm_ffn2_g': 5.447,
     'norm_final_g': 24.534,
     'cache_moba_k': 7.193,
     'cache_moba_v': 6.149,
     'cache_fox_logf': 36.636,
     'cache_fox_k': 4.509}
    for name, (base, spread) in spreads.items():
        noise = np.random.default_rng([zlib.crc32(name.encode()), seed]).standard_normal(out[name].shape)
        drawn = base * np.exp(spread * noise) if base else spread * noise
        out[name] = __import__('jax').numpy.asarray(drawn.astype(out[name].dtype))
    for name, factor in factors.items():
        out[name] = (out[name] * factor).astype(out[name].dtype)
    return out
```

```python
from contextlib import ExitStack

import numpy as np

import concourse.bass as bass
from concourse import mybir

F32 = mybir.dt.float32
F32R = mybir.dt.float32r
I32 = mybir.dt.int32
U32 = mybir.dt.uint32
ALU = mybir.AluOpType
ACT = mybir.ActivationFunctionType
AX = mybir.AxisListType
ds = bass.ds

D, SEQ, DEPTH, DB, DS = 1024, 256, 2, 8, 8
PAST, PAGE = 1024, 128
HD, AH, BH, CH = 64, 6, 5, 5
FF = 2816
NS = DB * DS
NT = SEQ + NS
KT_D = D // 128
FT = FF // 128
NPG = PAST // PAGE
NPOOL = DB * NPG * 5 // 4
BLK = 256
NBLK = PAST // BLK
EPS, NEG = 1e-6, -1e30
SCALE = HD ** -0.5
AW, BW = AH * HD, BH * HD
NH = AH + BH
ROWS = NH * DS
LEVELS = 7

_THIRD = [0, 128, 192]
_col = {}
_c = 0
for _n, _w in (("qa", AW), ("ka", AW), ("va", AW), ("qf", BW), ("kf", BW), ("vf", BW), ("ff", BH),
               ("qc", BW), ("fc", BW), ("ic", BW), ("gc", BW)):
    _col[_n] = _c
    _c += _w
D_IN = _c
TILES, T = [], {}
for _n in ("qa", "ka", "va", "qf", "kf", "vf", "ff", "qc", "fc", "ic", "gc"):
    T[_n] = len(TILES)
    if _n == "ff":
        TILES += [_col[_n]]
    elif _n in ("qa", "ka", "va"):
        TILES += [_col[_n] + 128 * j for j in range(3)]
    else:
        TILES += [_col[_n] + _THIRD[j] for j in range(3)]
TILES += [TILES[-1]]
WIN_CHUNKS = len(TILES) // 2
OUT_T = [T["va"], T["va"] + 1, T["va"] + 2, T["vf"], T["vf"] + 1, T["vf"] + 2, T["ic"], T["ic"] + 1, T["ic"] + 2]
HEADS5 = [(0, 0), (0, 1), (1, 0), (1, 1), (2, 1)]
ORD = [0, 2, 1, 3, 4]
HCOL = [0, 64, 128, 192, 320]

GU, DOWN, WIN, WOUT = FT // 2, 6, WIN_CHUNKS // 2, 4
OFF = {"ffn1": 0, "down1": GU, "win": GU + DOWN, "wout": GU + DOWN + WIN,
       "ffn2": GU + DOWN + WIN + WOUT, "down2": 2 * GU + DOWN + WIN + WOUT}
USES = 2 * GU + 2 * DOWN + WIN + WOUT

C, _w0 = {}, 0
for _n, _w in (("ident", 128), ("ones", 128), ("blk", 128), ("perm", 128), ("cos", NT), ("sin", NT),
               ("causal", 384), ("lmask", (LEVELS + 1) * 128), ("reset", NT), ("newmask", DB * DS),
               ("later", 128), ("seqof", DB), ("place", NBLK)):
    C[_n] = (_w0, _w)
    _w0 += _w
NC_COLS = _w0


def constants():
    c = np.zeros((128, NC_COLS), np.float32)

    def put(name, a):
        o, w = C[name]
        c[:a.shape[0], o:o + w] = a.reshape(a.shape[0], w)

    i = np.arange(128)
    put("ident", np.eye(128))
    put("ones", np.ones((128, 128)))
    put("blk", (i[:, None] // 64 == i[None, :] // 64).astype(np.float32))
    perm = np.zeros((128, 128))
    for m in range(128):
        if m % 64 < 32:
            perm[m + 32, m] = -1.0
        else:
            perm[m - 32, m] = 1.0
    put("perm", perm)
    half = HD // 2
    inv = np.power(np.float32(10000.0), -np.arange(half, dtype=np.float32) * np.float32(2.0) / np.float32(HD))
    pos = np.concatenate([np.arange(SEQ), np.tile(PAST + np.arange(DS), DB)]).astype(np.float32)
    ang = (pos[None, :] * inv[i % half, None]).astype(np.float32)
    put("cos", np.cos(ang))
    put("sin", np.sin(ang))
    tri = np.where(i[None, :] <= i[:, None], 0.0, NEG)
    put("causal", np.concatenate([tri, np.zeros((128, 128)), tri], 1))
    lm = np.zeros((128, LEVELS + 1, 128))
    for l in range(LEVELS):
        h = 1 << l
        s, t = i[:, None], i[None, :]
        lm[:, l] = (s // (2 * h) == t // (2 * h)) & (s % (2 * h) < h) & (t % (2 * h) >= h)
    lm[:, LEVELS] = np.eye(128)
    put("lmask", lm)
    reset = np.ones((128, NT))
    reset[:, 0] = 0
    reset[:, SEQ::DS] = 0
    put("reset", reset)
    k = np.arange(NS)
    nm = np.full((NS, DB, DS), NEG)
    for b in range(DB):
        for t in range(DS):
            nm[(k // DS == b) & (k % DS <= t), b, t] = 0.0
    put("newmask", nm)
    put("later", (i[:, None] > i[None, :]).astype(np.float32))
    put("seqof", (k[:, None] // DS == np.arange(DB)[None, :]).astype(np.float32))
    put("place", np.tile(2.0 ** np.arange(NBLK), (128, 1)))
    return c


ACT_STEPS = 5
DVE_STEPS = 353


class Chain:

    def __init__(self, eng, sem):
        self.eng, self.sem, self.base, self.n = eng, sem, 0, 0

    def mark(self, ins):
        self.n += 1
        return ins.then_inc(self.sem, 1)

    def catch_up(self):
        self.eng.wait_ge(self.sem, self.base + self.n)

    def link(self, ins):
        self.mark(ins)
        self.catch_up()

    def enter(self, i, steps):
        self._out = (self.base, self.n)
        self.base, self.n = self.base + self.n + i * steps, 0

    def leave(self, trips, steps):
        assert self.n == steps, (self.n, steps)
        self.base, self.n = self._out[0], self._out[1] + trips * steps


def trunk(nc, a, outs):
    ctx = ExitStack()
    with ctx:
        def sb(name, shape, dt=F32, into=ctx):
            return into.enter_context(nc.sbuf_tensor(name, shape, dt))

        def sem(name):
            return ctx.enter_context(nc.semaphore(name))

        X = sb("X", [128, KT_D * NT + 64])
        xt = lambda k: X[:, k * NT:(k + 1) * NT]
        K = sb("K", [128, NC_COLS])
        cst = lambda name: K[:, C[name][0]:C[name][0] + C[name][1]]
        gains = sb("gains", [128, DEPTH * 24 + 8])
        gcur = sb("gcur", [128, 24])
        lbt = sb("lbt", [128, DEPTH, 6])
        lbcur = sb("lbcur", [128, 6])
        gh = sb("gh", [128, DEPTH])
        ghcur = sb("ghcur", [128, 1])
        fb = sb("fb", [BH, DEPTH])
        fbcur = sb("fbcur", [BH, 1])
        pages = sb("pages", [1, DB * NPG], I32)
        pbias = sb("pbias", [128, DEPTH * DB * NPG, BH])
        ncn = sb("ncn", [BH, NT + 64])
        tokn = sb("tokn", [NS, BH])
        sqsum = sb("sqsum", [128, NT])
        rstd = sb("rstd", [128, NT])
        tmp = [sb(f"tmp{j}", [128, NT]) for j in range(4)]
        raw = [sb(f"raw{s}", [128, 8, 256]) for s in range(2)]
        whi = [sb(f"whi{s}", [128, 8, 256], F32R) for s in range(2)]
        wlo = [sb(f"wlo{s}", [128, 8, 256], F32R) for s in range(2)]
        with ExitStack() as r1:
            xh = sb("xh", [128, 9, NT], F32R, r1)
            xl = sb("xl", [128, 9, NT], F32R, r1)
        vpg = sb("vpg", [128, NPG, AW + BW])
        vfill = sb("vfill", [128, 18 * NT - NPG * (AW + BW)])
        with ExitStack() as r2:
            hh = sb("hh", [128, FT, NT], F32R, r2)
            hl = sb("hl", [128, FT, NT], F32R, r2)
        P = sb("P", [128, 32 * NT + 64])
        pt = lambda n: P[:, n * NT:(n + 1) * NT]
        p3 = lambda n: P[:, n * NT:(n + 3) * NT].rearrange("p (j t) -> p j t", j=3)
        tok = sb("tok", [128, 3, 5 * 384])
        tokf = sb("tokf", [128, 3, BH])
        with ExitStack() as r3:
            b = [sb(f"b{i}", [128, 3 * NT], F32, r3) for i in range(5)]
            kdt = sb("kdt", [128, 3, 384], F32, r3)
            am = sb("am", [128, CH, 256], F32, r3)
            asm = sb("asm", [NS, CH, NS], F32, r3)
            ac = sb("ac", [128, CH, 128], F32, r3)
            qe = sb("qe", [128, 3, NS], F32, r3)
            el = sb("el", [128, 3, DB], F32, r3)
            s0 = sb("s0", [128, 3, DB, 64], F32, r3)
            sp_ = sb("sp_", [128, 3, 64], F32, r3)
        with ExitStack() as r4:
            kpg = sb("kpg", [128, 4, AW + BW], F32, r4)
            ktp = sb("ktp", [128, 2, 768], F32, r4)
            st = sb("st", [128, 2, 440], F32, r4)
            sm = sb("sm", [ROWS, 1088], F32, r4)
            pe_ = sb("pe_", [ROWS, 1152], F32, r4)
            ptt = sb("ptt", [128, 9, ROWS], F32, r4)
            qb = sb("qb", [128, 6, DB, 16], F32, r4)
            newb = sb("newb", [NS, DB, ROWS], F32, r4)
            gm = sb("gm", [ROWS, NBLK], F32, r4)
            gs_ = sb("gs_", [48, 4, NBLK], F32, r4)
            rs = sb("rs", [ROWS, 4], F32, r4)
        V_ = lambda i, j: b[i][:, j * NT:(j + 1) * NT]
        VH = [(0, 0, 0), (0, 1, 1), (1, 0, 2), (1, 1, 3), (2, 0, 3), (2, 1, 4)]
        spr = [b[0][:, 0:384], b[0][:, 384:768], b[1][:, 0:384]]
        ppt = [b[1][:, 384:768], b[2][:, 0:384]]
        spx = b[2][:, 384:432]
        PS = ctx.enter_context(nc.psum_tensor("PS", [128, 8, 512], F32))

        s_c = sem("consts_in")
        waited = sem("waited")
        s_small = sem("small_in")
        s_x = sem("x_in")
        s_lf = sem("past_logf_in")
        s_idx = sem("page_rows_ready")
        s_pages = sem("page_table_in")
        lb_diff, lb_sig = sem("lb_diff"), sem("lb_sig")
        s_dve, s_act = sem("vector_step"), sem("scalar_step")
        raw_in = [sem(f"raw_in{s}") for s in range(2)]
        hi_done = [sem(f"hi_done{s}") for s in range(2)]
        split_done = [sem(f"split_done{s}") for s in range(2)]
        w_free = [sem(f"weights_free{s}") for s in range(2)]
        gate_ready, silu_done, up_ready, up_used, h_done = (
            sem(n) for n in ("gate_ready", "silu_done", "up_ready", "up_used", "h_done"))
        acc_ready, acc_used = sem("acc_ready"), sem("acc_used")
        ms_ready, sqsum_ready, rstd_ready, xs_ready, xh_ready, xl_ready, ms_eps = (
            sem(n) for n in ("ms_ready", "sqsum_ready", "rstd_ready", "xs_ready", "xh_ready", "xl_ready", "ms_eps"))
        win_ready, win_used = sem("win_ready"), sem("win_used")
        rot_ready, roped = sem("rot_ready"), sem("roped")
        qf_scaled = sem("qf_scaled")
        z_ready, z_exp, lf_ready = sem("z_ready"), sem("z_ln"), sem("lf_ready")
        tt_ready, tt_used = sem("tok_ready"), sem("tok_used")
        s_ready, p_ready, pT_ready, pT_used, o_ready, o_used, smax, pexp, s_used = (
            sem(n) for n in ("ps_ready", "pp_ready", "ppT_ready", "ppT_used", "po_ready", "po_used",
                             "p_max", "p_exp", "ps_used"))
        h_oa = sem("h_oa")
        h_sig, h_qk, h_logf = (sem(n) for n in ("h_sig", "h_qk", "h_logf"))
        h_abs, h_e, h_g, h_p, h_pused, h_ac = (sem(n) for n in ("h_abs", "h_e", "h_g", "h_p", "h_pused", "h_ac"))
        h_kd, h_kdT, h_kdU, h_o, h_sq, h_ms, h_mse, h_rs, h_out = (
            sem(n) for n in ("h_kd", "h_kdT", "h_kdU", "h_o", "h_sq", "h_ms", "h_mse", "h_rs", "h_out"))
        h_st, h_stU, h_vx, h_sn, h_snU, s0_in = (sem(n) for n in ("h_st", "h_stU", "h_vx", "h_sn", "h_snU", "s0_in"))
        k_in = [sem(f"k_in{j}") for j in range(4)]
        v_in = [sem(f"v_in{j}") for j in range(NPG)]
        d_init, kT_ready, kT_act, kT_dve, sT_ready, sT_act, sT_dve = (
            sem(n) for n in ("d_init", "kT_ready", "kT_act", "kT_dve", "sT_ready", "sT_act", "sT_dve"))
        r_ready, rn_ready, rows_used, rows_new, d_max, d_exp, dp_ready = (
            sem(n) for n in ("r_ready", "rn_ready", "rows_used", "rows_new", "d_max", "d_exp", "dp_ready"))
        dpT_ready, dpT_act, dpT_dve, do_ready, do_used, kT_used = (
            sem(n) for n in ("dpT_ready", "dpT_act", "dpT_dve", "do_ready", "do_used", "kT_used"))
        xT_ready, gT_ready, lfT_ready, pb_ready, later_ready = (
            sem(n) for n in ("xT_ready", "gT_ready", "lfT_ready", "pb_ready", "later_ready"))
        oh_ready, ol_ready = sem("oh_ready"), sem("ol_ready")
        f_T, f_U, f_out = sem("y_ready"), sem("y_copied"), sem("y_out")
        out_tok, out_st = sem("out_tok"), sem("out_state")

        block = ctx.enter_context(nc.Block())
        SMALL = DEPTH * 9 + 2

        wg = [a["ffn1_w_gate"], a["ffn2_w_gate"]]
        wu = [a["ffn1_w_up"], a["ffn2_w_up"]]
        wd = [a["ffn1_w_down"], a["ffn2_w_down"]]
        gu_v = lambda w: w.rearrange("l (k p) n -> p (l k) n", p=128)

        def tile_done(eng, j, first_ready, n, s, use):
            if j == 0:
                eng.wait_ge(first_ready, n + 1)
            else:
                eng.wait_ge(w_free[s], use + 2)

        def settle(eng):
            eng.sem_inc(waited, 1)

        @block.sync
        def _(sp):
            def fill(s, use, parts):
                sp.wait_ge(split_done[s], use + 1)
                for n, (dst, src) in enumerate(parts):
                    ins = sp.dma_start(dst, src)
                    ins.then_inc(raw_in[s], 16 if len(parts) == 2 else 32)

            def gu_chunk(f, L, i):
                u = L * USES + OFF[f"ffn{f + 1}"] + i
                for s, w in ((0, wg[f]), (1, wu[f])):
                    fill(s, u, [(raw[s][:, :, :], gu_v(w)[:, ds(L * 8, 8), ds(i * 256, 256)])])

            def down_chunks(f, L):
                wdv = wd[f].rearrange("l (k p) n -> p (l k) n", p=128)
                with sp.Fori(0, 2) as m:
                    for n in range(6):
                        dp, kk = divmod(n, 3)
                        nk = 8 if kk < 2 else FT - 16
                        fill(n % 2, L * USES + OFF[f"down{f + 1}"] + m * 3 + n // 2,
                             [(raw[n % 2][:, 0:nk, :], wdv[:, ds(L * FT + kk * 8, nk), ds(m * 512 + dp * 256, 256)])])

            def wout_chunks(L, m):
                u = L * USES + OFF["wout"] + m
                rows = lambda r0, n: a["w_out"][ds(L, 1), r0:r0 + n, ds(m * 256, 256)]
                fill(0, u, [(raw[0][:, 0:5, :], rows(0, 640).rearrange("l (k p) n -> p (l k) n", p=128)),
                            (raw[0][64:128, 5, :], rows(640, 64).rearrange("l p n -> (l p) n"))])
                fill(1, u, [(raw[1][:, 0:2, :], rows(704, 256).rearrange("l (k p) n -> p (l k) n", p=128)),
                            (raw[1][64:128, 2, :], rows(960, 64).rearrange("l p n -> (l p) n"))])

            sp.dma_start(K[:, :], a["consts"]).then_inc(s_c, 16)
            sp.dma_start(pages[:, :], a["page_table"].rearrange("(o b) n -> o (b n)", o=1)).then_inc(s_pages, 16)
            xtok = [raw[0].rearrange("p a b -> p (a b)")[:, 0:1024], raw[0].rearrange("p a b -> p (a b)")[:, 1024:2048],
                    raw[1].rearrange("p a b -> p (a b)")[:, 0:1024]]
            xp = a["x_prompt"].rearrange("b (n p) d -> (b n) p d", p=128)
            for n in range(2):
                sp.dma_start(xtok[n], xp[n]).then_inc(s_x, 16)
            sp.dma_start(xtok[2][0:NS, :], a["x_sample"].rearrange("b t d -> (b t) d")).then_inc(s_x, 16)
            sp.wait_ge(s_pages, 16)
            gu_chunk(0, 0, 0)
            with sp.Fori(0, DEPTH) as L:
                with sp.Fori(1, GU) as i:
                    gu_chunk(0, L, i)
                down_chunks(0, L)
                winv = a["w_in"].rearrange("l (k p) n -> p (l k) n", p=128)
                for c in range(WIN_CHUNKS):
                    s = c % 2
                    fill(s, L * USES + OFF["win"] + c // 2,
                         [(raw[s][:, :, 128 * j:128 * j + 128],
                           winv[:, ds(L * 8, 8), TILES[2 * c + j]:TILES[2 * c + j] + 128]) for j in range(2)])
                wout_chunks(L, 0)
                for j in range(3):
                    if j == 0:
                        sp.wait_ge(win_used, L * 32 + 36)
                    hs = [0, 2, 3][j]
                    sp.dma_start(s0[:, j, :, :],
                                 a["state_hgrn"][ds(L, 1), :, hs:hs + 2, :, :].rearrange("l b h d e -> (l h d) b e")
                                 ).then_inc(s0_in, 16)
                sp.wait_ge(tt_used, L * 16 + 16)
                for g, (op, os, w) in enumerate((("moba_k_prompt", "moba_k_sample", AW), ("moba_v_prompt", "moba_v_sample", AW),
                                                 ("fox_k_prompt", "fox_k_sample", BW), ("fox_v_prompt", "fox_v_sample", BW))):
                    for c0, n, t0 in ((0, 384, 0),) if w == AW else ((0, 256, 0), (256, 64, 320)):
                        pv = outs[op].rearrange("l b (n p) h d -> p (l b n) (h d)", p=128)
                        sv = outs[os].rearrange("l b t h d -> l (b t) (h d)")
                        sp.dma_start(pv[:, ds(L * 2, 2), c0:c0 + n], tok[:, 0:2, g * 384 + t0:g * 384 + t0 + n]).then_inc(out_tok, 16)
                        sp.dma_start(sv[ds(L, 1), :, c0:c0 + n].rearrange("l t c -> (l t) c"),
                                     tok[0:NS, 2, g * 384 + t0:g * 384 + t0 + n]).then_inc(out_tok, 16)
                sp.dma_start(outs["fox_logf_prompt"].rearrange("l b (n p) h -> p (l b n) h", p=128)[:, ds(L * 2, 2), :],
                             tokf[:, 0:2, :]).then_inc(out_tok, 16)
                sp.dma_start(outs["fox_logf_sample"].rearrange("l b t h -> l (b t) h")[ds(L, 1), :, :].rearrange("l t h -> (l t) h"),
                             tokf[0:NS, 2, :]).then_inc(out_tok, 16)
                sp.wait_ge(h_stU, L + 1)
                sp.wait_ge(h_snU, L * 3 + 3)
                for j, (hs, p0) in enumerate(((0, 0), (2, 0), (4, 64))):
                    nh = 2 - p0 // 64
                    sp.dma_start(outs["hgrn_state_prompt"][ds(L, 1), 0, hs:hs + nh, :, :].rearrange("l h d e -> (l h d) e"),
                                 sp_[p0:128, j, :]).then_inc(out_st, 16)
                    sp.dma_start(outs["hgrn_state_sample"][ds(L, 1), :, hs:hs + nh, :, :].rearrange("l b h d e -> (l h d) b e"),
                                 s0[p0:128, j, :, :]).then_inc(out_st, 16)
                sp.wait_ge(out_st, L * 96 + 96)
                kmv = a["cache_moba_k"].rearrange("l n p h d -> p (l n) (h d)")
                kfv = a["cache_fox_k"].rearrange("l n p h d -> p (l n) (h d)")
                sp.wait_ge(d_init, L + 1)
                settle(sp)
                with sp.Fori(0, DB) as q:
                    for pg in range(NPG):
                        s = pg % 4
                        sp.wait_ge(kT_ready, (L * DB + q) * NPG + pg + 1)
                        page = sp.value_load(pages[0:1, ds(q * NPG + pg, 1)], min_val=0, max_val=NPOOL - 1)
                        sp.dma_start(kpg[:, s, 0:AW], kmv[:, ds(page + L * NPOOL, 1), :].rearrange("p a c -> p (a c)")).then_inc(k_in[s], 16)
                        sp.dma_start(kpg[:, s, AW:AW + BW], kfv[:, ds(page + L * NPOOL, 1), :].rearrange("p a c -> p (a c)")).then_inc(k_in[s], 16)
                with sp.Fori(1, 4) as m:
                    wout_chunks(L, m)
                with sp.Fori(0, GU) as i:
                    gu_chunk(1, L, i)
                down_chunks(1, L)
                nl = L * -1 + 1
                for s, w in ((0, wg[0]), (1, wu[0])):
                    fill(s, L * USES + USES, [(raw[s][:, :, :], gu_v(w)[:, ds(nl * 8, 8), 0:256])])
            for n in range(3):
                sp.wait_ge(f_U, 2 * (n + 1))
                rows = 128 if n < 2 else NS
                dst = outs["y_prompt"].rearrange("b (n p) d -> (b n) p d", p=128)[n] if n < 2 else \
                    outs["y_sample"].rearrange("b t d -> (b t) d")
                sp.dma_start(dst, P[0:rows, n * 1024:(n + 1) * 1024]).then_inc(f_out, 16)
            sp.wait_ge(f_out, 48)
            sp.wait_ge(out_tok, 14 * 16 * DEPTH)
            sp.wait_ge(out_st, 6 * 16 * DEPTH)
            for s in range(2):
                sp.wait_ge(raw_in[s], 32 * (DEPTH * USES + 1))

        @block.gpsimd
        def _(pool):
            grow = vpg[:, 0, 0:128]
            n = 0
            with nc.allow_non_contiguous_dma(reason="small parameters"):
                for l in range(DEPTH):
                    for w, name in enumerate(("norm_ffn1_g", "norm_mix_g", "norm_ffn2_g")):
                        r = l * 24 + w * 8
                        pool.dma_start(grow[r:r + 8, :], a[name][l].rearrange("(k p) -> k p", p=128)).then_inc(s_small, 16)
                        n += 1
                    for j in range(3):
                        pool.dma_start(lbt[:, l, j:j + 1], a["hgrn_lb_logits"][l, _THIRD[j]:_THIRD[j] + 128].rearrange("(p o) -> p o", o=1)).then_inc(s_small, 16)
                        n += 1
                    for hf in range(2):
                        pool.dma_start(gh[64 * hf:64 * hf + 64, l:l + 1], a["hgrn_norm_g"][l].rearrange("(p o) -> p o", o=1)).then_inc(s_small, 16)
                        n += 1
                    pool.dma_start(fb[:, l:l + 1], a["fox_f_bias"][l].rearrange("(p o) -> p o", o=1)).then_inc(s_small, 16)
                    n += 1
                pool.dma_start(grow[DEPTH * 24:DEPTH * 24 + 8, :], a["norm_final_g"].rearrange("(k p) -> k p", p=128)).then_inc(s_small, 16)
                pool.dma_start(vpg[0:DB * NPG, 1, 0:1].bitcast(I32), a["page_table"].rearrange("b (n o) -> (b n) o", o=1)).then_inc(s_small, 16)
                n += 2
            assert n == SMALL
            lfv = a["cache_fox_logf"].rearrange("l n p h -> (l n) (p h)")
            pool.wait_ge(s_idx, DEPTH)
            for l in range(DEPTH):
                pool.indirect_dma_start(
                    vpg[0:DB * NPG, 2 + l, 0:PAGE * BH], None, lfv,
                    bass.IndirectOffsetOnAxis(ap=vpg[0:DB * NPG, 1, 2 + l:3 + l].bitcast(U32), axis=0)).then_inc(s_lf, 16)
            pool.wait_ge(s_pages, 16)
            vmv = a["cache_moba_v"].rearrange("l n p h d -> p (l n) (h d)")
            vfv = a["cache_fox_v"].rearrange("l n p h d -> p (l n) (h d)")
            with pool.Fori(0, DEPTH) as L:
                pool.wait_ge(win_used, L * 32 + 36)
                settle(pool)
                with pool.Fori(0, DB) as q:
                    pool.wait_ge(do_used, L * 4 * DB + q * 4 + 4)
                    for pg in range(NPG):
                        page = pool.value_load(pages[0:1, ds(q * NPG + pg, 1)], min_val=0, max_val=NPOOL - 1)
                        pool.dma_start(vpg[:, pg, 0:AW], vmv[:, ds(page + L * NPOOL, 1), :].rearrange("p a c -> p (a c)")).then_inc(v_in[pg], 16)
                        pool.dma_start(vpg[:, pg, AW:AW + BW], vfv[:, ds(page + L * NPOOL, 1), :].rearrange("p a c -> p (a c)")).then_inc(v_in[pg], 16)

        @block.scalar
        def _(act):
            ch = Chain(act, s_act)

            def hi(s, use):
                act.wait_ge(raw_in[s], (use + 1) * 32)
                act.wait_ge(w_free[s], use + 1)
                act.activation(whi[s][:, :, :], raw[s][:, :, :], ACT.Copy).then_inc(hi_done[s], 1)

            def norm(w):
                act.wait_ge(ms_eps, w + 1)
                ch.link(act.activation(rstd[:, :], rstd[:, :], ACT.Ln))
                act.activation(rstd[:, :], rstd[:, :], ACT.Exp, scale=-0.5).then_inc(rstd_ready, 1)

            def scaled(w):
                for k in range(KT_D):
                    act.wait_ge(xs_ready, w * KT_D + k + 1)
                    act.activation(xh[:, k, :], tmp[k % 4][:, :], ACT.Copy).then_inc(xh_ready, 1)

            def ffn(f, L):
                u0 = L * USES + OFF[f"ffn{f + 1}"]
                with act.Fori(0, GU) as i:
                    hi(1, u0 + i)
                    for j in range(2):
                        n = L * 2 * FT + f * FT + i * 2 + j
                        tile_done(act, j, gate_ready, L * 2 * GU + f * GU + i, 0, u0 + i)
                        act.wait_ge(up_used, n + 1)
                        act.activation(tmp[j][:, :], PS[:, j, 0:NT], ACT.Silu).then_inc(silu_done, 1)
                    hi(0, u0 + i + 1)
                u0 = L * USES + OFF[f"down{f + 1}"]
                with act.Fori(0, 2) as m:
                    for n in range(6):
                        hi((n + 1) % 2, u0 + m * 3 + (n + 1) // 2)

            act.wait_ge(s_c, 16)
            act.activation(tmp[0][:, 0:1], K[:, 0:1], ACT.Silu).then_inc(silu_done, 1)
            act.activation(tmp[0][:, 1:2], K[:, 0:1], ACT.Silu).then_inc(silu_done, 1)
            act.wait_ge(lb_diff, 1)
            act.activation(lbt[:, 1, 0:3], lbt[:, 1, 0:3], ACT.Sigmoid).then_inc(lb_sig, 1)
            hi(0, 0)
            with act.Fori(0, DEPTH) as L:
                ch.base, ch.n = L * ACT_STEPS, 0
                norm(L * 3)
                scaled(L * 3)
                ffn(0, L)
                norm(L * 3 + 1)
                scaled(L * 3 + 1)
                with act.Fori(0, WIN) as i:
                    hi(1, L * USES + OFF["win"] + i)
                    hi(0, L * USES + OFF["win"] + i + 1)
                act.wait_ge(win_used, L * 32 + 36)
                act.activation(p3(T["qf"]), p3(T["qf"]), ACT.Copy, scale=SCALE).then_inc(qf_scaled, 1)
                act.wait_ge(z_ready, L * 2 + 1)
                act.activation(tmp[2][0:BH, :], tmp[1][0:BH, :], ACT.Exp, scale=-1.0).then_inc(z_exp, 1)
                act.wait_ge(z_ready, L * 2 + 2)
                act.activation(tmp[1][0:BH, :], tmp[2][0:BH, :], ACT.Ln).then_inc(z_exp, 1)
                for h in range(NH + 1):
                    if h < NH:
                        for t in range(2):
                            act.wait_ge(smax, L * 2 * NH + 2 * h + t + 1)
                            c0, c1 = ((0, 128), (128, 384))[t]
                            act.activation(spr[h % 3][:, c0:c1], spr[h % 3][:, c0:c1], ACT.Exp,
                                           bias=spx[:, 4 * (h % 3) + t:4 * (h % 3) + t + 1],
                                           accum_out=spx[:, 16 + 4 * (h % 3) + t:17 + 4 * (h % 3) + t]).then_inc(pexp, 1)
                    if h >= 1:
                        n = h - 1
                        act.wait_ge(pT_ready, L * NH + n + 1)
                        if n >= 2:
                            act.wait_ge(o_ready, L * NH + n - 1)
                        act.activation(ppt[n % 2], PS[:, 2 + n % 2, 0:384], ACT.Copy).then_inc(pT_used, 1)
                act.wait_ge(o_ready, L * NH + NH)
                act.activation(b[1][:, :].rearrange("p (j t) -> p j t", j=3), p3(T["qc"]), ACT.Sigmoid).then_inc(h_sig, 1)
                act.activation(b[2][:, :].rearrange("p (j t) -> p j t", j=3), p3(T["gc"]), ACT.Sigmoid).then_inc(h_sig, 1)
                ch.link(act.activation(b[3][:, :].rearrange("p (j t) -> p j t", j=3), p3(T["fc"]), ACT.Sigmoid))
                act.activation(p3(T["fc"]), p3(T["fc"]), ACT.Sigmoid, scale=-1.0).then_inc(h_sig, 1)
                for j in range(3):
                    act.activation(b[0][:, j * NT:(j + 1) * NT], b[3][:, j * NT:(j + 1) * NT], ACT.Ln,
                                   bias=lbcur[:, j:j + 1], scale=lbcur[:, 3 + j:4 + j]).then_inc(h_logf, 1)
                for l in range(LEVELS + 1):
                    act.wait_ge(h_abs, L * 9 + l + 1)
                    v = b[3][:, :] if l < 6 else b[3][:, :].rearrange("p (j t) -> p j t", j=3)[:, :, 0:SEQ]
                    act.activation(v, v, ACT.Exp, scale=-1.0).then_inc(h_e, 1)
                cum3 = b[2][:, :].rearrange("p (j t) -> p j t", j=3)
                act.activation(qe[:, :, :], cum3[:, :, SEQ:NT], ACT.Exp).then_inc(h_e, 1)
                act.activation(el[:, :, :], cum3[:, :, SEQ + DS - 1:NT:DS], ACT.Exp).then_inc(h_e, 1)
                act.wait_ge(h_abs, L * 9 + 9)
                act.activation(b[3][:, :], b[3][:, :], ACT.Exp, scale=-1.0).then_inc(h_e, 1)
                act.wait_ge(h_p, L * 9 + 9)
                act.activation(ac[:, 0:2, :], PS[:, 0, 0:256].rearrange("p (h t) -> p h t", h=2), ACT.Copy).then_inc(h_ac, 1)
                act.activation(ac[:, 2:5, :], PS[:, 1, 0:384].rearrange("p (h t) -> p h t", h=3), ACT.Copy).then_inc(h_ac, 1)
                act.wait_ge(h_o, L + 1)
                act.wait_ge(h_kd, L + 1)
                act.activation(b[4][:, :].rearrange("p (j t) -> p j t", j=3), PS[:, 0:3, 0:NT], ACT.Square).then_inc(h_sq, 1)
                act.wait_ge(h_mse, L + 1)
                ch.link(act.activation(b[3][:, :], b[3][:, :], ACT.Ln))
                act.activation(b[3][:, :], b[3][:, :], ACT.Exp, scale=-0.5).then_inc(h_rs, 1)
                act.wait_ge(d_init, L + 1)

                with act.Fori(0, DB) as q:
                    Q = L * DB + q
                    for pg in range(NPG):
                        act.wait_ge(kT_ready, Q * NPG + pg + 5)
                        act.wait_ge(kT_used, Q * NPG + pg + 1)
                        act.activation(ktp[:, pg % 2, 0:384], PS[:, 2 * (pg % 2), 0:384], ACT.Copy).then_inc(kT_act, 1)
                        if pg % 4 == 3:
                            n4 = pg // 4
                            if n4 == 0:
                                act.wait_ge(kT_used, Q * NPG + 6)
                                act.wait_ge(r_ready, Q + 1)
                            else:
                                act.wait_ge(sT_ready, Q + 1)
                                act.wait_ge(rn_ready, Q + 1)
                            act.wait_ge(sT_dve, Q * 2 + n4 + 2)
                            act.activation(st[:, n4, 0:352].rearrange("p (g c) -> p g c", g=4)[:, :, 0:48],
                                           PS[:, 4, 0:352].rearrange("p (g c) -> p g c", g=4)[:, :, 0:48], ACT.Copy).then_inc(sT_act, 1)
                    act.wait_ge(rn_ready, Q + 2)
                    act.activation(sm[:, 1024:1088], PS[0:ROWS, 7, 128:192], ACT.Copy).then_inc(rows_new, 1)
                    act.wait_ge(d_max, Q + 1)
                    act.activation(pe_[:, 0:1088], sm[:, :], ACT.Exp, bias=rs[:, 0:1], accum_out=rs[:, 1:2]).then_inc(d_exp, 1)
                    act.wait_ge(dpT_ready, Q * 2 + 2)
                    act.activation(ptt[:, 5:9, :], PS[:, 1, 0:352].rearrange("p (g c) -> p g c", g=4), ACT.Copy).then_inc(dpT_act, 1)
                act.wait_ge(do_used, L * 4 * DB + 4 * DB + 4)
                act.wait_ge(h_out, L + 1)
                act.wait_ge(o_used, L * 6 + 6)
                for k in range(9):
                    r = slice(64, 128) if k in (5, 8) else slice(0, 128)
                    act.activation(xh[r, k, :], pt(OUT_T[k])[r, :], ACT.Copy).then_inc(oh_ready, 1)
                with act.Fori(0, 2) as m:
                    for dp in range(2):
                        hi(1, L * USES + OFF["wout"] + m * 2 + dp)
                        hi(0, L * USES + OFF["wout"] + m * 2 + dp + 1)
                norm(L * 3 + 2)
                scaled(L * 3 + 2)
                ffn(1, L)
                assert ch.n == ACT_STEPS, ch.n
            ch.base, ch.n = DEPTH * ACT_STEPS, 0
            norm(DEPTH * 3)

        @block.vector
        def _(dve):
            ch = Chain(dve, s_dve)
            link = ch.link
            V = lambda i: b[i][:, :].rearrange("p (j t) -> p j t", j=3)

            def give(s, n=1):
                dve.sem_inc(s, n)

            def lo(s, use):
                dve.wait_ge(hi_done[s], use + 1)
                dve.tensor_tensor(wlo[s][:, :, :], raw[s][:, :, :], whi[s][:, :, :].bitcast(F32), ALU.subtract).then_inc(split_done[s], 1)

            def norm(w):
                dve.wait_ge(ms_ready, w + 1)
                dve.tensor_scalar(rstd[:, :], PS[:, 7, 0:NT], 1.0 / D, EPS, ALU.mult, ALU.add).then_inc(ms_eps, 1)

            def low(w, k):
                dve.wait_ge(xh_ready, w * KT_D + k + 1)
                dve.tensor_tensor(xl[:, k, :], tmp[k % 4][:, :], xh[:, k, :].bitcast(F32), ALU.subtract).then_inc(xl_ready, 1)

            def scaled(w, which):
                dve.wait_ge(rstd_ready, w + 1)
                for k in range(KT_D):
                    if k >= 3:
                        low(w, k - 3)
                    if k >= 4:
                        dve.wait_ge(xl_ready, w * KT_D + k - 3)
                    dve.scalar_tensor_tensor(tmp[k % 4][:, :], xt(k), gcur[:, which * 8 + k:which * 8 + k + 1],
                                             rstd[:, :], ALU.mult, ALU.mult).then_inc(xs_ready, 1)
                for k in range(KT_D - 3, KT_D):
                    low(w, k)

            def accumulate(n0, half, at, bank, scale, s, use):
                for j in range(2):
                    tile_done(dve, j, acc_ready, half, s, use)
                    xs = X[:, ds(at + j * NT, NT)]
                    dve.scalar_tensor_tensor(xs, PS[:, bank + j, 0:NT], scale, xs, ALU.mult, ALU.add).then_inc(acc_used, 1)
                    dve.wait_ge(acc_used, n0 + j + 5)
                    link(dve.tensor_tensor(tmp[2][:, :], xs, xs, ALU.mult))
                    link(dve.tensor_tensor(sqsum[:, :], sqsum[:, :], tmp[2][:, :], ALU.add))

            def ffn(f, L):
                u0 = L * USES + OFF[f"ffn{f + 1}"]
                if f == 1:
                    dve.wait_ge(out_tok, L * 14 * 16 + 14 * 16)
                settle(dve)
                with dve.Fori(0, GU) as i:
                    ch.enter(i, 2)
                    lo(1, u0 + i)
                    lo(0, u0 + i + 1)
                    for j in range(2):
                        n = L * 2 * FT + f * FT + i * 2 + j
                        tile_done(dve, j, up_ready, L * 2 * GU + f * GU + i, 1, u0 + i)
                        dve.wait_ge(silu_done, n + 3)
                        dve.tensor_tensor(tmp[2 + j][:, :], tmp[j][:, :], PS[:, 2 + j, 0:NT], ALU.mult).then_inc(up_used, 1)
                        dve.wait_ge(up_used, n + 3)
                        hs, ls = hh[:, ds(i * 2 + j, 1), :], hl[:, ds(i * 2 + j, 1), :]
                        t = tmp[2 + j][:, :].rearrange("p (o t) -> p o t", o=1)
                        link(dve.tensor_scalar(hs, t, 1.0, None, ALU.mult))
                        dve.tensor_tensor(ls, t, hs.bitcast(F32), ALU.subtract).then_inc(h_done, 1)
                    ch.leave(GU, 2)
                link(dve.memset(sqsum[:, :], 0.0))
                settle(dve)
                u0 = L * USES + OFF[f"down{f + 1}"]
                with dve.Fori(0, 2) as m:
                    ch.enter(m, 8)
                    for n in range(6):
                        lo((n + 1) % 2, u0 + m * 3 + (n + 1) // 2)
                        if n % 3 == 2:
                            dp = n // 3
                            accumulate(L * 24 + f * 16 + m * 4 + 2 * dp, L * 12 + f * 8 + m * 2 + dp,
                                       m * (4 * NT) + dp * 2 * NT, 4 + 2 * dp, 0.5, n % 2, u0 + m * 3 + n // 2)
                    ch.leave(2, 8)
                give(sqsum_ready)

            for s, n in ((w_free[0], 1), (w_free[1], 1), (up_used, 2), (acc_used, 4), (do_used, 4), (do_ready, 1),
                         (win_used, 4), (kT_used, 2), (kT_act, 2), (kT_dve, 2), (sT_act, 1), (sT_dve, 1),
                         (r_ready, 1), (rn_ready, 1), (kT_ready, 4), (rows_used, 1), (rows_new, 1)):
                give(s, n)
            link(dve.memset(X[:, KT_D * NT:], 0.0))
            link(dve.memset(P[:, 32 * NT:], 0.0))
            link(dve.memset(ncn[:, :], 0.0))
            dve.wait_ge(s_small, 16 * SMALL)
            for l in range(DEPTH):
                dve.tensor_scalar(vpg[0:DB * NPG, 1, 2 + l:3 + l].bitcast(I32), vpg[0:DB * NPG, 1, 0:1].bitcast(I32),
                                  float(l * NPOOL), None, ALU.add).then_inc(s_idx, 1)
            dve.tensor_tensor(lbt[:, 1, 0:3], lbt[:, 1, 0:3], lbt[:, 0, 0:3], ALU.subtract).then_inc(lb_diff, 1)
            dve.wait_ge(lb_sig, 1)
            link(dve.memset(lbt[:, 0, 0:3], 0.0))
            link(dve.tensor_scalar(lbt[:, :, 3:6], lbt[:, :, 0:3], -1.0, 1.0, ALU.mult, ALU.add))
            for n in range(6):
                tt, hf = divmod(n, 2)
                r = 128 if tt < 2 else NS
                dve.wait_ge(xT_ready, n + 1)
                link(dve.tensor_copy(
                    X[:, 4 * hf * NT:(4 * hf + 4) * NT].rearrange("p (k t) -> p k t", k=4)[:, :, tt * 128:tt * 128 + r],
                    PS[:, n, :].rearrange("p (k t) -> p k t", k=4)[:, :, 0:r]))
            give(split_done[0]); give(split_done[1])
            dve.wait_ge(gT_ready, 1)
            link(dve.tensor_copy(gains[:, :], PS[:, 6, 0:DEPTH * 24 + 8]))
            link(dve.memset(sqsum[:, :], 0.0))
            for k in range(KT_D):
                link(dve.tensor_tensor(tmp[2][:, :], xt(k), xt(k), ALU.mult))
                link(dve.tensor_tensor(sqsum[:, :], sqsum[:, :], tmp[2][:, :], ALU.add))
            give(sqsum_ready)
            G = DB * NPG
            lft, later = tok[:, 0, 0:640], tok[:, 1, 0:640]
            l4 = lambda x: x.rearrange("p (l h b g) -> p (l h b) g", l=DEPTH, h=BH, b=DB)
            for l in range(DEPTH):
                dve.wait_ge(lfT_ready, l + 1)
                link(dve.tensor_copy(lft[:, l * 320:(l + 1) * 320], PS[:, l, 0:320]))
            link(dve.memset(later[:, :], 0.0))
            for pg in range(NPG - 2, -1, -1):
                link(dve.tensor_tensor(l4(later)[:, :, pg:pg + 1], l4(later)[:, :, pg + 1:pg + 2], l4(lft)[:, :, pg + 1:pg + 2], ALU.add))
            give(later_ready)
            for l in range(DEPTH):
                dve.wait_ge(pb_ready, l + 1)
                link(dve.tensor_copy(pbias[:, l * G:(l + 1) * G, :].rearrange("p g h -> p h g"),
                                     PS[:, 2 + l, 0:320].rearrange("p (h g) -> p h g", h=BH)))
            lo(0, 0)
            start_steps = ch.n
            with dve.Fori(0, DEPTH) as L:
                ch.base, ch.n = L * DVE_STEPS + start_steps, 0
                link(dve.tensor_scalar(gcur[:, :], gains[:, ds(L * 24, 24)], 1.0, None, ALU.mult))
                link(dve.tensor_scalar(lbcur[:, :].rearrange("p (o c) -> p o c", o=1), lbt[:, ds(L, 1), :], 1.0, None, ALU.mult))
                link(dve.tensor_scalar(ghcur[:, :], gh[:, ds(L, 1)], 1.0, None, ALU.mult))
                link(dve.tensor_scalar(fbcur[:, :], fb[:, ds(L, 1)], 1.0, None, ALU.mult))
                norm(L * 3)
                scaled(L * 3, 0)
                ffn(0, L)
                norm(L * 3 + 1)
                scaled(L * 3 + 1, 1)
                with dve.Fori(0, WIN) as i:
                    u = L * USES + OFF["win"] + i
                    for c in range(2):
                        lo(1 - c, u + c)
                        for j in range(2):
                            n = 2 * c + j
                            tile_done(dve, j, win_ready, L * 16 + 2 * i + c, c, u)
                            dve.tensor_scalar(P[:, ds(i * (4 * NT) + n * NT, NT)], PS[:, n, 0:NT], 1.0, None, ALU.mult).then_inc(win_used, 1)
                dve.wait_ge(win_used, L * 32 + 36)
                for n in range(6):
                    sc = SCALE if n < 3 else 1.0
                    dve.wait_ge(rot_ready, L * 6 + n + 1)
                    t1, t2 = tmp[2 * (n % 2)], tmp[2 * (n % 2) + 1]
                    link(dve.scalar_tensor_tensor(t1[:, :], pt(n), sc, cst("cos"), ALU.mult, ALU.mult))
                    link(dve.scalar_tensor_tensor(t2[:, :], PS[:, 4 + n % 2, 0:NT], sc, cst("sin"), ALU.mult, ALU.mult))
                    dve.tensor_tensor(pt(n), t1[:, :], t2[:, :], ALU.add).then_inc(roped, 1)
                z, e1, e2 = (tmp[j][0:BH, :] for j in range(3))
                link(dve.tensor_scalar(z, pt(T["ff"])[0:BH, :], fbcur[:, 0:1], None, ALU.add))
                dve.scalar_tensor_tensor(e1, z, -1.0, z, ALU.mult, ALU.max).then_inc(z_ready, 1)
                dve.wait_ge(z_exp, L * 2 + 1)
                dve.tensor_scalar(e2, e2, 1.0, None, ALU.add).then_inc(z_ready, 1)
                dve.wait_ge(z_exp, L * 2 + 2)
                link(dve.scalar_tensor_tensor(pt(T["ff"])[0:BH, :], z, 0.0, e1, ALU.min, ALU.subtract))
                dve.tensor_tensor_scan(ncn[:, 0:NT], cst("reset")[0:BH, :], pt(T["ff"])[0:BH, :], 0.0, ALU.mult, ALU.subtract).then_inc(lf_ready, 1)
                for n in range(15):
                    g, tt = divmod(n, 3)
                    r = 128 if tt < 2 else NS
                    dve.wait_ge(tt_ready, L * 16 + n + 1)
                    dve.tensor_copy(tok[0:r, tt, g * 384:(g + 1) * 384], PS[0:r, 4 + n % 4, 0:384]).then_inc(tt_used, 1)
                dve.wait_ge(tt_ready, L * 16 + 16)
                link(dve.tensor_copy(tokf[:, :, :], PS[:, 0, 0:24].rearrange("p (t c) -> p t c", t=3)[:, :, 0:BH]))
                dve.tensor_copy(tokn[:, :], PS[0:NS, 0, 24:24 + BH]).then_inc(tt_used, 1)
                for h in range(NH + 3):
                    if h < NH:
                        c = spr[h % 3]
                        dve.wait_ge(s_ready, L * NH + h + 1)
                        if h >= 3:
                            dve.wait_ge(pT_ready, L * NH + h - 2)
                        dve.tensor_tensor(c, PS[:, h % 2, 0:384], cst("causal"), ALU.add).then_inc(s_used, 1)
                        dve.wait_ge(s_used, L * NH + h + 1)
                        x = spx[:, 4 * (h % 3):4 * (h % 3) + 2]
                        dve.tensor_reduce(x[:, 0:1], c[:, 0:128], AX.X, ALU.max, negate=True).then_inc(smax, 1)
                        dve.tensor_reduce(x[:, 1:2], c[:, 128:384], AX.X, ALU.max, negate=True).then_inc(smax, 1)
                    if 1 <= h <= NH:
                        n = h - 1
                        c = spr[n % 3]
                        x = spx[:, 16 + 4 * (n % 3):16 + 4 * (n % 3) + 2]
                        dve.wait_ge(pexp, L * 2 * NH + 2 * n + 2)
                        link(dve.reciprocal(x, x))
                        dve.tensor_scalar(c[:, 0:128], c[:, 0:128], x[:, 0:1], None, ALU.mult).then_inc(p_ready, 1)
                        dve.tensor_scalar(c[:, 128:384], c[:, 128:384], x[:, 1:2], None, ALU.mult).then_inc(p_ready, 1)
                    if h >= 3 and (h - 3) in (1, 3, 5, 7, 9, 10):
                        pr = (1, 3, 5, 7, 9, 10).index(h - 3)
                        r = slice(0, 128) if pr < 5 else slice(64, 128)
                        dve.wait_ge(o_ready, L * NH + h - 2)
                        dve.tensor_copy(pt(OUT_T[pr])[r, 0:SEQ], PS[r, 4 + pr % 2, 0:SEQ]).then_inc(o_used, 1)
                q3, g3, k3 = p3(T["qc"]), p3(T["gc"]), p3(T["fc"])
                dve.wait_ge(h_sig, L * 3 + 3)
                link(dve.tensor_tensor(q3, q3, V(1), ALU.mult))
                link(dve.tensor_tensor(g3, g3, V(2), ALU.mult))
                for j in range(3):
                    link(dve.tensor_scalar(pt(T["fc"] + j), pt(T["fc"] + j), lbcur[:, 3 + j:4 + j], None, ALU.mult))
                give(h_qk)
                link(dve.memset(am[:, :, :], 0.0))
                link(dve.memset(asm[:, :, :], 0.0))
                dve.wait_ge(h_logf, L * 3 + 3)
                for j in range(3):
                    link(dve.tensor_tensor_scan(V(2)[:, j, :], cst("reset"), V(0)[:, j, :], 0.0, ALU.mult, ALU.add))
                lm = cst("lmask").rearrange("p (l t) -> p l t", l=LEVELS + 1).bitcast(I32)

                def take(n, mask):
                    dve.wait_ge(h_p, L * 9 + n + 1)
                    settle(dve)
                    bk = 4 * (n % 2)
                    for g in range(3):
                        nh = 2 if g < 2 else 1
                        ch.mark(dve.copy_predicated(
                            am[:, 2 * g:2 * g + nh, :].rearrange("p h (u t) -> p (h u) t", u=2),
                            lm[:, mask:mask + 1, :].to_broadcast([128, 2 * nh, 128]),
                            PS[:, bk + g, 0:256 * nh].rearrange("p (h t) -> p h t", t=128)))
                    if mask == LEVELS or mask < 3:
                        for a0, a1, g, c in ((0, 2, 3, 0), (2, 5, 2, 256)):
                            ch.mark(dve.copy_predicated(
                                asm[:, a0:a1, :], lm[0:NS, mask:mask + 1, 0:NS].to_broadcast([NS, a1 - a0, NS]),
                                PS[0:NS, bk + g, c:c + (a1 - a0) * NS].rearrange("p (h t) -> p h t", t=NS)))
                    ch.catch_up()
                    give(h_pused)

                for l in range(LEVELS + 1):
                    h = 1 << l
                    if l < 6:
                        seg = lambda x: x.rearrange("p (s c) -> p s c", c=2 * h)
                        dv, cv = seg(b[3][:, :]), seg(b[2][:, :])
                        qv, kv = (seg(P[:, T[w] * NT:(T[w] + 3) * NT]) for w in ("qc", "fc"))
                        gv = seg(b[4 if l % 2 == 0 else 0][:, :])
                        mid = cv[:, :, h - 1:h].to_broadcast([128, 3 * NT // (2 * h), 2 * h])
                        parts = [(dv, cv, qv, kv, gv, mid)]
                    else:
                        parts = []
                        for j in range(3):
                            ns = SEQ // (2 * h)
                            seg = lambda x: x.rearrange("p (s c) -> p s c", c=2 * h)
                            dv, cv = seg(V(3)[:, j, 0:SEQ]), seg(V(2)[:, j, 0:SEQ])
                            qv, kv = seg(pt(T["qc"] + j)[:, 0:SEQ]), seg(pt(T["fc"] + j)[:, 0:SEQ])
                            gv = seg(V(4 if l % 2 == 0 else 0)[:, j, 0:SEQ])
                            parts.append((dv, cv, qv, kv, gv, cv[:, :, h - 1:h].to_broadcast([128, ns, 2 * h])))
                    for dv, cv, qv, kv, gv, mid in parts:
                        link(dve.tensor_tensor(dv, cv, mid, ALU.subtract))
                    w = b[3][:, :] if l < 6 else V(3)[:, :, 0:SEQ]
                    dve.scalar_tensor_tensor(w, w, -1.0, w, ALU.mult, ALU.max).then_inc(h_abs, 1)
                    if l >= 1:
                        take(l, l - 1)
                    else:
                        take(0, LEVELS)
                    dve.wait_ge(h_e, L * 11 + l + 1)
                    for dv, cv, qv, kv, gv, mid in parts:
                        link(dve.tensor_tensor(gv[:, :, h:2 * h], dv[:, :, h:2 * h], qv[:, :, h:2 * h], ALU.mult))
                        link(dve.tensor_tensor(gv[:, :, 0:h], dv[:, :, 0:h], kv[:, :, 0:h], ALU.mult))
                    give(h_g)
                link(dve.tensor_tensor(V(3)[:, :, 0:SEQ], V(2)[:, :, 0:SEQ], V(2)[:, :, SEQ - 1:SEQ].to_broadcast([128, 3, SEQ]), ALU.subtract))
                for j in range(3):
                    v = lambda x: x[:, j, SEQ:NT].rearrange("p (b t) -> p b t", t=DS)
                    link(dve.tensor_tensor(v(V(3)), v(V(2)), v(V(2))[:, :, DS - 1:DS].to_broadcast([128, DB, DS]), ALU.subtract))
                give(h_abs)
                dve.wait_ge(h_e, L * 11 + 9)
                link(dve.tensor_tensor(qe[:, :, :], qe[:, :, :], q3[:, :, SEQ:NT], ALU.mult))
                dve.wait_ge(h_e, L * 11 + 11)
                link(dve.tensor_tensor(V(1), V(3), k3, ALU.mult))
                give(h_kd)
                for tt in range(3):
                    r = 128 if tt < 2 else NS
                    dve.wait_ge(h_kdT, L * 3 + tt + 1)
                    dve.tensor_copy(kdt[0:r, tt, :], PS[0:r, 4 + tt, 0:384]).then_inc(h_kdU, 1)
                vx = [b[0][0:NS, 0:512], P[0:NS, T["qc"] * NT:T["qc"] * NT + 512]]
                dve.wait_ge(h_o, L + 1)
                for e in range(CH):
                    if e >= 2:
                        dve.wait_ge(h_sn, L * CH + e - 1)
                    dve.tensor_tensor(vx[e % 2].rearrange("p (b e) -> p b e", b=DB),
                                      tok[0:NS, 2, 4 * 384 + HCOL[e]:4 * 384 + HCOL[e] + 64].rearrange("p (o e) -> p o e", o=1).to_broadcast([NS, DB, 64]),
                                      cst("seqof")[0:NS, :].rearrange("p (b o) -> p b o", o=1).to_broadcast([NS, DB, 64]),
                                      ALU.mult).then_inc(h_vx, 1)
                dve.wait_ge(h_st, L + 1)
                link(dve.tensor_copy(sp_[:, 0:2, :], PS[:, 7, 0:128].rearrange("p (j e) -> p j e", j=2)))
                dve.tensor_copy(sp_[64:128, 2, :], PS[64:128, 7, 128:192]).then_inc(h_stU, 1)
                dve.wait_ge(h_sn, L * CH + CH)
                for j in range(3):
                    r = slice(0, 128) if j < 2 else slice(64, 128)
                    n = 128 if j < 2 else 64
                    link(dve.tensor_tensor(s0[r, j, :, :], s0[r, j, :, :],
                                           el[r, j, :].rearrange("p (b o) -> p b o", o=1).to_broadcast([n, DB, 64]), ALU.mult))
                    dve.tensor_tensor(s0[r, j, :, :], s0[r, j, :, :], PS[r, 4 + j, :].rearrange("p (b e) -> p b e", b=DB), ALU.add).then_inc(h_snU, 1)
                dve.wait_ge(h_ms, L + 1)
                dve.tensor_scalar(V(3), PS[:, 4:7, 0:NT], 1.0 / HD, EPS, ALU.mult, ALU.add).then_inc(h_mse, 1)
                dve.wait_ge(h_rs, L + 1)
                for j in range(3):
                    link(dve.scalar_tensor_tensor(V(4)[:, j, :], PS[:, j, 0:NT], ghcur[:, 0:1], V(3)[:, j, :], ALU.mult, ALU.mult))
                dve.tensor_tensor(p3(T["ic"]), V(4), g3, ALU.mult).then_inc(h_out, 1)
                dve.wait_ge(out_st, L * 96 + 96)
                dve.wait_ge(h_out, L + 1)
                link(dve.memset(qb[:, :, :, :], 0.0))
                link(dve.memset(gm[:, :], 0.0))
                link(dve.memset(pe_[:, 1088:1152], 0.0))
                dve.wait_ge(qf_scaled, L + 1)
                for t0, p0, n, hf in ((T["qa"], 0, 3, 0), (T["qa"], 0, 3, 1), (T["qf"], 3, 2, 0), (T["qf"], 3, 3, 1)):
                    r = slice(64 * hf, 64 * hf + 64)
                    src = P[r, t0 * NT:(t0 + n) * NT].rearrange("p (j t) -> p j t", j=n)[:, :, SEQ:NT]
                    for j in range(n):
                        link(dve.tensor_copy(qb[r, p0 + j, :, 8 * hf:8 * hf + 8], src[:, j, :].rearrange("p (b t) -> p b t", t=DS)))
                nm = cst("newmask")[0:NS, :].rearrange("p (b t) -> p b t", b=DB)
                for h in range(NH):
                    if h < AH:
                        link(dve.tensor_copy(newb[:, :, 8 * h:8 * h + 8], nm))
                    else:
                        link(dve.tensor_scalar(newb[:, :, 8 * h:8 * h + 8], nm, tokn[:, h - AH:h - AH + 1], None, ALU.add))
                give(d_init)
                settle(dve)
                with dve.Fori(0, DB) as q:
                    ch.enter(q, 14)
                    Q = L * DB + q
                    for pg in range(NPG):
                        dve.wait_ge(kT_ready, Q * NPG + pg + 5)
                        dve.wait_ge(kT_used, Q * NPG + pg + 1)
                        dve.tensor_copy(ktp[:, pg % 2, 384:768], PS[:, 2 * (pg % 2) + 1, 0:384]).then_inc(kT_dve, 1)
                        if pg % 4 == 3:
                            n4 = pg // 4
                            if n4 == 0:
                                dve.wait_ge(kT_used, Q * NPG + 6)
                                dve.wait_ge(r_ready, Q + 1)
                            else:
                                dve.wait_ge(sT_ready, Q + 1)
                                dve.wait_ge(rn_ready, Q + 1)
                                link(dve.tensor_tensor(st[0:NS, 1, 352:440].rearrange("p (o c) -> p o c", o=1),
                                                       PS[0:NS, 4, 352:440].rearrange("p (o c) -> p o c", o=1), newb[:, ds(q, 1), :], ALU.add))
                            for g in range(4):
                                ins = dve.tensor_tensor(
                                    st[:, n4, 88 * g + 48:88 * g + 88].rearrange("p (h t) -> p h t", h=BH),
                                    PS[:, 4, 88 * g + 48:88 * g + 88].rearrange("p (h t) -> p h t", h=BH),
                                    pbias[:, ds(Q * NPG + n4 * 4 + g, 1), :].rearrange("p o h -> p h o").to_broadcast([128, BH, DS]), ALU.add)
                                if g == 3:
                                    ins.then_inc(sT_dve, 1)
                                else:
                                    link(ins)
                    dve.wait_ge(rn_ready, Q + 2)
                    for n4 in range(2):
                        link(dve.tensor_reduce(gs_[:, 0, 2 * n4:2 * n4 + 2], PS[0:48, 5 + n4, :].rearrange("p (n c) -> p n c", n=2), AX.X, ALU.add))
                    link(dve.tensor_reduce(gs_[:, 1, 0:1], gs_[:, 0, :], AX.X, ALU.min))
                    link(dve.scalar_tensor_tensor(gs_[:, 2, :], gs_[:, 0, :], gs_[:, 1, 0:1], cst("place")[0:48, :], ALU.is_equal, ALU.mult))
                    link(dve.tensor_reduce(gs_[:, 3, 0:1], gs_[:, 2, :], AX.X, ALU.max))
                    link(dve.tensor_scalar(gm[0:48, :], gs_[:, 2, :], gs_[:, 3, 0:1], NEG, ALU.is_equal, ALU.mult))
                    dve.tensor_tensor(sm[:, 0:1024].rearrange("p (n c) -> p n c", n=NBLK), PS[0:ROWS, 5:7, :].rearrange("p a (n c) -> p (a n) c", n=2),
                                      gm[:, :].rearrange("p (n o) -> p n o", o=1).to_broadcast([ROWS, NBLK, BLK]), ALU.add).then_inc(rows_used, 1)
                    dve.wait_ge(rows_used, Q + 2)
                    dve.wait_ge(rows_new, Q + 2)
                    dve.tensor_reduce(rs[:, 0:1], sm[:, :], AX.X, ALU.max, negate=True).then_inc(d_max, 1)
                    dve.wait_ge(d_exp, Q + 1)
                    link(dve.reciprocal(rs[:, 2:3], rs[:, 1:2]))
                    dve.tensor_scalar(pe_[:, 0:1088], pe_[:, 0:1088], rs[:, 2:3], None, ALU.mult).then_inc(dp_ready, 1)
                    dve.wait_ge(dpT_ready, Q * 2 + 1)
                    dve.tensor_copy(ptt[:, 0:5, :], PS[:, 0, 0:440].rearrange("p (g c) -> p g c", g=5)).then_inc(dpT_dve, 1)
                    dve.wait_ge(do_ready, Q + 2)
                    for r0, t0, p0, n in ((0, T["va"], 0, 3), (64, T["va"], 0, 3), (0, T["vf"], 3, 2), (64, T["vf"], 3, 3)):
                        r = slice(r0, r0 + 64)
                        dve.tensor_scalar(P[r, t0 * NT:(t0 + n) * NT].rearrange("p (j t) -> p j t", j=n)[:, :, ds(q * DS + SEQ, DS)],
                                          PS[r, 7, 16 * p0:16 * (p0 + n)].rearrange("p (j c) -> p j c", j=n)[:, :, r0 // 8:r0 // 8 + 8],
                                          1.0, None, ALU.mult).then_inc(do_used, 1)
                    assert ch.n == 14, ch.n
                    ch.leave(DB, 14)
                for k in range(9):
                    r = slice(64, 128) if k in (5, 8) else slice(0, 128)
                    dve.wait_ge(oh_ready, L * 9 + k + 1)
                    dve.tensor_tensor(xl[r, k, :], pt(OUT_T[k])[r, :], xh[r, k, :].bitcast(F32), ALU.subtract).then_inc(ol_ready, 1)
                link(dve.memset(sqsum[:, :], 0.0))
                settle(dve)
                with dve.Fori(0, 2) as m:
                    ch.enter(m, 8)
                    for dp in range(2):
                        u = L * USES + OFF["wout"] + m * 2 + dp
                        lo(1, u)
                        lo(0, u + 1)
                        accumulate(L * 24 + 8 + m * 4 + 2 * dp, L * 12 + 4 + m * 2 + dp, m * (4 * NT) + dp * 2 * NT, 4 + 2 * dp, 1.0, 1, u)
                    ch.leave(2, 8)
                give(sqsum_ready)
                norm(L * 3 + 2)
                scaled(L * 3 + 2, 2)
                ffn(1, L)
                assert ch.n == DVE_STEPS, ch.n
            ch.base, ch.n = DEPTH * DVE_STEPS + start_steps, 0
            norm(DEPTH * 3)
            dve.wait_ge(rstd_ready, DEPTH * 3 + 1)
            for k in range(KT_D):
                ins = dve.scalar_tensor_tensor(xt(k), xt(k), gains[:, DEPTH * 24 + k:DEPTH * 24 + k + 1], rstd[:, :], ALU.mult, ALU.mult)
                ins.then_inc(xs_ready, 1)
            for n in range(6):
                tt, hf = divmod(n, 2)
                r = 128 if tt < 2 else NS
                dve.wait_ge(f_T, n + 1)
                dve.tensor_copy(P[0:r, tt * 1024 + hf * 512:tt * 1024 + hf * 512 + 512], PS[0:r, n, :]).then_inc(f_U, 1)

        @block.tensor
        def _(te):
            ident = cst("ident")

            def dense(out, wslot, cols, rhs, ktiles, start, stop):
                hs, ls = rhs
                last = None
                for n, (kt, at, r) in enumerate(ktiles):
                    for m, (w, x) in enumerate(((whi, hs), (wlo, hs), (whi, ls))):
                        last = te.matmul(out, w[wslot][r, kt, cols], x[r, at, :],
                                         start=start and n == 0 and m == 0, stop=stop and n == len(ktiles) - 1 and m == 2)
                return last

            ALLR = slice(0, 128)

            def norm(w):
                te.wait_ge(sqsum_ready, w + 1)
                te.matmul(PS[:, 7, 0:NT], cst("ones"), sqsum[:, :], start=True, stop=True).then_inc(ms_ready, 1)

            def chunk(s, use):
                te.wait_ge(split_done[s], use + 2)

            def ffn(f, L, w):
                te.wait_ge(xl_ready, w * KT_D + KT_D)
                settle(te)
                u0 = L * USES + OFF[f"ffn{f + 1}"]
                kts = [(k, k, ALLR) for k in range(KT_D)]
                with te.Fori(0, GU) as i:
                    n0 = L * 2 * FT + f * FT + i * 2
                    for s in range(2):
                        chunk(s, u0 + i)
                        for j in range(2):
                            te.wait_ge(silu_done if s == 0 else up_used, n0 + j + 1)
                            dense(PS[:, 2 * s + j, 0:NT], s, slice(128 * j, 128 * j + 128), (xh, xl), kts, True, True
                                  ).then_inc(w_free[s] if j else (gate_ready, up_ready)[s], 1)
                te.wait_ge(h_done, L * 2 * FT + f * FT + FT)
                settle(te)
                u0 = L * USES + OFF[f"down{f + 1}"]
                with te.Fori(0, 2) as m:
                    for n in range(6):
                        dp, kk = divmod(n, 3)
                        chunk(n % 2, u0 + m * 3 + n // 2)
                        kts = [(k, kk * 8 + k, ALLR) for k in range(8 if kk < 2 else FT - 16)]
                        for j in range(2):
                            a0 = L * 24 + f * 16 + m * 4 + 2 * dp + j
                            if kk == 0:
                                te.wait_ge(acc_used, a0 + 1)
                            last = dense(PS[:, 4 + 2 * dp + j, 0:NT], n % 2, slice(128 * j, 128 * j + 128), (hh, hl), kts, kk == 0, kk == 2)
                            if j == 1:
                                last.then_inc(w_free[n % 2], 1)
                            elif kk == 2:
                                last.then_inc(acc_ready, 1)

            def scores(q, kts, n, c0):
                for pr in range(6):
                    w, qs = (16, slice(0, 16)) if pr < 5 else (8, slice(8, 16))
                    at = c0 + 16 * pr
                    last = te.matmul(PS[0:n, 4, at:at + w], kts[pr], qb[:, pr, ds(q, 1), qs].rearrange("p o c -> p (o c)"), start=True, stop=True)
                return last

            te.wait_ge(s_c, 16)
            te.wait_ge(s_x, 48)
            xtok = [raw[0].rearrange("p a b -> p (a b)")[:, 0:1024], raw[0].rearrange("p a b -> p (a b)")[:, 1024:2048],
                    raw[1].rearrange("p a b -> p (a b)")[:, 0:1024]]
            for n in range(6):
                tt, hf = divmod(n, 2)
                r = 128 if tt < 2 else NS
                for k in range(4):
                    last = te.transpose(PS[:, n, 128 * k:128 * k + r], xtok[tt][0:r, (4 * hf + k) * 128:(4 * hf + k + 1) * 128], ident[0:r, 0:r])
                last.then_inc(xT_ready, 1)
            te.wait_ge(s_small, 16 * SMALL)
            n = DEPTH * 24 + 8
            te.transpose(PS[:, 6, 0:n], vpg[0:n, 0, 0:128], ident[0:n, 0:n]).then_inc(gT_ready, 1)
            te.wait_ge(s_lf, 32)
            te.wait_ge(sqsum_ready, 1)
            G = DB * NPG
            for l in range(DEPTH):
                for h in range(BH):
                    last = te.transpose(PS[:, l, h * G:(h + 1) * G], vpg[0:G, 2 + l, 0:PAGE * BH].rearrange("p (k h) -> p h k", h=BH)[:, h, :], ident[0:G, 0:G])
                last.then_inc(lfT_ready, 1)
            te.wait_ge(later_ready, 1)
            for l in range(DEPTH):
                te.matmul(PS[:, 2 + l, 0:320], cst("later"), tok[:, 0, l * 320:(l + 1) * 320], start=True, stop=False)
                te.matmul(PS[:, 2 + l, 0:320], cst("ones"), tok[:, 1, l * 320:(l + 1) * 320], start=False, stop=True).then_inc(pb_ready, 1)
            with te.Fori(0, DEPTH) as L:
                norm(L * 3)
                ffn(0, L, L * 3)
                norm(L * 3 + 1)
                te.wait_ge(xl_ready, (L * 3 + 1) * KT_D + KT_D)
                settle(te)
                with te.Fori(0, WIN) as i:
                    for s in range(2):
                        chunk(s, L * USES + OFF["win"] + i)
                        for j in range(2):
                            te.wait_ge(win_used, L * 32 + i * 4 + 2 * s + j + 1)
                            dense(PS[:, 2 * s + j, 0:NT], s, slice(128 * j, 128 * j + 128), (xh, xl),
                                  [(k, k, ALLR) for k in range(KT_D)], True, True).then_inc(w_free[s] if j else win_ready, 1)
                te.wait_ge(win_used, L * 32 + 36)
                for n in range(6):
                    if n >= 2:
                        te.wait_ge(roped, L * 6 + n - 1)
                    te.matmul(PS[:, 4 + n % 2, 0:NT], cst("perm"), pt(n), start=True, stop=True).then_inc(rot_ready, 1)
                te.wait_ge(roped, L * 6 + 6)
                for n in range(15):
                    g, tt = divmod(n, 3)
                    t0 = T[("ka", "va", "kf", "vf", "ic")[g]]
                    if n >= 4:
                        te.wait_ge(tt_used, L * 16 + n - 3)
                    for j in range(3):
                        at = (t0 + j) * NT + tt * 128
                        last = te.transpose(PS[:, 4 + n % 4, 128 * j:128 * j + 128], P[:, at:at + 128], ident)
                    last.then_inc(tt_ready, 1)
                te.wait_ge(lf_ready, L + 1)
                settle(te)
                for tt in range(3):
                    at = T["ff"] * NT + tt * 128
                    te.transpose(PS[:, 0, 8 * tt:8 * tt + BH], P[0:BH, at:at + 128], ident[0:BH, 0:BH])
                te.transpose(PS[:, 0, 24:24 + BH], ncn[:, SEQ:SEQ + 128], ident[0:BH, 0:BH]).then_inc(tt_ready, 1)
                te.wait_ge(tt_used, L * 16 + 16)
                te.wait_ge(qf_scaled, L + 1)
                for h in range(NH + 2):
                    if h < NH:
                        moba = h < AH
                        j, hf = (h // 2, h % 2) if moba else HEADS5[h - AH]
                        r = slice(64 * hf, 64 * hf + 64)
                        qt, kt = pt((T["qa"] if moba else T["qf"]) + j), pt((T["ka"] if moba else T["kf"]) + j)
                        if h >= 2:
                            te.wait_ge(s_used, L * NH + h - 1)
                        for t in range(2):
                            out = PS[:, h % 2, 128 * t:128 * t + 128 * (t + 1)]
                            last = te.matmul(out, qt[r, 128 * t:128 * t + 128], kt[r, 0:128 * (t + 1)], start=True, stop=moba)
                            if not moba:
                                e = h - AH
                                last = te.matmul(out, ident[0:BH, e:e + 1].to_broadcast([BH, 128]), ncn[:, 0:128 * (t + 1)], start=False, stop=True)
                        last.then_inc(s_ready, 1)
                    if 1 <= h <= NH:
                        n = h - 1
                        te.wait_ge(p_ready, L * 2 * NH + 2 * n + 2)
                        if n >= 2:
                            te.wait_ge(pT_used, L * NH + n - 1)
                        for t in range(3):
                            last = te.transpose(PS[:, 2 + n % 2, 128 * t:128 * t + 128], spr[n % 3][:, 128 * t:128 * t + 128], ident)
                        last.then_inc(pT_ready, 1)
                    if h >= 2:
                        n = h - 2
                        moba = n < AH
                        e = n if moba else n - AH
                        pr = n // 2 if n < 10 else 5
                        hf = n % 2 if n < 10 else 1
                        te.wait_ge(pT_used, L * NH + n + 1)
                        if pr >= 2 and (n % 2 == 0):
                            te.wait_ge(o_used, L * 6 + pr - 1)
                        settle(te)
                        g, c0 = (1, 64 * e) if moba else (3, HCOL[e])
                        out = PS[64 * hf:64 * hf + 64, 4 + pr % 2, 0:SEQ]
                        te.matmul(out, tok[:, 0, g * 384 + c0:g * 384 + c0 + 64], ppt[n % 2][:, 0:256], start=True, stop=True)
                        te.matmul(out[:, 128:256], tok[:, 1, g * 384 + c0:g * 384 + c0 + 64], ppt[n % 2][:, 256:384], start=False, stop=True,
                                  skip_group_check=True).then_inc(o_ready, 1)
                te.wait_ge(h_qk, L + 1)
                te.wait_ge(o_used, L * 6 + 6)
                for n in range(9):
                    if n >= 2:
                        te.wait_ge(h_pused, L * 8 + n - 1)
                    if n >= 1:
                        te.wait_ge(h_g, L * 8 + n)
                    settle(te)
                    bk = 4 * (n % 2)
                    for at, h in enumerate(ORD):
                        j, hf = HEADS5[h]
                        r = slice(64 * hf, 64 * hf + 64)
                        if n == 0:
                            kk, qq = pt(T["fc"] + j), pt(T["qc"] + j)
                        else:
                            kk = qq = V_(4 if n % 2 == 1 else 0, j)
                        if n < 8:
                            for t in range(2):
                                c = 256 * (at % 2) + 128 * t
                                last = te.matmul(PS[:, bk + at // 2, c:c + 128],
                                                 kk[r, 128 * t:128 * t + 128], qq[r, 128 * t:128 * t + 128], start=True, stop=True)
                            if n < 4:
                                c = NS * at if at < 2 else 256 + NS * (at - 2)
                                last = te.matmul(PS[0:NS, bk + (3 if at < 2 else 2), c:c + NS], kk[r, SEQ:NT], qq[r, SEQ:NT], start=True, stop=True)
                        else:
                            c = 128 * (at if at < 2 else at - 2)
                            last = te.matmul(PS[:, bk + (0 if at < 2 else 1), c:c + 128], kk[r, 0:128], qq[r, 128:256], start=True, stop=True)
                    last.then_inc(h_p, 1)
                te.wait_ge(h_kd, L + 1)
                te.wait_ge(h_pused, L * 8 + 8)
                for tt in range(2):
                    for j in range(3):
                        last = te.transpose(PS[:, 4 + tt, 128 * j:128 * j + 128], V_(1, j)[:, 128 * tt:128 * tt + 128], ident)
                    last.then_inc(h_kdT, 1)
                for j in range(3):
                    last = te.matmul(PS[0:NS, 6, 128 * j:128 * j + 128], V_(1, j)[:, SEQ:NT], ident, start=True, stop=True)
                last.then_inc(h_kdT, 1)
                te.wait_ge(h_ac, L * 2 + 2)
                te.wait_ge(s0_in, L * 48 + 48)
                for j, hf, h in VH:
                    r = slice(64 * hf, 64 * hf + 64)
                    c = 4 * 384 + 128 * j + 64 * hf
                    o, at = PS[r, j, :], ORD.index(h)
                    te.matmul(o[:, 0:128], tok[:, 0, c:c + 64], am[:, at, 0:128], start=True, stop=True)
                    te.matmul(o[:, 128:256], tok[:, 0, c:c + 64], ac[:, at, :], start=True, stop=False)
                    te.matmul(o[:, 128:256], tok[:, 1, c:c + 64], am[:, at, 128:256], start=False, stop=True)
                    last = te.matmul(o[:, 256:320], tok[0:NS, 2, c:c + 64], asm[:, at, :], start=True, stop=False, skip_group_check=True)
                last.then_inc(h_oa, 1)
                te.wait_ge(h_oa, L + 1)
                settle(te)
                for j, hf, h in VH:
                    r = slice(64 * hf, 64 * hf + 64)
                    o = PS[r, j, :]
                    for q in range(DB):
                        last = te.matmul(o[:, 256 + 8 * q:264 + 8 * q], s0[r, j, q, :], qe[r, j, 8 * q:8 * q + 8], start=False, stop=q == DB - 1, skip_group_check=True)
                last.then_inc(h_o, 1)
                te.wait_ge(h_kdU, L * 3 + 3)
                settle(te)
                for e, (j, hf) in enumerate(HEADS5):
                    r = slice(64 * hf, 64 * hf + 64)
                    for tt in range(2):
                        last = te.matmul(PS[r, 7, 64 * j:64 * j + 64], kdt[:, tt, HCOL[e]:HCOL[e] + 64], tok[:, tt, 4 * 384 + HCOL[e]:4 * 384 + HCOL[e] + 64],
                                         start=tt == 0, stop=tt == 1)
                last.then_inc(h_st, 1)
                for e, (j, hf) in enumerate(HEADS5):
                    r = slice(64 * hf, 64 * hf + 64)
                    te.wait_ge(h_vx, L * CH + e + 1)
                    settle(te)
                    vx = [b[0][0:NS, 0:512], P[0:NS, T["qc"] * NT:T["qc"] * NT + 512]][e % 2]
                    te.matmul(PS[r, 4 + j, :], kdt[0:NS, 2, HCOL[e]:HCOL[e] + 64], vx, start=True, stop=True).then_inc(h_sn, 1)
                te.wait_ge(h_sq, L + 1)
                te.wait_ge(h_snU, L * 3 + 3)
                for j in range(3):
                    last = te.matmul(PS[:, 4 + j, 0:NT], cst("blk"), V_(4, j), start=True, stop=True)
                last.then_inc(h_ms, 1)
                te.wait_ge(d_init, L + 1)
                settle(te)
                with te.Fori(0, DB) as q:
                    Q = L * DB + q
                    for pg in range(NPG + 1):
                        if pg < NPG:
                            s = pg % 4
                            te.wait_ge(k_in[s], (Q * 2 + pg // 4) * 32 + 32)
                            te.wait_ge(kT_act, Q * NPG + pg + 1)
                            te.wait_ge(kT_dve, Q * NPG + pg + 1)
                            for j, c in enumerate((0, 128, 256, AW, AW + 128, AW + 192)):
                                last = te.transpose(PS[:, 2 * (pg % 2) + j // 3, 128 * (j % 3):128 * (j % 3) + 128], kpg[:, s, c:c + 128], ident)
                            last.then_inc(kT_ready, 1)
                        if pg >= 1:
                            m = pg - 1
                            if m % 4 == 0:
                                te.wait_ge(sT_act, Q * 2 + m // 4 + 1)
                                te.wait_ge(sT_dve, Q * 2 + m // 4 + 1)
                            te.wait_ge(kT_act, Q * NPG + m + 3)
                            te.wait_ge(kT_dve, Q * NPG + m + 3)
                            last = scores(q, [ktp[:, m % 2, 128 * j:128 * j + 128] for j in range(6)], 128, 88 * (m % 4))
                            last.then_inc(kT_used, 1)
                            if m == NPG - 1:
                                kts = [pt(T["ka"] + j)[:, SEQ:NT] for j in range(3)] + [pt(T["kf"] + j)[:, SEQ:NT] for j in range(3)]
                                last = scores(q, kts, NS, 352)
                                last.then_inc(sT_ready, 1)
                            if m % 4 == 3:
                                n4 = m // 4
                                if n4 == 0:
                                    te.wait_ge(rows_used, Q + 1)
                                    te.wait_ge(rows_new, Q + 1)
                                te.wait_ge(sT_act, Q * 2 + n4 + 2)
                                te.wait_ge(sT_dve, Q * 2 + n4 + 2)
                                for g in range(4):
                                    last = te.transpose(PS[0:ROWS, 5 + n4, 128 * g:128 * g + 128], st[:, n4, 88 * g:88 * g + 88], ident)
                                if n4 == 0:
                                    last.then_inc(r_ready, 1)
                    te.wait_ge(sT_dve, Q * 2 + 3)
                    settle(te)
                    te.transpose(PS[0:ROWS, 7, 128:192], st[0:NS, 1, 352:440], ident[0:NS, 0:NS]).then_inc(rn_ready, 1)
                    te.wait_ge(dp_ready, Q + 1)
                    for g in range(9):
                        last = te.transpose(PS[:, g // 5, 88 * (g % 5):88 * (g % 5) + 88], pe_[:, 128 * g:128 * g + 128], ident[0:ROWS, 0:ROWS])
                        if g in (4, 8):
                            last.then_inc(dpT_ready, 1)
                    te.wait_ge(dpT_act, Q + 1)
                    te.wait_ge(dpT_dve, Q + 1)
                    te.wait_ge(do_used, Q * 4 + 4)
                    te.wait_ge(rows_new, Q + 2)
                    for g in range(9):
                        if g < NPG:
                            te.wait_ge(v_in[g], Q * 32 + 32)
                        for pr in range(6):
                            c = (0, 128, 256, AW, AW + 128, AW + 192)[pr]
                            if g < NPG:
                                v, p = vpg[:, g, c:c + 128], ptt[:, g, :]
                            else:
                                gc = (1 if pr < 3 else 3) * 384 + 128 * (pr % 3)
                                v, p = tok[0:NS, 2, gc:gc + 128], ptt[0:NS, g, :]
                            c0, c1, o0 = (16 * pr, 16 * pr + 16, 16 * pr) if pr < 5 else (80, 88, 88)
                            last = te.matmul(PS[:, 7, o0:o0 + c1 - c0], v, p[:, c0:c1], start=g == 0 and pr == 0, stop=g == 8, skip_group_check=True)
                    last.then_inc(do_ready, 1)
                te.wait_ge(ol_ready, L * 9 + 9)
                settle(te)
                with te.Fori(0, 2) as m:
                    for dp in range(2):
                        for s in range(2):
                            chunk(s, L * USES + OFF["wout"] + m * 2 + dp)
                            if s == 0:
                                kts = [(k, k, ALLR) for k in range(5)] + [(5, 5, slice(64, 128))]
                            else:
                                kts = [(0, 6, ALLR), (1, 7, ALLR), (2, 8, slice(64, 128))]
                            for j in range(2):
                                if s == 0:
                                    te.wait_ge(acc_used, L * 24 + 8 + m * 4 + 2 * dp + j + 1)
                                last = dense(PS[:, 4 + 2 * dp + j, 0:NT], s, slice(128 * j, 128 * j + 128), (xh, xl), kts, s == 0, s == 1)
                                if j == 1:
                                    last.then_inc(w_free[s], 1)
                                elif s == 1:
                                    last.then_inc(acc_ready, 1)
                norm(L * 3 + 2)
                ffn(1, L, L * 3 + 2)
            norm(DEPTH * 3)
            te.wait_ge(xs_ready, DEPTH * 3 * KT_D + KT_D)
            for n in range(6):
                tt, hf = divmod(n, 2)
                for k in range(4):
                    at = (4 * hf + k) * NT + tt * 128
                    last = te.transpose(PS[:, n, 128 * k:128 * k + 128], X[:, at:at + 128], ident)
                last.then_inc(f_T, 1)


INS = ["x_prompt", "x_sample", "cache_moba_k", "cache_moba_v", "cache_fox_k", "cache_fox_v", "cache_fox_logf", "state_hgrn",
       "page_table", "norm_ffn1_g", "ffn1_w_gate", "ffn1_w_up", "ffn1_w_down", "norm_mix_g", "w_in", "fox_f_bias",
       "hgrn_lb_logits", "hgrn_norm_g", "w_out", "norm_ffn2_g", "ffn2_w_gate", "ffn2_w_up", "ffn2_w_down", "norm_final_g"]
OUTS = [("y_prompt", (1, SEQ, D)), ("y_sample", (DB, DS, D)),
        ("moba_k_prompt", (DEPTH, 1, SEQ, AH, HD)), ("moba_v_prompt", (DEPTH, 1, SEQ, AH, HD)),
        ("fox_k_prompt", (DEPTH, 1, SEQ, BH, HD)), ("fox_v_prompt", (DEPTH, 1, SEQ, BH, HD)),
        ("fox_logf_prompt", (DEPTH, 1, SEQ, BH)), ("hgrn_state_prompt", (DEPTH, 1, CH, HD, HD)),
        ("moba_k_sample", (DEPTH, DB, DS, AH, HD)), ("moba_v_sample", (DEPTH, DB, DS, AH, HD)),
        ("fox_k_sample", (DEPTH, DB, DS, BH, HD)), ("fox_v_sample", (DEPTH, DB, DS, BH, HD)),
        ("fox_logf_sample", (DEPTH, DB, DS, BH)), ("hgrn_state_sample", (DEPTH, DB, CH, HD, HD))]


def kernel(**inputs):
    import concourse.bacc as bacc
    from concourse.bass_utils import run_bass_kernel_spmd

    nc = bacc.Bacc("TRN2", target_bir_lowering=False, num_devices=1)
    arrays, a = {}, {}
    for name in INS + ["consts"]:
        v = constants() if name == "consts" else np.ascontiguousarray(inputs[name])
        arrays["in_" + name] = v
        a[name] = nc.dram_tensor("in_" + name, v.shape, mybir.dt.from_np(v.dtype), kind="ExternalInput").ap()
    outs = {n: nc.dram_tensor("out_" + n, s, F32, kind="ExternalOutput").ap() for n, s in OUTS}
    trunk(nc, a, outs)
    r = run_bass_kernel_spmd(nc, [arrays], core_ids=[0])
    return tuple(r.results[0]["out_" + n] for n, _ in OUTS)
```

```python
from contextlib import ExitStack

import numpy as np

import concourse.bass as bass
from concourse import mybir

F32 = mybir.dt.float32
F32R = mybir.dt.float32r
I32 = mybir.dt.int32
U32 = mybir.dt.uint32
ALU = mybir.AluOpType
ACT = mybir.ActivationFunctionType
AX = mybir.AxisListType
ds = bass.ds

D, SEQ, DEPTH, DB, DS = 1024, 256, 2, 8, 8
PAST, PAGE = 1024, 128
HD, AH, BH, CH = 64, 6, 5, 5
FF = 2816
NS = DB * DS
NT = SEQ + NS
KT_D = D // 128
FT = FF // 128
NPG = PAST // PAGE
NPOOL = DB * NPG * 5 // 4
BLK = 256
NBLK = PAST // BLK
EPS, NEG = 1e-6, -1e30
SCALE = HD ** -0.5
AW, BW = AH * HD, BH * HD
NH = AH + BH
ROWS = NH * DS
LEVELS = 7

_THIRD = [0, 128, 192]
_col = {}
_c = 0
for _n, _w in (("qa", AW), ("ka", AW), ("va", AW), ("qf", BW), ("kf", BW), ("vf", BW), ("ff", BH),
               ("qc", BW), ("fc", BW), ("ic", BW), ("gc", BW)):
    _col[_n] = _c
    _c += _w
D_IN = _c
TILES, T = [], {}
for _n in ("qa", "ka", "va", "qf", "kf", "vf", "ff", "qc", "fc", "ic", "gc"):
    T[_n] = len(TILES)
    if _n == "ff":
        TILES += [_col[_n]]
    elif _n in ("qa", "ka", "va"):
        TILES += [_col[_n] + 128 * j for j in range(3)]
    else:
        TILES += [_col[_n] + _THIRD[j] for j in range(3)]
TILES += [TILES[-1]]
WIN_CHUNKS = len(TILES) // 2
OUT_T = [T["va"], T["va"] + 1, T["va"] + 2, T["vf"], T["vf"] + 1, T["vf"] + 2, T["ic"], T["ic"] + 1, T["ic"] + 2]
HEADS5 = [(0, 0), (0, 1), (1, 0), (1, 1), (2, 1)]
ORD = [0, 2, 1, 3, 4]
HCOL = [0, 64, 128, 192, 320]

GU, DOWN, WIN, WOUT = FT // 2, 6, WIN_CHUNKS // 2, 4
OFF = {"ffn1": 0, "down1": GU, "win": GU + DOWN, "wout": GU + DOWN + WIN,
       "ffn2": GU + DOWN + WIN + WOUT, "down2": 2 * GU + DOWN + WIN + WOUT}
USES = 2 * GU + 2 * DOWN + WIN + WOUT

C, _w0 = {}, 0
for _n, _w in (("ident", 128), ("ones", 128), ("blk", 128), ("perm", 128), ("cos", NT), ("sin", NT),
               ("causal", 384), ("lmask", (LEVELS + 1) * 128), ("reset", NT), ("newmask", DB * DS),
               ("later", 128), ("seqof", DB), ("place", NBLK),
               ("hsel", NH * DS), ("rowsel", DEPTH * DB)):
    C[_n] = (_w0, _w)
    _w0 += _w
NC_COLS = _w0


def constants():
    c = np.zeros((128, NC_COLS), np.float32)

    def put(name, a):
        o, w = C[name]
        c[:a.shape[0], o:o + w] = a.reshape(a.shape[0], w)

    i = np.arange(128)
    put("ident", np.eye(128))
    put("ones", np.ones((128, 128)))
    put("blk", (i[:, None] // 64 == i[None, :] // 64).astype(np.float32))
    perm = np.zeros((128, 128))
    for m in range(128):
        if m % 64 < 32:
            perm[m + 32, m] = -1.0
        else:
            perm[m - 32, m] = 1.0
    put("perm", perm)
    half = HD // 2
    inv = np.power(np.float32(10000.0), -np.arange(half, dtype=np.float32) * np.float32(2.0) / np.float32(HD))
    pos = np.concatenate([np.arange(SEQ), np.tile(PAST + np.arange(DS), DB)]).astype(np.float32)
    ang = (pos[None, :] * inv[i % half, None]).astype(np.float32)
    put("cos", np.cos(ang))
    put("sin", np.sin(ang))
    tri = np.where(i[None, :] <= i[:, None], 0.0, NEG)
    put("causal", np.concatenate([tri, np.zeros((128, 128)), tri], 1))
    lm = np.zeros((128, LEVELS + 1, 128))
    for l in range(LEVELS):
        h = 1 << l
        s, t = i[:, None], i[None, :]
        lm[:, l] = (s // (2 * h) == t // (2 * h)) & (s % (2 * h) < h) & (t % (2 * h) >= h)
    lm[:, LEVELS] = np.eye(128)
    put("lmask", lm)
    reset = np.ones((128, NT))
    reset[:, 0] = 0
    reset[:, SEQ::DS] = 0
    put("reset", reset)
    k = np.arange(NS)
    nm = np.full((NS, DB, DS), NEG)
    for b in range(DB):
        for t in range(DS):
            nm[(k // DS == b) & (k % DS <= t), b, t] = 0.0
    put("newmask", nm)
    put("later", (i[:, None] > i[None, :]).astype(np.float32))
    put("seqof", (k[:, None] // DS == np.arange(DB)[None, :]).astype(np.float32))
    r = np.arange(DEPTH * BH * DB)
    put("hsel", (np.arange(ROWS)[None, :] // DS == AH + (r[:, None] // DB) % BH).astype(np.float32))
    q = np.arange(DEPTH * DB)
    put("rowsel", ((r[:, None] // (BH * DB) == q[None, :] // DB) & (r[:, None] % DB == q[None, :] % DB)).astype(np.float32))
    put("place", np.tile(2.0 ** np.arange(NBLK), (128, 1)))
    return c


ACT_STEPS = 5
DVE_STEPS = 382
DECODE_STEPS = 17


class Chain:

    def __init__(self, eng, sem):
        self.eng, self.sem, self.base, self.n = eng, sem, 0, 0

    def mark(self, ins):
        self.n += 1
        return ins.then_inc(self.sem, 1)

    def catch_up(self):
        self.eng.wait_ge(self.sem, self.base + self.n)

    def link(self, ins):
        self.mark(ins)
        self.catch_up()

    def enter(self, i, steps):
        self._out = (self.base, self.n)
        self.base, self.n = self.base + self.n + i * steps, 0

    def leave(self, trips, steps):
        assert self.n == steps, (self.n, steps)
        self.base, self.n = self._out[0], self._out[1] + trips * steps


def trunk(nc, a, outs):
    ctx = ExitStack()
    with ctx:
        def sb(name, shape, dt=F32, into=ctx):
            return into.enter_context(nc.sbuf_tensor(name, shape, dt))

        def sem(name):
            return ctx.enter_context(nc.semaphore(name))

        X = sb("X", [128, KT_D * NT + 64])
        xt = lambda k: X[:, k * NT:(k + 1) * NT]
        K = sb("K", [128, NC_COLS])
        cst = lambda name: K[:, C[name][0]:C[name][0] + C[name][1]]
        gains = sb("gains", [128, DEPTH * 24 + 8])
        gcur = sb("gcur", [128, 24])
        lbt = sb("lbt", [128, DEPTH, 6])
        lbcur = sb("lbcur", [128, 6])
        gh = sb("gh", [128, DEPTH])
        ghcur = sb("ghcur", [128, 1])
        fb = sb("fb", [BH, DEPTH])
        fbcur = sb("fbcur", [BH, 1])
        pages = sb("pages", [1, DB * NPG], I32)
        brow = sb("brow", [DEPTH * BH * DB, PAST])
        ncn = sb("ncn", [BH, NT + 64])
        tokn = sb("tokn", [NS, BH])
        sqsum = sb("sqsum", [128, NT])
        rstd = sb("rstd", [128, NT])
        tmp = [sb(f"tmp{j}", [128, NT]) for j in range(4)]
        raw = [sb(f"raw{s}", [128, 8, 256]) for s in range(2)]
        whi = [sb(f"whi{s}", [128, 8, 256], F32R) for s in range(2)]
        wlo = [sb(f"wlo{s}", [128, 8, 256], F32R) for s in range(2)]
        with ExitStack() as r1:
            xh = sb("xh", [128, 9, NT], F32R, r1)
            xl = sb("xl", [128, 9, NT], F32R, r1)
        vpg = sb("vpg", [128, NPG, AW + BW])
        vfill = sb("vfill", [128, 18 * NT - NPG * (AW + BW)])
        with ExitStack() as r2:
            hh = sb("hh", [128, FT, NT], F32R, r2)
            hl = sb("hl", [128, FT, NT], F32R, r2)
        P = sb("P", [128, 32 * NT + 64])
        pt = lambda n: P[:, n * NT:(n + 1) * NT]
        p3 = lambda n: P[:, n * NT:(n + 3) * NT].rearrange("p (j t) -> p j t", j=3)
        tok = sb("tok", [128, 3, 5 * 384])
        tokf = sb("tokf", [128, 3, BH])
        with ExitStack() as r3:
            b = [sb(f"b{i}", [128, 3 * NT], F32, r3) for i in range(5)]
            kdt = sb("kdt", [128, 3, 384], F32, r3)
            am = sb("am", [128, CH, 256], F32, r3)
            ac = sb("ac", [128, CH, 128], F32, r3)
            s0 = sb("s0", [128, 3, DB, 64], F32, r3)
        with ExitStack() as r4:
            kpg = sb("kpg", [128, 4, AW + BW], F32, r4)
            smn = sb("smn", [ROWS, NS], F32, r4)
            smna = sb("smna", [ROWS, DB, NS], F32, r4)
            pe_ = sb("pe_", [ROWS, 1152], F32, r4)
            ptt = sb("ptt", [128, 9, ROWS], F32, r4)
            ob = sb("ob", [ROWS, AW + BW], F32, r4)
            qb = sb("qb", [128, 6, DB, 16], F32, r4)
            qz = sb("qz", [128, 6, ROWS], F32, r4)
            sel = sb("sel", [DEPTH * BH * DB, ROWS], F32, r4)
            newb = sb("newb", [NS, DB, ROWS], F32, r4)
            gm = sb("gm", [ROWS, NBLK + 1], F32, r4)
            gs_ = sb("gs_", [48, 4, NBLK], F32, r4)
            bm = sb("bm", [ROWS, NBLK + 1], F32, r4)
            nb = sb("nb", [ROWS, NBLK + 1], F32, r4)
            es = sb("es", [ROWS, NBLK + 1], F32, r4)
            rs = sb("rs", [ROWS, 2], F32, r4)
        qe = tmp[0][:, 0:192].rearrange("p (j t) -> p j t", j=3)
        el = tmp[0][:, 192:216].rearrange("p (j t) -> p j t", j=3)
        asm = tmp[1][0:NS, :].rearrange("p (h t) -> p h t", h=CH)
        sp_ = tmp[3][:, 0:192].rearrange("p (j t) -> p j t", j=3)
        ktb = [tok[:, n, 0:1536].rearrange("p (j c) -> p j c", j=6) for n in range(2)]
        V_ = lambda i, j: b[i][:, j * NT:(j + 1) * NT]
        VH = [(0, 0, 0), (0, 1, 1), (1, 0, 2), (1, 1, 3), (2, 0, 3), (2, 1, 4)]
        spr = [b[0][:, 0:384], b[0][:, 384:768], b[1][:, 0:384]]
        ppt = [b[1][:, 384:768], b[2][:, 0:384]]
        spx = b[2][:, 384:432]
        PS = ctx.enter_context(nc.psum_tensor("PS", [128, 8, 512], F32))

        s_c = sem("consts_in")
        waited = sem("waited")
        s_small = sem("small_in")
        s_x = sem("x_in")
        s_lf = sem("past_logf_in")
        s_idx = sem("page_rows_ready")
        s_pages = sem("page_table_in")
        lb_diff, lb_sig = sem("lb_diff"), sem("lb_sig")
        s_dve, s_act = sem("vector_step"), sem("scalar_step")
        raw_in = [sem(f"raw_in{s}") for s in range(2)]
        hi_done = [sem(f"hi_done{s}") for s in range(2)]
        split_done = [sem(f"split_done{s}") for s in range(2)]
        w_free = [sem(f"weights_free{s}") for s in range(2)]
        gate_ready, silu_done, up_ready, up_used, h_done = (
            sem(n) for n in ("gate_ready", "silu_done", "up_ready", "up_used", "h_done"))
        acc_ready, acc_used = sem("acc_ready"), sem("acc_used")
        ms_ready, sqsum_ready, rstd_ready, xs_ready, xh_ready, xl_ready, ms_eps = (
            sem(n) for n in ("ms_ready", "sqsum_ready", "rstd_ready", "xs_ready", "xh_ready", "xl_ready", "ms_eps"))
        win_ready, win_used = sem("win_ready"), sem("win_used")
        rot_ready, roped = sem("rot_ready"), sem("roped")
        qf_scaled = sem("qf_scaled")
        z_ready, z_exp, lf_ready = sem("z_ready"), sem("z_ln"), sem("lf_ready")
        tt_ready, tt_used = sem("tok_ready"), sem("tok_used")
        s_ready, p_ready, pT_ready, pT_used, o_ready, o_used, smax, pexp, s_used = (
            sem(n) for n in ("ps_ready", "pp_ready", "ppT_ready", "ppT_used", "po_ready", "po_used",
                             "p_max", "p_exp", "ps_used"))
        h_oa = sem("h_oa")
        h_sig, h_qk, h_logf = (sem(n) for n in ("h_sig", "h_qk", "h_logf"))
        h_abs, h_e, h_g, h_p, h_pused, h_ac = (sem(n) for n in ("h_abs", "h_e", "h_g", "h_p", "h_pused", "h_ac"))
        h_kd, h_kdT, h_kdU, h_o, h_sq, h_ms, h_mse, h_rs, h_out = (
            sem(n) for n in ("h_kd", "h_kdT", "h_kdU", "h_o", "h_sq", "h_ms", "h_mse", "h_rs", "h_out"))
        h_st, h_stU, h_vx, h_sn, h_snU, s0_in = (sem(n) for n in ("h_st", "h_stU", "h_vx", "h_sn", "h_snU", "s0_in"))
        k_in = [sem(f"k_in{j}") for j in range(4)]
        v_in = [sem(f"v_in{j}") for j in range(NPG)]
        q_ready = sem("q_ready")
        d_init, kT_ready, kT_act, kT_dve, qz_ready, sn_ready, sn_used, snT_ready, snT_used = (
            sem(n) for n in ("d_init", "kT_ready", "kT_act", "kT_dve", "qz_ready", "sn_ready", "sn_used", "snT_ready", "snT_used"))
        d_bias, d_exp, d_norm, v_used, ob_ready, obT_ready = (
            sem(n) for n in ("d_bias", "d_exp", "d_norm", "v_used", "ob_ready", "obT_ready"))
        dpT_ready, dpT_act, dpT_dve, do_ready, do_used, kT_used = (
            sem(n) for n in ("dpT_ready", "dpT_act", "dpT_dve", "do_ready", "do_used", "kT_used"))
        xT_ready, gT_ready, lfT_ready, pb_ready, later_ready = (
            sem(n) for n in ("xT_ready", "gT_ready", "lfT_ready", "pb_ready", "later_ready"))
        pbT_used, pbT_ready = sem("pb_copied"), sem("pbT_ready")
        oh_ready, ol_ready = sem("oh_ready"), sem("ol_ready")
        f_T, f_U, f_out = sem("y_ready"), sem("y_copied"), sem("y_out")
        out_tok, out_st = sem("out_tok"), sem("out_state")

        block = ctx.enter_context(nc.Block())
        SMALL = DEPTH * 9 + 2

        wg = [a["ffn1_w_gate"], a["ffn2_w_gate"]]
        wu = [a["ffn1_w_up"], a["ffn2_w_up"]]
        wd = [a["ffn1_w_down"], a["ffn2_w_down"]]
        gu_v = lambda w: w.rearrange("l (k p) n -> p (l k) n", p=128)

        def tile_done(eng, j, first_ready, n, s, use):
            if j == 0:
                eng.wait_ge(first_ready, n + 1)
            else:
                eng.wait_ge(w_free[s], use + 2)

        def settle(eng):
            eng.sem_inc(waited, 1)

        @block.sync
        def _(sp):
            def fill(s, use, parts):
                sp.wait_ge(split_done[s], use + 1)
                for n, (dst, src) in enumerate(parts):
                    ins = sp.dma_start(dst, src)
                    ins.then_inc(raw_in[s], 16 if len(parts) == 2 else 32)

            def gu_chunk(f, L, i):
                u = L * USES + OFF[f"ffn{f + 1}"] + i
                for s, w in ((0, wg[f]), (1, wu[f])):
                    fill(s, u, [(raw[s][:, :, :], gu_v(w)[:, ds(L * 8, 8), ds(i * 256, 256)])])

            def down_chunks(f, L):
                wdv = wd[f].rearrange("l (k p) n -> p (l k) n", p=128)
                with sp.Fori(0, 2) as m:
                    for n in range(6):
                        dp, kk = divmod(n, 3)
                        nk = 8 if kk < 2 else FT - 16
                        fill(n % 2, L * USES + OFF[f"down{f + 1}"] + m * 3 + n // 2,
                             [(raw[n % 2][:, 0:nk, :], wdv[:, ds(L * FT + kk * 8, nk), ds(m * 512 + dp * 256, 256)])])

            def wout_chunks(L, m):
                u = L * USES + OFF["wout"] + m
                rows = lambda r0, n: a["w_out"][ds(L, 1), r0:r0 + n, ds(m * 256, 256)]
                fill(0, u, [(raw[0][:, 0:5, :], rows(0, 640).rearrange("l (k p) n -> p (l k) n", p=128)),
                            (raw[0][64:128, 5, :], rows(640, 64).rearrange("l p n -> (l p) n"))])
                fill(1, u, [(raw[1][:, 0:2, :], rows(704, 256).rearrange("l (k p) n -> p (l k) n", p=128)),
                            (raw[1][64:128, 2, :], rows(960, 64).rearrange("l p n -> (l p) n"))])

            sp.dma_start(K[:, :], a["consts"]).then_inc(s_c, 16)
            sp.dma_start(pages[:, :], a["page_table"].rearrange("(o b) n -> o (b n)", o=1)).then_inc(s_pages, 16)
            xtok = [raw[0].rearrange("p a b -> p (a b)")[:, 0:1024], raw[0].rearrange("p a b -> p (a b)")[:, 1024:2048],
                    raw[1].rearrange("p a b -> p (a b)")[:, 0:1024]]
            xp = a["x_prompt"].rearrange("b (n p) d -> (b n) p d", p=128)
            for n in range(2):
                sp.dma_start(xtok[n], xp[n]).then_inc(s_x, 16)
            sp.dma_start(xtok[2][0:NS, :], a["x_sample"].rearrange("b t d -> (b t) d")).then_inc(s_x, 16)
            sp.wait_ge(s_pages, 16)
            gu_chunk(0, 0, 0)
            with sp.Fori(0, DEPTH) as L:
                with sp.Fori(1, GU) as i:
                    gu_chunk(0, L, i)
                down_chunks(0, L)
                winv = a["w_in"].rearrange("l (k p) n -> p (l k) n", p=128)
                for c in range(WIN_CHUNKS):
                    s = c % 2
                    fill(s, L * USES + OFF["win"] + c // 2,
                         [(raw[s][:, :, 128 * j:128 * j + 128],
                           winv[:, ds(L * 8, 8), TILES[2 * c + j]:TILES[2 * c + j] + 128]) for j in range(2)])
                wout_chunks(L, 0)
                for j in range(3):
                    if j == 0:
                        sp.wait_ge(win_used, L * 32 + 36)
                    hs = [0, 2, 3][j]
                    sp.dma_start(s0[:, j, :, :],
                                 a["state_hgrn"][ds(L, 1), :, hs:hs + 2, :, :].rearrange("l b h d e -> (l h d) b e")
                                 ).then_inc(s0_in, 16)
                sp.wait_ge(tt_used, L * 16 + 16)
                for g, (op, os, w) in enumerate((("moba_k_prompt", "moba_k_sample", AW), ("moba_v_prompt", "moba_v_sample", AW),
                                                 ("fox_k_prompt", "fox_k_sample", BW), ("fox_v_prompt", "fox_v_sample", BW))):
                    for c0, n, t0 in ((0, 384, 0),) if w == AW else ((0, 256, 0), (256, 64, 320)):
                        pv = outs[op].rearrange("l b (n p) h d -> p (l b n) (h d)", p=128)
                        sv = outs[os].rearrange("l b t h d -> l (b t) (h d)")
                        sp.dma_start(pv[:, ds(L * 2, 2), c0:c0 + n], tok[:, 0:2, g * 384 + t0:g * 384 + t0 + n]).then_inc(out_tok, 16)
                        sp.dma_start(sv[ds(L, 1), :, c0:c0 + n].rearrange("l t c -> (l t) c"),
                                     tok[0:NS, 2, g * 384 + t0:g * 384 + t0 + n]).then_inc(out_tok, 16)
                sp.dma_start(outs["fox_logf_prompt"].rearrange("l b (n p) h -> p (l b n) h", p=128)[:, ds(L * 2, 2), :],
                             tokf[:, 0:2, :]).then_inc(out_tok, 16)
                sp.dma_start(outs["fox_logf_sample"].rearrange("l b t h -> l (b t) h")[ds(L, 1), :, :].rearrange("l t h -> (l t) h"),
                             tokf[0:NS, 2, :]).then_inc(out_tok, 16)
                sp.wait_ge(h_stU, L + 1)
                sp.wait_ge(h_snU, L * 3 + 3)
                for j, (hs, p0) in enumerate(((0, 0), (2, 0), (4, 64))):
                    nh = 2 - p0 // 64
                    sp.dma_start(outs["hgrn_state_prompt"][ds(L, 1), 0, hs:hs + nh, :, :].rearrange("l h d e -> (l h d) e"),
                                 sp_[p0:128, j, :]).then_inc(out_st, 16)
                    sp.dma_start(outs["hgrn_state_sample"][ds(L, 1), :, hs:hs + nh, :, :].rearrange("l b h d e -> (l h d) b e"),
                                 s0[p0:128, j, :, :]).then_inc(out_st, 16)
                sp.wait_ge(out_st, L * 96 + 96)
                kmv = a["cache_moba_k"].rearrange("l n p h d -> p (l n) (h d)")
                kfv = a["cache_fox_k"].rearrange("l n p h d -> p (l n) (h d)")
                sp.wait_ge(d_init, L + 1)
                settle(sp)
                with sp.Fori(0, DB) as q:
                    for pg in range(NPG):
                        s = pg % 4
                        sp.wait_ge(kT_ready, (L * DB + q) * NPG + pg + 1)
                        page = sp.value_load(pages[0:1, ds(q * NPG + pg, 1)], min_val=0, max_val=NPOOL - 1)
                        sp.dma_start(kpg[:, s, 0:AW], kmv[:, ds(page + L * NPOOL, 1), :].rearrange("p a c -> p (a c)")).then_inc(k_in[s], 16)
                        sp.dma_start(kpg[:, s, AW:AW + BW], kfv[:, ds(page + L * NPOOL, 1), :].rearrange("p a c -> p (a c)")).then_inc(k_in[s], 16)
                with sp.Fori(1, 4) as m:
                    wout_chunks(L, m)
                with sp.Fori(0, GU) as i:
                    gu_chunk(1, L, i)
                down_chunks(1, L)
                nl = L * -1 + 1
                for s, w in ((0, wg[0]), (1, wu[0])):
                    fill(s, L * USES + USES, [(raw[s][:, :, :], gu_v(w)[:, ds(nl * 8, 8), 0:256])])
            for n in range(3):
                sp.wait_ge(f_U, 2 * (n + 1))
                rows = 128 if n < 2 else NS
                dst = outs["y_prompt"].rearrange("b (n p) d -> (b n) p d", p=128)[n] if n < 2 else \
                    outs["y_sample"].rearrange("b t d -> (b t) d")
                sp.dma_start(dst, P[0:rows, n * 1024:(n + 1) * 1024]).then_inc(f_out, 16)
            sp.wait_ge(f_out, 48)
            sp.wait_ge(out_tok, 14 * 16 * DEPTH)
            sp.wait_ge(out_st, 6 * 16 * DEPTH)
            for s in range(2):
                sp.wait_ge(raw_in[s], 32 * (DEPTH * USES + 1))

        @block.gpsimd
        def _(pool):
            grow = vpg[:, 0, 0:128]
            n = 0
            with nc.allow_non_contiguous_dma(reason="small parameters"):
                for l in range(DEPTH):
                    for w, name in enumerate(("norm_ffn1_g", "norm_mix_g", "norm_ffn2_g")):
                        r = l * 24 + w * 8
                        pool.dma_start(grow[r:r + 8, :], a[name][l].rearrange("(k p) -> k p", p=128)).then_inc(s_small, 16)
                        n += 1
                    for j in range(3):
                        pool.dma_start(lbt[:, l, j:j + 1], a["hgrn_lb_logits"][l, _THIRD[j]:_THIRD[j] + 128].rearrange("(p o) -> p o", o=1)).then_inc(s_small, 16)
                        n += 1
                    for hf in range(2):
                        pool.dma_start(gh[64 * hf:64 * hf + 64, l:l + 1], a["hgrn_norm_g"][l].rearrange("(p o) -> p o", o=1)).then_inc(s_small, 16)
                        n += 1
                    pool.dma_start(fb[:, l:l + 1], a["fox_f_bias"][l].rearrange("(p o) -> p o", o=1)).then_inc(s_small, 16)
                    n += 1
                pool.dma_start(grow[DEPTH * 24:DEPTH * 24 + 8, :], a["norm_final_g"].rearrange("(k p) -> k p", p=128)).then_inc(s_small, 16)
                pool.dma_start(vpg[0:DB * NPG, 1, 0:1].bitcast(I32), a["page_table"].rearrange("b (n o) -> (b n) o", o=1)).then_inc(s_small, 16)
                n += 2
            assert n == SMALL
            lfv = a["cache_fox_logf"].rearrange("l n p h -> (l n) (p h)")
            pool.wait_ge(s_idx, DEPTH)
            for l in range(DEPTH):
                pool.indirect_dma_start(
                    vpg[0:DB * NPG, 2 + l, 0:PAGE * BH], None, lfv,
                    bass.IndirectOffsetOnAxis(ap=vpg[0:DB * NPG, 1, 2 + l:3 + l].bitcast(U32), axis=0)).then_inc(s_lf, 16)
            pool.wait_ge(s_pages, 16)
            vmv = a["cache_moba_v"].rearrange("l n p h d -> p (l n) (h d)")
            vfv = a["cache_fox_v"].rearrange("l n p h d -> p (l n) (h d)")
            with pool.Fori(0, DEPTH) as L:
                pool.wait_ge(win_used, L * 32 + 36)
                settle(pool)
                with pool.Fori(0, DB) as q:
                    for pg in range(NPG):
                        pool.wait_ge(v_used, (L * DB + q) * NPG + pg + 1)
                        page = pool.value_load(pages[0:1, ds(q * NPG + pg, 1)], min_val=0, max_val=NPOOL - 1)
                        pool.dma_start(vpg[:, pg, 0:AW], vmv[:, ds(page + L * NPOOL, 1), :].rearrange("p a c -> p (a c)")).then_inc(v_in[pg], 16)
                        pool.dma_start(vpg[:, pg, AW:AW + BW], vfv[:, ds(page + L * NPOOL, 1), :].rearrange("p a c -> p (a c)")).then_inc(v_in[pg], 16)

        @block.scalar
        def _(act):
            ch = Chain(act, s_act)

            def hi(s, use):
                act.wait_ge(raw_in[s], (use + 1) * 32)
                act.wait_ge(w_free[s], use + 1)
                act.activation(whi[s][:, :, :], raw[s][:, :, :], ACT.Copy).then_inc(hi_done[s], 1)

            def norm(w):
                act.wait_ge(ms_eps, w + 1)
                ch.link(act.activation(rstd[:, :], rstd[:, :], ACT.Ln))
                act.activation(rstd[:, :], rstd[:, :], ACT.Exp, scale=-0.5).then_inc(rstd_ready, 1)

            def scaled(w):
                for k in range(KT_D):
                    act.wait_ge(xs_ready, w * KT_D + k + 1)
                    act.activation(xh[:, k, :], tmp[k % 4][:, :], ACT.Copy).then_inc(xh_ready, 1)

            def ffn(f, L):
                u0 = L * USES + OFF[f"ffn{f + 1}"]
                with act.Fori(0, GU) as i:
                    hi(1, u0 + i)
                    for j in range(2):
                        n = L * 2 * FT + f * FT + i * 2 + j
                        tile_done(act, j, gate_ready, L * 2 * GU + f * GU + i, 0, u0 + i)
                        act.wait_ge(up_used, n + 1)
                        act.activation(tmp[j][:, :], PS[:, j, 0:NT], ACT.Silu).then_inc(silu_done, 1)
                    hi(0, u0 + i + 1)
                u0 = L * USES + OFF[f"down{f + 1}"]
                with act.Fori(0, 2) as m:
                    for n in range(6):
                        hi((n + 1) % 2, u0 + m * 3 + (n + 1) // 2)

            act.wait_ge(s_c, 16)
            act.activation(tmp[0][:, 0:1], K[:, 0:1], ACT.Silu).then_inc(silu_done, 1)
            act.activation(tmp[0][:, 1:2], K[:, 0:1], ACT.Silu).then_inc(silu_done, 1)
            act.wait_ge(lb_diff, 1)
            act.activation(lbt[:, 1, 0:3], lbt[:, 1, 0:3], ACT.Sigmoid).then_inc(lb_sig, 1)
            hi(0, 0)
            with act.Fori(0, DEPTH) as L:
                ch.base, ch.n = L * ACT_STEPS, 0
                norm(L * 3)
                scaled(L * 3)
                ffn(0, L)
                norm(L * 3 + 1)
                scaled(L * 3 + 1)
                with act.Fori(0, WIN) as i:
                    hi(1, L * USES + OFF["win"] + i)
                    hi(0, L * USES + OFF["win"] + i + 1)
                act.wait_ge(win_used, L * 32 + 36)
                act.activation(p3(T["qf"]), p3(T["qf"]), ACT.Copy, scale=SCALE).then_inc(qf_scaled, 1)
                act.wait_ge(z_ready, L * 2 + 1)
                act.activation(tmp[2][0:BH, :], tmp[1][0:BH, :], ACT.Exp, scale=-1.0).then_inc(z_exp, 1)
                act.wait_ge(z_ready, L * 2 + 2)
                act.activation(tmp[1][0:BH, :], tmp[2][0:BH, :], ACT.Ln).then_inc(z_exp, 1)
                for h in range(NH + 1):
                    if h < NH:
                        for t in range(2):
                            act.wait_ge(smax, L * 2 * NH + 2 * h + t + 1)
                            c0, c1 = ((0, 128), (128, 384))[t]
                            act.activation(spr[h % 3][:, c0:c1], spr[h % 3][:, c0:c1], ACT.Exp,
                                           bias=spx[:, 4 * (h % 3) + t:4 * (h % 3) + t + 1],
                                           accum_out=spx[:, 16 + 4 * (h % 3) + t:17 + 4 * (h % 3) + t]).then_inc(pexp, 1)
                    if h >= 1:
                        n = h - 1
                        act.wait_ge(pT_ready, L * NH + n + 1)
                        if n >= 2:
                            act.wait_ge(o_ready, L * NH + n - 1)
                        act.activation(ppt[n % 2], PS[:, 2 + n % 2, 0:384], ACT.Copy).then_inc(pT_used, 1)
                act.wait_ge(o_ready, L * NH + NH)
                act.activation(b[1][:, :].rearrange("p (j t) -> p j t", j=3), p3(T["qc"]), ACT.Sigmoid).then_inc(h_sig, 1)
                act.activation(b[2][:, :].rearrange("p (j t) -> p j t", j=3), p3(T["gc"]), ACT.Sigmoid).then_inc(h_sig, 1)
                ch.link(act.activation(b[3][:, :].rearrange("p (j t) -> p j t", j=3), p3(T["fc"]), ACT.Sigmoid))
                act.activation(p3(T["fc"]), p3(T["fc"]), ACT.Sigmoid, scale=-1.0).then_inc(h_sig, 1)
                for j in range(3):
                    act.activation(b[0][:, j * NT:(j + 1) * NT], b[3][:, j * NT:(j + 1) * NT], ACT.Ln,
                                   bias=lbcur[:, j:j + 1], scale=lbcur[:, 3 + j:4 + j]).then_inc(h_logf, 1)
                for l in range(LEVELS + 1):
                    act.wait_ge(h_abs, L * 9 + l + 1)
                    v = b[3][:, :] if l < 6 else b[3][:, :].rearrange("p (j t) -> p j t", j=3)[:, :, 0:SEQ]
                    act.activation(v, v, ACT.Exp, scale=-1.0).then_inc(h_e, 1)
                cum3 = b[2][:, :].rearrange("p (j t) -> p j t", j=3)
                act.activation(qe[:, :, :], cum3[:, :, SEQ:NT], ACT.Exp).then_inc(h_e, 1)
                act.activation(el[:, :, :], cum3[:, :, SEQ + DS - 1:NT:DS], ACT.Exp).then_inc(h_e, 1)
                act.wait_ge(h_abs, L * 9 + 9)
                act.activation(b[3][:, :], b[3][:, :], ACT.Exp, scale=-1.0).then_inc(h_e, 1)
                act.wait_ge(h_p, L * 9 + 9)
                act.activation(ac[:, 0:2, :], PS[:, 0, 0:256].rearrange("p (h t) -> p h t", h=2), ACT.Copy).then_inc(h_ac, 1)
                act.activation(ac[:, 2:5, :], PS[:, 1, 0:384].rearrange("p (h t) -> p h t", h=3), ACT.Copy).then_inc(h_ac, 1)
                act.wait_ge(h_o, L + 1)
                act.wait_ge(h_kd, L + 1)
                act.activation(b[4][:, :].rearrange("p (j t) -> p j t", j=3), PS[:, 0:3, 0:NT], ACT.Square).then_inc(h_sq, 1)
                act.wait_ge(h_mse, L + 1)
                ch.link(act.activation(b[3][:, :], b[3][:, :], ACT.Ln))
                act.activation(b[3][:, :], b[3][:, :], ACT.Exp, scale=-0.5).then_inc(h_rs, 1)
                act.wait_ge(d_init, L + 1)

                def keys(Q, pg):
                    act.wait_ge(kT_ready, Q * NPG + pg + 5)
                    act.wait_ge(kT_used, Q * 4 + pg // 2 + 1)
                    act.activation(ktb[pg // 2 % 2][:, 0:3, 128 * (pg % 2):128 * (pg % 2) + 128],
                                   PS[:, 2 * (pg % 2), 0:384].rearrange("p (j c) -> p j c", j=3), ACT.Copy).then_inc(kT_act, 1)

                def weights(Q):
                    act.wait_ge(d_bias, Q + 1)
                    for n in range(NBLK + 1):
                        src = PS[0:ROWS, 4 + n // 2, 256 * (n % 2):256 * (n % 2) + 256] if n < NBLK else smn[:, :]
                        act.activation(pe_[:, 256 * n:256 * n + (256 if n < NBLK else NS)], src, ACT.Exp,
                                       bias=nb[:, n:n + 1], accum_out=es[:, n:n + 1]).then_inc(d_exp, 1)

                def turned(Q):
                    act.wait_ge(dpT_ready, Q * 2 + 2)
                    act.wait_ge(do_ready, Q + 1)
                    act.activation(ptt[:, 5:9, :], PS[:, 1, 0:352].rearrange("p (g c) -> p g c", g=4), ACT.Copy).then_inc(dpT_act, 1)

                def step(Q, softmax):
                    keys(Q, 0)
                    keys(Q, 1)
                    if softmax:
                        weights(Q - 1)
                    for pg in range(2, NPG):
                        keys(Q, pg)
                    if softmax:
                        turned(Q - 1)

                step(L * DB, False)
                with act.Fori(1, DB) as q:
                    step(L * DB + q, True)
                weights(L * DB + DB - 1)
                turned(L * DB + DB - 1)
                act.wait_ge(do_used, L * 11 * DB + 11 * DB + 4)
                act.wait_ge(h_out, L + 1)
                act.wait_ge(o_used, L * 6 + 6)
                for k in range(9):
                    r = slice(64, 128) if k in (5, 8) else slice(0, 128)
                    act.activation(xh[r, k, :], pt(OUT_T[k])[r, :], ACT.Copy).then_inc(oh_ready, 1)
                with act.Fori(0, 2) as m:
                    for dp in range(2):
                        hi(1, L * USES + OFF["wout"] + m * 2 + dp)
                        hi(0, L * USES + OFF["wout"] + m * 2 + dp + 1)
                norm(L * 3 + 2)
                scaled(L * 3 + 2)
                ffn(1, L)
                assert ch.n == ACT_STEPS, ch.n
            ch.base, ch.n = DEPTH * ACT_STEPS, 0
            norm(DEPTH * 3)

        @block.vector
        def _(dve):
            ch = Chain(dve, s_dve)
            link = ch.link
            V = lambda i: b[i][:, :].rearrange("p (j t) -> p j t", j=3)

            def give(s, n=1):
                dve.sem_inc(s, n)

            def lo(s, use):
                dve.wait_ge(hi_done[s], use + 1)
                dve.tensor_tensor(wlo[s][:, :, :], raw[s][:, :, :], whi[s][:, :, :].bitcast(F32), ALU.subtract).then_inc(split_done[s], 1)

            def norm(w):
                dve.wait_ge(ms_ready, w + 1)
                dve.tensor_scalar(rstd[:, :], PS[:, 7, 0:NT], 1.0 / D, EPS, ALU.mult, ALU.add).then_inc(ms_eps, 1)

            def low(w, k):
                dve.wait_ge(xh_ready, w * KT_D + k + 1)
                dve.tensor_tensor(xl[:, k, :], tmp[k % 4][:, :], xh[:, k, :].bitcast(F32), ALU.subtract).then_inc(xl_ready, 1)

            def scaled(w, which):
                dve.wait_ge(rstd_ready, w + 1)
                for k in range(KT_D):
                    if k >= 3:
                        low(w, k - 3)
                    if k >= 4:
                        dve.wait_ge(xl_ready, w * KT_D + k - 3)
                    dve.scalar_tensor_tensor(tmp[k % 4][:, :], xt(k), gcur[:, which * 8 + k:which * 8 + k + 1],
                                             rstd[:, :], ALU.mult, ALU.mult).then_inc(xs_ready, 1)
                for k in range(KT_D - 3, KT_D):
                    low(w, k)

            def accumulate(n0, half, at, bank, scale, s, use):
                for j in range(2):
                    tile_done(dve, j, acc_ready, half, s, use)
                    xs = X[:, ds(at + j * NT, NT)]
                    dve.scalar_tensor_tensor(xs, PS[:, bank + j, 0:NT], scale, xs, ALU.mult, ALU.add).then_inc(acc_used, 1)
                    dve.wait_ge(acc_used, n0 + j + 5)
                    link(dve.tensor_tensor(tmp[2][:, :], xs, xs, ALU.mult))
                    link(dve.tensor_tensor(sqsum[:, :], sqsum[:, :], tmp[2][:, :], ALU.add))

            def ffn(f, L):
                u0 = L * USES + OFF[f"ffn{f + 1}"]
                if f == 1:
                    dve.wait_ge(out_tok, L * 14 * 16 + 14 * 16)
                settle(dve)
                with dve.Fori(0, GU) as i:
                    ch.enter(i, 2)
                    lo(1, u0 + i)
                    lo(0, u0 + i + 1)
                    for j in range(2):
                        n = L * 2 * FT + f * FT + i * 2 + j
                        tile_done(dve, j, up_ready, L * 2 * GU + f * GU + i, 1, u0 + i)
                        dve.wait_ge(silu_done, n + 3)
                        dve.tensor_tensor(tmp[2 + j][:, :], tmp[j][:, :], PS[:, 2 + j, 0:NT], ALU.mult).then_inc(up_used, 1)
                        dve.wait_ge(up_used, n + 3)
                        hs, ls = hh[:, ds(i * 2 + j, 1), :], hl[:, ds(i * 2 + j, 1), :]
                        t = tmp[2 + j][:, :].rearrange("p (o t) -> p o t", o=1)
                        link(dve.tensor_scalar(hs, t, 1.0, None, ALU.mult))
                        dve.tensor_tensor(ls, t, hs.bitcast(F32), ALU.subtract).then_inc(h_done, 1)
                    ch.leave(GU, 2)
                link(dve.memset(sqsum[:, :], 0.0))
                settle(dve)
                u0 = L * USES + OFF[f"down{f + 1}"]
                with dve.Fori(0, 2) as m:
                    ch.enter(m, 8)
                    for n in range(6):
                        lo((n + 1) % 2, u0 + m * 3 + (n + 1) // 2)
                        if n % 3 == 2:
                            dp = n // 3
                            accumulate(L * 24 + f * 16 + m * 4 + 2 * dp, L * 12 + f * 8 + m * 2 + dp,
                                       m * (4 * NT) + dp * 2 * NT, 4 + 2 * dp, 0.5, n % 2, u0 + m * 3 + n // 2)
                    ch.leave(2, 8)
                give(sqsum_ready)

            for s, n in ((w_free[0], 1), (w_free[1], 1), (up_used, 2), (acc_used, 4), (do_used, 4), (do_ready, 1),
                         (win_used, 4), (kT_used, 2), (kT_act, 2), (kT_dve, 2),
                         (kT_ready, 4), (v_used, NPG), (obT_ready, 1)):
                give(s, n)
            link(dve.memset(X[:, KT_D * NT:], 0.0))
            link(dve.memset(P[:, 32 * NT:], 0.0))
            link(dve.memset(ncn[:, :], 0.0))
            dve.wait_ge(s_small, 16 * SMALL)
            for l in range(DEPTH):
                dve.tensor_scalar(vpg[0:DB * NPG, 1, 2 + l:3 + l].bitcast(I32), vpg[0:DB * NPG, 1, 0:1].bitcast(I32),
                                  float(l * NPOOL), None, ALU.add).then_inc(s_idx, 1)
            dve.tensor_tensor(lbt[:, 1, 0:3], lbt[:, 1, 0:3], lbt[:, 0, 0:3], ALU.subtract).then_inc(lb_diff, 1)
            dve.wait_ge(lb_sig, 1)
            link(dve.memset(lbt[:, 0, 0:3], 0.0))
            link(dve.tensor_scalar(lbt[:, :, 3:6], lbt[:, :, 0:3], -1.0, 1.0, ALU.mult, ALU.add))
            for n in range(6):
                tt, hf = divmod(n, 2)
                r = 128 if tt < 2 else NS
                dve.wait_ge(xT_ready, n + 1)
                link(dve.tensor_copy(
                    X[:, 4 * hf * NT:(4 * hf + 4) * NT].rearrange("p (k t) -> p k t", k=4)[:, :, tt * 128:tt * 128 + r],
                    PS[:, n, :].rearrange("p (k t) -> p k t", k=4)[:, :, 0:r]))
            give(split_done[0]); give(split_done[1])
            dve.wait_ge(gT_ready, 1)
            link(dve.tensor_copy(gains[:, :], PS[:, 6, 0:DEPTH * 24 + 8]))
            link(dve.memset(sqsum[:, :], 0.0))
            for k in range(KT_D):
                link(dve.tensor_tensor(tmp[2][:, :], xt(k), xt(k), ALU.mult))
                link(dve.tensor_tensor(sqsum[:, :], sqsum[:, :], tmp[2][:, :], ALU.add))
            give(sqsum_ready)
            G = DB * NPG
            lft, later = tok[:, 0, 0:640], tok[:, 1, 0:640]
            l4 = lambda x: x.rearrange("p (l h b g) -> p (l h b) g", l=DEPTH, h=BH, b=DB)
            for l in range(DEPTH):
                dve.wait_ge(lfT_ready, l + 1)
                link(dve.tensor_copy(lft[:, l * 320:(l + 1) * 320], PS[:, l, 0:320]))
            link(dve.memset(later[:, :], 0.0))
            for pg in range(NPG - 2, -1, -1):
                link(dve.tensor_tensor(l4(later)[:, :, pg:pg + 1], l4(later)[:, :, pg + 1:pg + 2], l4(lft)[:, :, pg + 1:pg + 2], ALU.add))
            give(later_ready)
            for l in range(DEPTH):
                dve.wait_ge(pb_ready, l + 1)
                link(dve.tensor_copy(tok[:, 2, l * 320:(l + 1) * 320], PS[:, 2 + l, 0:320]))
            give(pbT_used)
            dve.wait_ge(pbT_ready, 1)
            link(dve.tensor_copy(brow[:, :].rearrange("p (a c) -> p a c", a=2), PS[0:DEPTH * BH * DB, 0:2, :]))
            lo(0, 0)
            start_steps = ch.n
            with dve.Fori(0, DEPTH) as L:
                ch.base, ch.n = L * DVE_STEPS + start_steps, 0
                link(dve.tensor_scalar(gcur[:, :], gains[:, ds(L * 24, 24)], 1.0, None, ALU.mult))
                link(dve.tensor_scalar(lbcur[:, :].rearrange("p (o c) -> p o c", o=1), lbt[:, ds(L, 1), :], 1.0, None, ALU.mult))
                link(dve.tensor_scalar(ghcur[:, :], gh[:, ds(L, 1)], 1.0, None, ALU.mult))
                link(dve.tensor_scalar(fbcur[:, :], fb[:, ds(L, 1)], 1.0, None, ALU.mult))
                norm(L * 3)
                scaled(L * 3, 0)
                ffn(0, L)
                norm(L * 3 + 1)
                scaled(L * 3 + 1, 1)
                with dve.Fori(0, WIN) as i:
                    u = L * USES + OFF["win"] + i
                    for c in range(2):
                        lo(1 - c, u + c)
                        for j in range(2):
                            n = 2 * c + j
                            tile_done(dve, j, win_ready, L * 16 + 2 * i + c, c, u)
                            dve.tensor_scalar(P[:, ds(i * (4 * NT) + n * NT, NT)], PS[:, n, 0:NT], 1.0, None, ALU.mult).then_inc(win_used, 1)
                dve.wait_ge(win_used, L * 32 + 36)
                for n in range(6):
                    sc = SCALE if n < 3 else 1.0
                    dve.wait_ge(rot_ready, L * 6 + n + 1)
                    t1, t2 = tmp[2 * (n % 2)], tmp[2 * (n % 2) + 1]
                    link(dve.scalar_tensor_tensor(t1[:, :], pt(n), sc, cst("cos"), ALU.mult, ALU.mult))
                    link(dve.scalar_tensor_tensor(t2[:, :], PS[:, 4 + n % 2, 0:NT], sc, cst("sin"), ALU.mult, ALU.mult))
                    dve.tensor_tensor(pt(n), t1[:, :], t2[:, :], ALU.add).then_inc(roped, 1)
                z, e1, e2 = (tmp[j][0:BH, :] for j in range(3))
                link(dve.tensor_scalar(z, pt(T["ff"])[0:BH, :], fbcur[:, 0:1], None, ALU.add))
                dve.scalar_tensor_tensor(e1, z, -1.0, z, ALU.mult, ALU.max).then_inc(z_ready, 1)
                dve.wait_ge(z_exp, L * 2 + 1)
                dve.tensor_scalar(e2, e2, 1.0, None, ALU.add).then_inc(z_ready, 1)
                dve.wait_ge(z_exp, L * 2 + 2)
                link(dve.scalar_tensor_tensor(pt(T["ff"])[0:BH, :], z, 0.0, e1, ALU.min, ALU.subtract))
                dve.tensor_tensor_scan(ncn[:, 0:NT], cst("reset")[0:BH, :], pt(T["ff"])[0:BH, :], 0.0, ALU.mult, ALU.subtract).then_inc(lf_ready, 1)
                for n in range(15):
                    g, tt = divmod(n, 3)
                    r = 128 if tt < 2 else NS
                    dve.wait_ge(tt_ready, L * 16 + n + 1)
                    dve.tensor_copy(tok[0:r, tt, g * 384:(g + 1) * 384], PS[0:r, 4 + n % 4, 0:384]).then_inc(tt_used, 1)
                dve.wait_ge(tt_ready, L * 16 + 16)
                link(dve.tensor_copy(tokf[:, :, :], PS[:, 0, 0:24].rearrange("p (t c) -> p t c", t=3)[:, :, 0:BH]))
                dve.tensor_copy(tokn[:, :], PS[0:NS, 0, 24:24 + BH]).then_inc(tt_used, 1)
                for h in range(NH + 3):
                    if h < NH:
                        c = spr[h % 3]
                        dve.wait_ge(s_ready, L * NH + h + 1)
                        if h >= 3:
                            dve.wait_ge(pT_ready, L * NH + h - 2)
                        dve.tensor_tensor(c, PS[:, h % 2, 0:384], cst("causal"), ALU.add).then_inc(s_used, 1)
                        dve.wait_ge(s_used, L * NH + h + 1)
                        x = spx[:, 4 * (h % 3):4 * (h % 3) + 2]
                        dve.tensor_reduce(x[:, 0:1], c[:, 0:128], AX.X, ALU.max, negate=True).then_inc(smax, 1)
                        dve.tensor_reduce(x[:, 1:2], c[:, 128:384], AX.X, ALU.max, negate=True).then_inc(smax, 1)
                    if 1 <= h <= NH:
                        n = h - 1
                        c = spr[n % 3]
                        x = spx[:, 16 + 4 * (n % 3):16 + 4 * (n % 3) + 2]
                        dve.wait_ge(pexp, L * 2 * NH + 2 * n + 2)
                        link(dve.reciprocal(x, x))
                        dve.tensor_scalar(c[:, 0:128], c[:, 0:128], x[:, 0:1], None, ALU.mult).then_inc(p_ready, 1)
                        dve.tensor_scalar(c[:, 128:384], c[:, 128:384], x[:, 1:2], None, ALU.mult).then_inc(p_ready, 1)
                    if h >= 3 and (h - 3) in (1, 3, 5, 7, 9, 10):
                        pr = (1, 3, 5, 7, 9, 10).index(h - 3)
                        r = slice(0, 128) if pr < 5 else slice(64, 128)
                        dve.wait_ge(o_ready, L * NH + h - 2)
                        dve.tensor_copy(pt(OUT_T[pr])[r, 0:SEQ], PS[r, 4 + pr % 2, 0:SEQ]).then_inc(o_used, 1)
                q3, g3, k3 = p3(T["qc"]), p3(T["gc"]), p3(T["fc"])
                dve.wait_ge(h_sig, L * 3 + 3)
                link(dve.tensor_tensor(q3, q3, V(1), ALU.mult))
                link(dve.tensor_tensor(g3, g3, V(2), ALU.mult))
                for j in range(3):
                    link(dve.tensor_scalar(pt(T["fc"] + j), pt(T["fc"] + j), lbcur[:, 3 + j:4 + j], None, ALU.mult))
                give(h_qk)
                link(dve.memset(am[:, :, :], 0.0))
                link(dve.memset(asm[:, :, :], 0.0))
                dve.wait_ge(h_logf, L * 3 + 3)
                for j in range(3):
                    link(dve.tensor_tensor_scan(V(2)[:, j, :], cst("reset"), V(0)[:, j, :], 0.0, ALU.mult, ALU.add))
                lm = cst("lmask").rearrange("p (l t) -> p l t", l=LEVELS + 1).bitcast(I32)

                def take(n, mask):
                    dve.wait_ge(h_p, L * 9 + n + 1)
                    settle(dve)
                    bk = 4 * (n % 2)
                    for g in range(3):
                        nh = 2 if g < 2 else 1
                        ch.mark(dve.copy_predicated(
                            am[:, 2 * g:2 * g + nh, :].rearrange("p h (u t) -> p (h u) t", u=2),
                            lm[:, mask:mask + 1, :].to_broadcast([128, 2 * nh, 128]),
                            PS[:, bk + g, 0:256 * nh].rearrange("p (h t) -> p h t", t=128)))
                    if mask == LEVELS or mask < 3:
                        for a0, a1, g, c in ((0, 2, 3, 0), (2, 5, 2, 256)):
                            ch.mark(dve.copy_predicated(
                                asm[:, a0:a1, :], lm[0:NS, mask:mask + 1, 0:NS].to_broadcast([NS, a1 - a0, NS]),
                                PS[0:NS, bk + g, c:c + (a1 - a0) * NS].rearrange("p (h t) -> p h t", t=NS)))
                    ch.catch_up()
                    give(h_pused)

                for l in range(LEVELS + 1):
                    h = 1 << l
                    if l < 6:
                        seg = lambda x: x.rearrange("p (s c) -> p s c", c=2 * h)
                        dv, cv = seg(b[3][:, :]), seg(b[2][:, :])
                        qv, kv = (seg(P[:, T[w] * NT:(T[w] + 3) * NT]) for w in ("qc", "fc"))
                        gv = seg(b[4 if l % 2 == 0 else 0][:, :])
                        mid = cv[:, :, h - 1:h].to_broadcast([128, 3 * NT // (2 * h), 2 * h])
                        parts = [(dv, cv, qv, kv, gv, mid)]
                    else:
                        parts = []
                        for j in range(3):
                            ns = SEQ // (2 * h)
                            seg = lambda x: x.rearrange("p (s c) -> p s c", c=2 * h)
                            dv, cv = seg(V(3)[:, j, 0:SEQ]), seg(V(2)[:, j, 0:SEQ])
                            qv, kv = seg(pt(T["qc"] + j)[:, 0:SEQ]), seg(pt(T["fc"] + j)[:, 0:SEQ])
                            gv = seg(V(4 if l % 2 == 0 else 0)[:, j, 0:SEQ])
                            parts.append((dv, cv, qv, kv, gv, cv[:, :, h - 1:h].to_broadcast([128, ns, 2 * h])))
                    for dv, cv, qv, kv, gv, mid in parts:
                        link(dve.tensor_tensor(dv, cv, mid, ALU.subtract))
                    w = b[3][:, :] if l < 6 else V(3)[:, :, 0:SEQ]
                    dve.scalar_tensor_tensor(w, w, -1.0, w, ALU.mult, ALU.max).then_inc(h_abs, 1)
                    if l >= 1:
                        take(l, l - 1)
                    else:
                        take(0, LEVELS)
                    dve.wait_ge(h_e, L * 11 + l + 1)
                    for dv, cv, qv, kv, gv, mid in parts:
                        link(dve.tensor_tensor(gv[:, :, h:2 * h], dv[:, :, h:2 * h], qv[:, :, h:2 * h], ALU.mult))
                        link(dve.tensor_tensor(gv[:, :, 0:h], dv[:, :, 0:h], kv[:, :, 0:h], ALU.mult))
                    give(h_g)
                link(dve.tensor_tensor(V(3)[:, :, 0:SEQ], V(2)[:, :, 0:SEQ], V(2)[:, :, SEQ - 1:SEQ].to_broadcast([128, 3, SEQ]), ALU.subtract))
                for j in range(3):
                    v = lambda x: x[:, j, SEQ:NT].rearrange("p (b t) -> p b t", t=DS)
                    link(dve.tensor_tensor(v(V(3)), v(V(2)), v(V(2))[:, :, DS - 1:DS].to_broadcast([128, DB, DS]), ALU.subtract))
                give(h_abs)
                dve.wait_ge(h_e, L * 11 + 9)
                link(dve.tensor_tensor(qe[:, :, :], qe[:, :, :], q3[:, :, SEQ:NT], ALU.mult))
                dve.wait_ge(h_e, L * 11 + 11)
                link(dve.tensor_tensor(V(1), V(3), k3, ALU.mult))
                give(h_kd)
                for tt in range(3):
                    r = 128 if tt < 2 else NS
                    dve.wait_ge(h_kdT, L * 3 + tt + 1)
                    dve.tensor_copy(kdt[0:r, tt, :], PS[0:r, 4 + tt, 0:384]).then_inc(h_kdU, 1)
                vx = [b[0][0:NS, 0:512], P[0:NS, T["qc"] * NT:T["qc"] * NT + 512]]
                dve.wait_ge(h_o, L + 1)
                for e in range(CH):
                    if e >= 2:
                        dve.wait_ge(h_sn, L * CH + e - 1)
                    dve.tensor_tensor(vx[e % 2].rearrange("p (b e) -> p b e", b=DB),
                                      tok[0:NS, 2, 4 * 384 + HCOL[e]:4 * 384 + HCOL[e] + 64].rearrange("p (o e) -> p o e", o=1).to_broadcast([NS, DB, 64]),
                                      cst("seqof")[0:NS, :].rearrange("p (b o) -> p b o", o=1).to_broadcast([NS, DB, 64]),
                                      ALU.mult).then_inc(h_vx, 1)
                dve.wait_ge(h_st, L + 1)
                link(dve.tensor_copy(sp_[:, 0:2, :], PS[:, 7, 0:128].rearrange("p (j e) -> p j e", j=2)))
                dve.tensor_copy(sp_[64:128, 2, :], PS[64:128, 7, 128:192]).then_inc(h_stU, 1)
                dve.wait_ge(h_sn, L * CH + CH)
                for j in range(3):
                    r = slice(0, 128) if j < 2 else slice(64, 128)
                    n = 128 if j < 2 else 64
                    link(dve.tensor_tensor(s0[r, j, :, :], s0[r, j, :, :],
                                           el[r, j, :].rearrange("p (b o) -> p b o", o=1).to_broadcast([n, DB, 64]), ALU.mult))
                    dve.tensor_tensor(s0[r, j, :, :], s0[r, j, :, :], PS[r, 4 + j, :].rearrange("p (b e) -> p b e", b=DB), ALU.add).then_inc(h_snU, 1)
                dve.wait_ge(h_ms, L + 1)
                dve.tensor_scalar(V(3), PS[:, 4:7, 0:NT], 1.0 / HD, EPS, ALU.mult, ALU.add).then_inc(h_mse, 1)
                dve.wait_ge(h_rs, L + 1)
                for j in range(3):
                    link(dve.scalar_tensor_tensor(V(4)[:, j, :], PS[:, j, 0:NT], ghcur[:, 0:1], V(3)[:, j, :], ALU.mult, ALU.mult))
                dve.tensor_tensor(p3(T["ic"]), V(4), g3, ALU.mult).then_inc(h_out, 1)
                qzd = qz[:, :, :].rearrange("p j c -> p (j c)")[:, 0:5 * (ROWS + 16)].rearrange("p (j c) -> p j c", j=5)[:, :, 0:16]
                dve.wait_ge(out_st, L * 96 + 96)
                dve.wait_ge(h_out, L + 1)
                link(dve.memset(qb[:, :, :, :], 0.0))
                link(dve.memset(gm[:, :], 0.0))
                link(dve.memset(pe_[:, 1088:1152], 0.0))
                dve.wait_ge(qf_scaled, L + 1)
                for t0, p0, n, hf in ((T["qa"], 0, 3, 0), (T["qa"], 0, 3, 1), (T["qf"], 3, 2, 0), (T["qf"], 3, 3, 1)):
                    r = slice(64 * hf, 64 * hf + 64)
                    src = P[r, t0 * NT:(t0 + n) * NT].rearrange("p (j t) -> p j t", j=n)[:, :, SEQ:NT]
                    for j in range(n):
                        link(dve.tensor_copy(qb[r, p0 + j, :, 8 * hf:8 * hf + 8], src[:, j, :].rearrange("p (b t) -> p b t", t=DS)))
                link(dve.memset(qz[:, :, :], 0.0))
                give(q_ready)
                dve.wait_ge(out_tok, L * 14 * 16 + 14 * 16)
                nm = cst("newmask")[0:NS, :].rearrange("p (b t) -> p b t", b=DB)
                for h in range(NH):
                    if h < AH:
                        link(dve.tensor_copy(newb[:, :, 8 * h:8 * h + 8], nm))
                    else:
                        link(dve.tensor_scalar(newb[:, :, 8 * h:8 * h + 8], nm, tokn[:, h - AH:h - AH + 1], None, ALU.add))
                dve.wait_ge(sn_ready, L + 1)
                nbv = newb[:, :, 0:64].rearrange("p b (j c) -> p j b c", j=4)
                link(dve.tensor_tensor(nbv, nbv, PS[0:NS, 4, :].rearrange("p (j b c) -> p j b c", j=4, b=DB), ALU.add))
                for c0, lo_ in ((64, 0), (80, 8)):
                    nbv = newb[:, :, c0:c0 + 16 - lo_]
                    link(dve.tensor_tensor(nbv, nbv, PS[0:NS, 5, 8 * (c0 - 64):8 * (c0 - 64) + 128].rearrange("p (b c) -> p b c", b=DB)[:, :, lo_:16], ALU.add))
                give(sn_used)
                dve.wait_ge(snT_ready, L + 1)
                link(dve.tensor_copy(smna[:, :, :], PS[0:ROWS, 6, :].rearrange("p (b c) -> p b c", b=DB)))
                give(d_init)

                def queries(Q, q):
                    dve.wait_ge(kT_used, Q * 4 + 2)
                    ch.mark(dve.tensor_scalar(qzd, qb[:, 0:5, ds(q, 1), :].rearrange("p j o c -> p j (o c)"), 1.0, None, ALU.mult))
                    ch.mark(dve.tensor_scalar(qz[:, 5, 80:88].rearrange("p (o c) -> p o c", o=1), qb[:, 5, ds(q, 1), 8:16], 1.0, None, ALU.mult))
                    ch.mark(dve.tensor_tensor(sel[:, :], cst("hsel")[0:DEPTH * BH * DB, :],
                                              cst("rowsel")[0:DEPTH * BH * DB, ds(Q, 1)].to_broadcast([DEPTH * BH * DB, ROWS]), ALU.mult))
                    ch.catch_up()
                    give(qz_ready)

                def keys(Q, pg):
                    dve.wait_ge(kT_ready, Q * NPG + pg + 5)
                    dve.wait_ge(kT_used, Q * 4 + pg // 2 + 1)
                    dve.tensor_copy(ktb[pg // 2 % 2][:, 3:6, 128 * (pg % 2):128 * (pg % 2) + 128],
                                    PS[:, 2 * (pg % 2) + 1, 0:384].rearrange("p (j c) -> p j c", j=3)).then_inc(kT_dve, 1)

                def block_sums(Q, q):
                    dve.wait_ge(kT_used, Q * 4 + 6)
                    rows = PS[0:ROWS, 4:6, :].rearrange("p a (n c) -> p (a n) c", n=2)
                    ch.mark(dve.tensor_reduce(gs_[:, 0, :], rows[0:48], AX.X, ALU.add))
                    ch.mark(dve.tensor_reduce(bm[:, 0:NBLK], rows, AX.X, ALU.max))
                    link(dve.tensor_scalar(smn[:, :].rearrange("p (o c) -> p o c", o=1), smna[:, ds(q, 1), :], 1.0, None, ALU.mult))
                    link(dve.tensor_reduce(bm[:, NBLK:NBLK + 1], smn[:, :], AX.X, ALU.max))

                def gates(Q):
                    link(dve.tensor_reduce(gs_[:, 1, 0:1], gs_[:, 0, :], AX.X, ALU.min))
                    link(dve.scalar_tensor_tensor(gs_[:, 2, :], gs_[:, 0, :], gs_[:, 1, 0:1], cst("place")[0:48, :], ALU.is_equal, ALU.mult))
                    link(dve.tensor_reduce(gs_[:, 3, 0:1], gs_[:, 2, :], AX.X, ALU.max))
                    link(dve.tensor_scalar(gm[0:48, 0:NBLK], gs_[:, 2, :], gs_[:, 3, 0:1], NEG, ALU.is_equal, ALU.mult))
                    link(dve.tensor_tensor(bm[:, :], bm[:, :], gm[:, :], ALU.add))
                    link(dve.tensor_reduce(rs[:, 0:1], bm[:, :], AX.X, ALU.max, negate=True))
                    dve.tensor_scalar(nb[:, :], gm[:, :], rs[:, 0:1], None, ALU.add).then_inc(d_bias, 1)

                def norms(Q):
                    dve.wait_ge(d_exp, Q * 5 + 5)
                    link(dve.tensor_reduce(rs[:, 1:2], es[:, :], AX.X, ALU.add))
                    link(dve.reciprocal(rs[:, 1:2], rs[:, 1:2]))

                def turned(Q):
                    dve.wait_ge(dpT_ready, Q * 2 + 1)
                    dve.wait_ge(do_ready, Q + 1)
                    dve.tensor_copy(ptt[:, 0:5, :], PS[:, 0, 0:440].rearrange("p (g c) -> p g c", g=5)).then_inc(dpT_dve, 1)

                def scale_outputs(Q):
                    dve.wait_ge(do_ready, Q + 2)
                    dve.wait_ge(obT_ready, Q + 1)
                    ch.mark(dve.tensor_scalar(ob[:, 0:AW], PS[0:ROWS, 6, 0:AW], rs[:, 1:2], None, ALU.mult))
                    ch.mark(dve.tensor_scalar(ob[:, AW:AW + BW], PS[0:ROWS, 7, 0:BW], rs[:, 1:2], None, ALU.mult))
                    ch.catch_up()
                    give(ob_ready)

                def outputs(Q, q):
                    dve.wait_ge(obT_ready, Q + 2)
                    for r0, t0, p0, n in ((0, T["va"], 0, 3), (64, T["va"], 0, 3), (0, T["vf"], 3, 2), (64, T["vf"], 3, 2), (64, T["vf"] + 2, 5, 1)):
                        r = slice(r0, r0 + 64)
                        if p0 < 5:
                            src = [PS[r, 6, 104 * (p0 + k) + r0 // 8:104 * (p0 + k) + r0 // 8 + 8] for k in range(n)]
                        else:
                            src = [PS[r, 7, 80:88]]
                        for k in range(n):
                            dst = P[r, ds(q * DS + (t0 + k) * NT + SEQ, DS)]
                            dve.tensor_scalar(dst, src[k], 1.0, None, ALU.mult).then_inc(do_used, 1)

                def step(Q, q, softmax, products):
                    queries(Q, q)
                    if softmax:
                        block_sums(Q - 1, q - 1)
                        gates(Q - 1)
                    keys(Q, 0)
                    keys(Q, 1)
                    if products:
                        scale_outputs(Q - 2)
                    keys(Q, 2)
                    keys(Q, 3)
                    if products:
                        outputs(Q - 2, q - 2)
                    if softmax:
                        norms(Q - 1)
                    for pg in range(4, NPG):
                        keys(Q, pg)
                    if softmax:
                        turned(Q - 1)

                step(L * DB, 0, False, False)
                step(L * DB + 1, 1, True, False)
                settle(dve)
                with dve.Fori(2, DB) as q:
                    ch.enter(q - 2, DECODE_STEPS)
                    step(L * DB + q, q, True, True)
                    ch.leave(DB - 2, DECODE_STEPS)
                Q = L * DB + DB - 1
                block_sums(Q, DB - 1)
                gates(Q)
                scale_outputs(Q - 1)
                outputs(Q - 1, DB - 2)
                norms(Q)
                turned(Q)
                scale_outputs(Q)
                outputs(Q, DB - 1)
                for k in range(9):
                    r = slice(64, 128) if k in (5, 8) else slice(0, 128)
                    dve.wait_ge(oh_ready, L * 9 + k + 1)
                    dve.tensor_tensor(xl[r, k, :], pt(OUT_T[k])[r, :], xh[r, k, :].bitcast(F32), ALU.subtract).then_inc(ol_ready, 1)
                link(dve.memset(sqsum[:, :], 0.0))
                settle(dve)
                with dve.Fori(0, 2) as m:
                    ch.enter(m, 8)
                    for dp in range(2):
                        u = L * USES + OFF["wout"] + m * 2 + dp
                        lo(1, u)
                        lo(0, u + 1)
                        accumulate(L * 24 + 8 + m * 4 + 2 * dp, L * 12 + 4 + m * 2 + dp, m * (4 * NT) + dp * 2 * NT, 4 + 2 * dp, 1.0, 1, u)
                    ch.leave(2, 8)
                give(sqsum_ready)
                norm(L * 3 + 2)
                scaled(L * 3 + 2, 2)
                ffn(1, L)
                assert ch.n == DVE_STEPS, ch.n
            ch.base, ch.n = DEPTH * DVE_STEPS + start_steps, 0
            norm(DEPTH * 3)
            dve.wait_ge(rstd_ready, DEPTH * 3 + 1)
            for k in range(KT_D):
                ins = dve.scalar_tensor_tensor(xt(k), xt(k), gains[:, DEPTH * 24 + k:DEPTH * 24 + k + 1], rstd[:, :], ALU.mult, ALU.mult)
                ins.then_inc(xs_ready, 1)
            for n in range(6):
                tt, hf = divmod(n, 2)
                r = 128 if tt < 2 else NS
                dve.wait_ge(f_T, n + 1)
                dve.tensor_copy(P[0:r, tt * 1024 + hf * 512:tt * 1024 + hf * 512 + 512], PS[0:r, n, :]).then_inc(f_U, 1)

        @block.tensor
        def _(te):
            ident = cst("ident")

            def dense(out, wslot, cols, rhs, ktiles, start, stop):
                hs, ls = rhs
                last = None
                for n, (kt, at, r) in enumerate(ktiles):
                    for m, (w, x) in enumerate(((whi, hs), (wlo, hs), (whi, ls))):
                        last = te.matmul(out, w[wslot][r, kt, cols], x[r, at, :],
                                         start=start and n == 0 and m == 0, stop=stop and n == len(ktiles) - 1 and m == 2)
                return last

            ALLR = slice(0, 128)

            def norm(w):
                te.wait_ge(sqsum_ready, w + 1)
                te.matmul(PS[:, 7, 0:NT], cst("ones"), sqsum[:, :], start=True, stop=True).then_inc(ms_ready, 1)

            def chunk(s, use):
                te.wait_ge(split_done[s], use + 2)

            def ffn(f, L, w):
                te.wait_ge(xl_ready, w * KT_D + KT_D)
                settle(te)
                u0 = L * USES + OFF[f"ffn{f + 1}"]
                kts = [(k, k, ALLR) for k in range(KT_D)]
                with te.Fori(0, GU) as i:
                    n0 = L * 2 * FT + f * FT + i * 2
                    for s in range(2):
                        chunk(s, u0 + i)
                        for j in range(2):
                            te.wait_ge(silu_done if s == 0 else up_used, n0 + j + 1)
                            dense(PS[:, 2 * s + j, 0:NT], s, slice(128 * j, 128 * j + 128), (xh, xl), kts, True, True
                                  ).then_inc(w_free[s] if j else (gate_ready, up_ready)[s], 1)
                te.wait_ge(h_done, L * 2 * FT + f * FT + FT)
                settle(te)
                u0 = L * USES + OFF[f"down{f + 1}"]
                with te.Fori(0, 2) as m:
                    for n in range(6):
                        dp, kk = divmod(n, 3)
                        chunk(n % 2, u0 + m * 3 + n // 2)
                        kts = [(k, kk * 8 + k, ALLR) for k in range(8 if kk < 2 else FT - 16)]
                        for j in range(2):
                            a0 = L * 24 + f * 16 + m * 4 + 2 * dp + j
                            if kk == 0:
                                te.wait_ge(acc_used, a0 + 1)
                            last = dense(PS[:, 4 + 2 * dp + j, 0:NT], n % 2, slice(128 * j, 128 * j + 128), (hh, hl), kts, kk == 0, kk == 2)
                            if j == 1:
                                last.then_inc(w_free[n % 2], 1)
                            elif kk == 2:
                                last.then_inc(acc_ready, 1)

            te.wait_ge(s_c, 16)
            te.wait_ge(s_x, 48)
            xtok = [raw[0].rearrange("p a b -> p (a b)")[:, 0:1024], raw[0].rearrange("p a b -> p (a b)")[:, 1024:2048],
                    raw[1].rearrange("p a b -> p (a b)")[:, 0:1024]]
            for n in range(6):
                tt, hf = divmod(n, 2)
                r = 128 if tt < 2 else NS
                for k in range(4):
                    last = te.transpose(PS[:, n, 128 * k:128 * k + r], xtok[tt][0:r, (4 * hf + k) * 128:(4 * hf + k + 1) * 128], ident[0:r, 0:r])
                last.then_inc(xT_ready, 1)
            te.wait_ge(s_small, 16 * SMALL)
            n = DEPTH * 24 + 8
            te.transpose(PS[:, 6, 0:n], vpg[0:n, 0, 0:128], ident[0:n, 0:n]).then_inc(gT_ready, 1)
            te.wait_ge(s_lf, 32)
            te.wait_ge(sqsum_ready, 1)
            G = DB * NPG
            for l in range(DEPTH):
                for h in range(BH):
                    last = te.transpose(PS[:, l, h * G:(h + 1) * G], vpg[0:G, 2 + l, 0:PAGE * BH].rearrange("p (k h) -> p h k", h=BH)[:, h, :], ident[0:G, 0:G])
                last.then_inc(lfT_ready, 1)
            te.wait_ge(later_ready, 1)
            for l in range(DEPTH):
                te.matmul(PS[:, 2 + l, 0:320], cst("later"), tok[:, 0, l * 320:(l + 1) * 320], start=True, stop=False)
                te.matmul(PS[:, 2 + l, 0:320], cst("ones"), tok[:, 1, l * 320:(l + 1) * 320], start=False, stop=True).then_inc(pb_ready, 1)
            te.wait_ge(pbT_used, 1)
            n = DEPTH * BH * DB
            for g in range(NPG):
                last = te.transpose(PS[0:n, g // 4, 128 * (g % 4):128 * (g % 4) + 128],
                                    tok[:, 2, 0:640].rearrange("p (r g) -> p g r", g=NPG)[:, g, :], ident)
            last.then_inc(pbT_ready, 1)
            with te.Fori(0, DEPTH) as L:
                norm(L * 3)
                ffn(0, L, L * 3)
                norm(L * 3 + 1)
                te.wait_ge(xl_ready, (L * 3 + 1) * KT_D + KT_D)
                settle(te)
                with te.Fori(0, WIN) as i:
                    for s in range(2):
                        chunk(s, L * USES + OFF["win"] + i)
                        for j in range(2):
                            te.wait_ge(win_used, L * 32 + i * 4 + 2 * s + j + 1)
                            dense(PS[:, 2 * s + j, 0:NT], s, slice(128 * j, 128 * j + 128), (xh, xl),
                                  [(k, k, ALLR) for k in range(KT_D)], True, True).then_inc(w_free[s] if j else win_ready, 1)
                te.wait_ge(win_used, L * 32 + 36)
                for n in range(6):
                    if n >= 2:
                        te.wait_ge(roped, L * 6 + n - 1)
                    te.matmul(PS[:, 4 + n % 2, 0:NT], cst("perm"), pt(n), start=True, stop=True).then_inc(rot_ready, 1)
                te.wait_ge(roped, L * 6 + 6)
                for n in range(15):
                    g, tt = divmod(n, 3)
                    t0 = T[("ka", "va", "kf", "vf", "ic")[g]]
                    if n >= 4:
                        te.wait_ge(tt_used, L * 16 + n - 3)
                    for j in range(3):
                        at = (t0 + j) * NT + tt * 128
                        last = te.transpose(PS[:, 4 + n % 4, 128 * j:128 * j + 128], P[:, at:at + 128], ident)
                    last.then_inc(tt_ready, 1)
                te.wait_ge(lf_ready, L + 1)
                settle(te)
                for tt in range(3):
                    at = T["ff"] * NT + tt * 128
                    te.transpose(PS[:, 0, 8 * tt:8 * tt + BH], P[0:BH, at:at + 128], ident[0:BH, 0:BH])
                te.transpose(PS[:, 0, 24:24 + BH], ncn[:, SEQ:SEQ + 128], ident[0:BH, 0:BH]).then_inc(tt_ready, 1)
                te.wait_ge(tt_used, L * 16 + 16)
                te.wait_ge(qf_scaled, L + 1)
                for h in range(NH + 2):
                    if h < NH:
                        moba = h < AH
                        j, hf = (h // 2, h % 2) if moba else HEADS5[h - AH]
                        r = slice(64 * hf, 64 * hf + 64)
                        qt, kt = pt((T["qa"] if moba else T["qf"]) + j), pt((T["ka"] if moba else T["kf"]) + j)
                        if h >= 2:
                            te.wait_ge(s_used, L * NH + h - 1)
                        for t in range(2):
                            out = PS[:, h % 2, 128 * t:128 * t + 128 * (t + 1)]
                            last = te.matmul(out, qt[r, 128 * t:128 * t + 128], kt[r, 0:128 * (t + 1)], start=True, stop=moba)
                            if not moba:
                                e = h - AH
                                last = te.matmul(out, ident[0:BH, e:e + 1].to_broadcast([BH, 128]), ncn[:, 0:128 * (t + 1)], start=False, stop=True)
                        last.then_inc(s_ready, 1)
                    if 1 <= h <= NH:
                        n = h - 1
                        te.wait_ge(p_ready, L * 2 * NH + 2 * n + 2)
                        if n >= 2:
                            te.wait_ge(pT_used, L * NH + n - 1)
                        for t in range(3):
                            last = te.transpose(PS[:, 2 + n % 2, 128 * t:128 * t + 128], spr[n % 3][:, 128 * t:128 * t + 128], ident)
                        last.then_inc(pT_ready, 1)
                    if h >= 2:
                        n = h - 2
                        moba = n < AH
                        e = n if moba else n - AH
                        pr = n // 2 if n < 10 else 5
                        hf = n % 2 if n < 10 else 1
                        te.wait_ge(pT_used, L * NH + n + 1)
                        if pr >= 2 and (n % 2 == 0):
                            te.wait_ge(o_used, L * 6 + pr - 1)
                        settle(te)
                        g, c0 = (1, 64 * e) if moba else (3, HCOL[e])
                        out = PS[64 * hf:64 * hf + 64, 4 + pr % 2, 0:SEQ]
                        te.matmul(out, tok[:, 0, g * 384 + c0:g * 384 + c0 + 64], ppt[n % 2][:, 0:256], start=True, stop=True)
                        te.matmul(out[:, 128:256], tok[:, 1, g * 384 + c0:g * 384 + c0 + 64], ppt[n % 2][:, 256:384], start=False, stop=True,
                                  skip_group_check=True).then_inc(o_ready, 1)
                te.wait_ge(h_qk, L + 1)
                te.wait_ge(o_used, L * 6 + 6)
                for n in range(9):
                    if n >= 2:
                        te.wait_ge(h_pused, L * 8 + n - 1)
                    if n >= 1:
                        te.wait_ge(h_g, L * 8 + n)
                    settle(te)
                    bk = 4 * (n % 2)
                    for at, h in enumerate(ORD):
                        j, hf = HEADS5[h]
                        r = slice(64 * hf, 64 * hf + 64)
                        if n == 0:
                            kk, qq = pt(T["fc"] + j), pt(T["qc"] + j)
                        else:
                            kk = qq = V_(4 if n % 2 == 1 else 0, j)
                        if n < 8:
                            for t in range(2):
                                c = 256 * (at % 2) + 128 * t
                                last = te.matmul(PS[:, bk + at // 2, c:c + 128],
                                                 kk[r, 128 * t:128 * t + 128], qq[r, 128 * t:128 * t + 128], start=True, stop=True)
                            if n < 4:
                                c = NS * at if at < 2 else 256 + NS * (at - 2)
                                last = te.matmul(PS[0:NS, bk + (3 if at < 2 else 2), c:c + NS], kk[r, SEQ:NT], qq[r, SEQ:NT], start=True, stop=True)
                        else:
                            c = 128 * (at if at < 2 else at - 2)
                            last = te.matmul(PS[:, bk + (0 if at < 2 else 1), c:c + 128], kk[r, 0:128], qq[r, 128:256], start=True, stop=True)
                    last.then_inc(h_p, 1)
                te.wait_ge(h_kd, L + 1)
                te.wait_ge(h_pused, L * 8 + 8)
                for tt in range(2):
                    for j in range(3):
                        last = te.transpose(PS[:, 4 + tt, 128 * j:128 * j + 128], V_(1, j)[:, 128 * tt:128 * tt + 128], ident)
                    last.then_inc(h_kdT, 1)
                for j in range(3):
                    last = te.matmul(PS[0:NS, 6, 128 * j:128 * j + 128], V_(1, j)[:, SEQ:NT], ident, start=True, stop=True)
                last.then_inc(h_kdT, 1)
                te.wait_ge(h_ac, L * 2 + 2)
                te.wait_ge(s0_in, L * 48 + 48)
                for j, hf, h in VH:
                    r = slice(64 * hf, 64 * hf + 64)
                    c = 4 * 384 + 128 * j + 64 * hf
                    o, at = PS[r, j, :], ORD.index(h)
                    te.matmul(o[:, 0:128], tok[:, 0, c:c + 64], am[:, at, 0:128], start=True, stop=True)
                    te.matmul(o[:, 128:256], tok[:, 0, c:c + 64], ac[:, at, :], start=True, stop=False)
                    te.matmul(o[:, 128:256], tok[:, 1, c:c + 64], am[:, at, 128:256], start=False, stop=True)
                    last = te.matmul(o[:, 256:320], tok[0:NS, 2, c:c + 64], asm[:, at, :], start=True, stop=False, skip_group_check=True)
                last.then_inc(h_oa, 1)
                te.wait_ge(h_oa, L + 1)
                settle(te)
                for j, hf, h in VH:
                    r = slice(64 * hf, 64 * hf + 64)
                    o = PS[r, j, :]
                    for q in range(DB):
                        last = te.matmul(o[:, 256 + 8 * q:264 + 8 * q], s0[r, j, q, :], qe[r, j, 8 * q:8 * q + 8], start=False, stop=q == DB - 1, skip_group_check=True)
                last.then_inc(h_o, 1)
                te.wait_ge(h_kdU, L * 3 + 3)
                settle(te)
                for e, (j, hf) in enumerate(HEADS5):
                    r = slice(64 * hf, 64 * hf + 64)
                    for tt in range(2):
                        last = te.matmul(PS[r, 7, 64 * j:64 * j + 64], kdt[:, tt, HCOL[e]:HCOL[e] + 64], tok[:, tt, 4 * 384 + HCOL[e]:4 * 384 + HCOL[e] + 64],
                                         start=tt == 0, stop=tt == 1)
                last.then_inc(h_st, 1)
                for e, (j, hf) in enumerate(HEADS5):
                    r = slice(64 * hf, 64 * hf + 64)
                    te.wait_ge(h_vx, L * CH + e + 1)
                    settle(te)
                    vx = [b[0][0:NS, 0:512], P[0:NS, T["qc"] * NT:T["qc"] * NT + 512]][e % 2]
                    te.matmul(PS[r, 4 + j, :], kdt[0:NS, 2, HCOL[e]:HCOL[e] + 64], vx, start=True, stop=True).then_inc(h_sn, 1)
                te.wait_ge(h_sq, L + 1)
                te.wait_ge(h_snU, L * 3 + 3)
                for j in range(3):
                    last = te.matmul(PS[:, 4 + j, 0:NT], cst("blk"), V_(4, j), start=True, stop=True)
                last.then_inc(h_ms, 1)
                te.wait_ge(q_ready, L + 1)
                settle(te)
                for pr in range(6):
                    t = pt((T["ka"] if pr < 3 else T["kf"]) + pr % 3)[:, SEQ:NT]
                    last = te.matmul(PS[0:NS, 4 + pr // 4, 128 * (pr % 4):128 * (pr % 4) + 128], t,
                                     qb[:, pr, :, :].rearrange("p b c -> p (b c)"), start=True, stop=True)
                last.then_inc(sn_ready, 1)
                te.wait_ge(sn_used, L + 1)
                settle(te)
                for b_ in range(DB):
                    last = te.transpose(PS[0:ROWS, 6, 64 * b_:64 * b_ + 64], newb[:, b_, :], ident[0:NS, 0:NS])
                last.then_inc(snT_ready, 1)
                te.wait_ge(d_init, L + 1)
                settle(te)
                PAIRS = (0, 128, 256, AW, AW + 128, AW + 192)

                def turn_page(Q, pg):
                    s = pg % 4
                    te.wait_ge(k_in[s], (Q * 2 + pg // 4) * 32 + 32)
                    te.wait_ge(kT_act, Q * NPG + pg + 1)
                    te.wait_ge(kT_dve, Q * NPG + pg + 1)
                    for j, c in enumerate(PAIRS):
                        last = te.transpose(PS[:, 2 * (pg % 2) + j // 3, 128 * (j % 3):128 * (j % 3) + 128], kpg[:, s, c:c + 128], ident)
                    last.then_inc(kT_ready, 1)

                def block_scores(Q, n, softmax):
                    if n == 0:
                        te.wait_ge(qz_ready, Q + 1)
                        if softmax:
                            te.wait_ge(d_exp, Q * 5)
                    te.wait_ge(kT_act, Q * NPG + 2 * n + 4)
                    te.wait_ge(kT_dve, Q * NPG + 2 * n + 4)
                    o = PS[0:ROWS, 4 + n // 2, 256 * (n % 2):256 * (n % 2) + 256]
                    te.matmul(o, sel[:, :], brow[:, 256 * n:256 * n + 256], start=True, stop=False)
                    for pr in range(6):
                        last = te.matmul(o, qz[:, pr, :], ktb[n % 2][:, pr, :], start=False, stop=pr == 5)
                    last.then_inc(kT_used, 1)

                def turn_weights(Q):
                    te.wait_ge(d_exp, Q * 5 + 5)
                    for g in range(9):
                        last = te.transpose(PS[:, g // 5, 88 * (g % 5):88 * (g % 5) + 88], pe_[:, 128 * g:128 * g + 128], ident[0:ROWS, 0:ROWS])
                        if g in (4, 8):
                            last.then_inc(dpT_ready, 1)

                def values(Q):
                    te.wait_ge(dpT_act, Q + 1)
                    te.wait_ge(dpT_dve, Q + 1)
                    te.wait_ge(do_used, Q * 11 + 4)
                    for g in range(NPG):
                        te.wait_ge(v_in[g], Q * 32 + 32)
                        te.matmul(PS[0:ROWS, 6, 0:AW], ptt[:, g, :], vpg[:, g, 0:AW], start=g == 0, stop=False, skip_group_check=True)
                        te.matmul(PS[0:ROWS, 7, 0:BW], ptt[:, g, :], vpg[:, g, AW:AW + BW], start=g == 0, stop=False, skip_group_check=True
                                  ).then_inc(v_used, 1)
                    p, v = ptt[0:NS, NPG, :], tok[0:NS, 2, :]
                    te.matmul(PS[0:ROWS, 6, 0:AW], p, v[:, 384:384 + AW], start=False, stop=True, skip_group_check=True)
                    te.matmul(PS[0:ROWS, 7, 0:256], p, v[:, 3 * 384:3 * 384 + 256], start=False, stop=True, skip_group_check=True)
                    te.matmul(PS[0:ROWS, 7, 256:320], p, v[:, 3 * 384 + 320:3 * 384 + 384], start=False, stop=True, skip_group_check=True
                              ).then_inc(do_ready, 1)

                def turn_outputs(Q):
                    te.wait_ge(ob_ready, Q + 1)
                    for pr, c in enumerate(PAIRS):
                        last = te.transpose(PS[:, 6 + pr // 5, 88 * (pr % 5):88 * (pr % 5) + 88], ob[:, c:c + 128], ident[0:ROWS, 0:ROWS])
                    last.then_inc(obT_ready, 1)

                def step(Q, softmax, products):
                    if products:
                        te.wait_ge(dpT_act, Q - 1)
                        te.wait_ge(dpT_dve, Q - 1)
                    turn_page(Q, 0)
                    turn_page(Q, 1)
                    if products:
                        values(Q - 2)
                    turn_page(Q, 2)
                    block_scores(Q, 0, softmax)
                    if products:
                        turn_outputs(Q - 2)
                    turn_page(Q, 3)
                    for n in range(1, 4):
                        if n < 3:
                            turn_page(Q, 2 * n + 2)
                        block_scores(Q, n, softmax)
                        if n < 3:
                            turn_page(Q, 2 * n + 3)
                        if n == 2 and softmax:
                            te.wait_ge(kT_act, Q * NPG + 9)
                            te.wait_ge(kT_dve, Q * NPG + 9)
                            turn_weights(Q - 1)

                step(L * DB, False, False)
                step(L * DB + 1, True, False)
                with te.Fori(2, DB) as q:
                    step(L * DB + q, True, True)
                Q = L * DB + DB - 1
                values(Q - 1)
                turn_outputs(Q - 1)
                turn_weights(Q)
                values(Q)
                turn_outputs(Q)
                te.wait_ge(ol_ready, L * 9 + 9)
                settle(te)
                with te.Fori(0, 2) as m:
                    for dp in range(2):
                        for s in range(2):
                            chunk(s, L * USES + OFF["wout"] + m * 2 + dp)
                            if s == 0:
                                kts = [(k, k, ALLR) for k in range(5)] + [(5, 5, slice(64, 128))]
                            else:
                                kts = [(0, 6, ALLR), (1, 7, ALLR), (2, 8, slice(64, 128))]
                            for j in range(2):
                                if s == 0:
                                    te.wait_ge(acc_used, L * 24 + 8 + m * 4 + 2 * dp + j + 1)
                                last = dense(PS[:, 4 + 2 * dp + j, 0:NT], s, slice(128 * j, 128 * j + 128), (xh, xl), kts, s == 0, s == 1)
                                if j == 1:
                                    last.then_inc(w_free[s], 1)
                                elif s == 1:
                                    last.then_inc(acc_ready, 1)
                norm(L * 3 + 2)
                ffn(1, L, L * 3 + 2)
            norm(DEPTH * 3)
            te.wait_ge(xs_ready, DEPTH * 3 * KT_D + KT_D)
            for n in range(6):
                tt, hf = divmod(n, 2)
                for k in range(4):
                    at = (4 * hf + k) * NT + tt * 128
                    last = te.transpose(PS[:, n, 128 * k:128 * k + 128], X[:, at:at + 128], ident)
                last.then_inc(f_T, 1)


INS = ["x_prompt", "x_sample", "cache_moba_k", "cache_moba_v", "cache_fox_k", "cache_fox_v", "cache_fox_logf", "state_hgrn",
       "page_table", "norm_ffn1_g", "ffn1_w_gate", "ffn1_w_up", "ffn1_w_down", "norm_mix_g", "w_in", "fox_f_bias",
       "hgrn_lb_logits", "hgrn_norm_g", "w_out", "norm_ffn2_g", "ffn2_w_gate", "ffn2_w_up", "ffn2_w_down", "norm_final_g"]
OUTS = [("y_prompt", (1, SEQ, D)), ("y_sample", (DB, DS, D)),
        ("moba_k_prompt", (DEPTH, 1, SEQ, AH, HD)), ("moba_v_prompt", (DEPTH, 1, SEQ, AH, HD)),
        ("fox_k_prompt", (DEPTH, 1, SEQ, BH, HD)), ("fox_v_prompt", (DEPTH, 1, SEQ, BH, HD)),
        ("fox_logf_prompt", (DEPTH, 1, SEQ, BH)), ("hgrn_state_prompt", (DEPTH, 1, CH, HD, HD)),
        ("moba_k_sample", (DEPTH, DB, DS, AH, HD)), ("moba_v_sample", (DEPTH, DB, DS, AH, HD)),
        ("fox_k_sample", (DEPTH, DB, DS, BH, HD)), ("fox_v_sample", (DEPTH, DB, DS, BH, HD)),
        ("fox_logf_sample", (DEPTH, DB, DS, BH)), ("hgrn_state_sample", (DEPTH, DB, CH, HD, HD))]


def kernel(**inputs):
    import concourse.bacc as bacc
    from concourse.bass_utils import run_bass_kernel_spmd

    nc = bacc.Bacc("TRN2", target_bir_lowering=False, num_devices=1)
    arrays, a = {}, {}
    for name in INS + ["consts"]:
        v = constants() if name == "consts" else np.ascontiguousarray(inputs[name])
        arrays["in_" + name] = v
        a[name] = nc.dram_tensor("in_" + name, v.shape, mybir.dt.from_np(v.dtype), kind="ExternalInput").ap()
    outs = {n: nc.dram_tensor("out_" + n, s, F32, kind="ExternalOutput").ap() for n, s in OUTS}
    trunk(nc, a, outs)
    r = run_bass_kernel_spmd(nc, [arrays], core_ids=[0])
    return tuple(r.results[0]["out_" + n] for n, _ in OUTS)
```

```python
from contextlib import ExitStack

import numpy as np

import concourse.bass as bass
from concourse import mybir

F32 = mybir.dt.float32
F32R = mybir.dt.float32r
I32 = mybir.dt.int32
U32 = mybir.dt.uint32
ALU = mybir.AluOpType
ACT = mybir.ActivationFunctionType
AX = mybir.AxisListType
ds = bass.ds

D, SEQ, DEPTH, DB, DS = 1024, 256, 2, 8, 8
PAST, PAGE = 1024, 128
HD, AH, BH, CH = 64, 6, 5, 5
FF = 2816
NS = DB * DS
NT = SEQ + NS
KT_D = D // 128
FT = FF // 128
NPG = PAST // PAGE
NPOOL = DB * NPG * 5 // 4
BLK = 256
NBLK = PAST // BLK
EPS, NEG = 1e-6, -1e30
SCALE = HD ** -0.5
AW, BW = AH * HD, BH * HD
NH = AH + BH
ROWS = NH * DS
LEVELS = 7

_THIRD = [0, 128, 192]
_col = {}
_c = 0
for _n, _w in (("qa", AW), ("ka", AW), ("va", AW), ("qf", BW), ("kf", BW), ("vf", BW), ("ff", BH),
               ("qc", BW), ("fc", BW), ("ic", BW), ("gc", BW)):
    _col[_n] = _c
    _c += _w
D_IN = _c
TILES, T = [], {}
for _n in ("qa", "ka", "va", "qf", "kf", "vf", "ff", "qc", "fc", "ic", "gc"):
    T[_n] = len(TILES)
    if _n == "ff":
        TILES += [_col[_n]]
    elif _n in ("qa", "ka", "va"):
        TILES += [_col[_n] + 128 * j for j in range(3)]
    else:
        TILES += [_col[_n] + _THIRD[j] for j in range(3)]
TILES += [TILES[-1]]
WIN_CHUNKS = len(TILES) // 2
OUT_T = [T["va"], T["va"] + 1, T["va"] + 2, T["vf"], T["vf"] + 1, T["vf"] + 2, T["ic"], T["ic"] + 1, T["ic"] + 2]
HEADS5 = [(0, 0), (0, 1), (1, 0), (1, 1), (2, 1)]
ORD = [0, 2, 1, 3, 4]
HCOL = [0, 64, 128, 192, 320]

GU, DOWN, WIN, WOUT = FT // 2, 6, WIN_CHUNKS // 2, 4
OFF = {"ffn1": 0, "down1": GU, "win": GU + DOWN, "wout": GU + DOWN + WIN,
       "ffn2": GU + DOWN + WIN + WOUT, "down2": 2 * GU + DOWN + WIN + WOUT}
USES = 2 * GU + 2 * DOWN + WIN + WOUT

C, _w0 = {}, 0
for _n, _w in (("ident", 128), ("ones", 128), ("blk", 128), ("perm", 128), ("cos", NT), ("sin", NT),
               ("causal", 384), ("lmask", (LEVELS + 1) * 128), ("reset", NT), ("newmask", DB * DS),
               ("later", 128), ("seqof", DB), ("place", NBLK),
               ("hsel", NH * DS), ("rowsel", DEPTH * DB), ("eps", 1)):
    C[_n] = (_w0, _w)
    _w0 += _w
NC_COLS = _w0


def constants():
    c = np.zeros((128, NC_COLS), np.float32)

    def put(name, a):
        o, w = C[name]
        c[:a.shape[0], o:o + w] = a.reshape(a.shape[0], w)

    i = np.arange(128)
    put("ident", np.eye(128))
    put("ones", np.ones((128, 128)))
    put("blk", (i[:, None] // 64 == i[None, :] // 64).astype(np.float32))
    perm = np.zeros((128, 128))
    for m in range(128):
        if m % 64 < 32:
            perm[m + 32, m] = -1.0
        else:
            perm[m - 32, m] = 1.0
    put("perm", perm)
    half = HD // 2
    inv = np.power(np.float32(10000.0), -np.arange(half, dtype=np.float32) * np.float32(2.0) / np.float32(HD))
    pos = np.concatenate([np.arange(SEQ), np.tile(PAST + np.arange(DS), DB)]).astype(np.float32)
    ang = (pos[None, :] * inv[i % half, None]).astype(np.float32)
    put("cos", np.cos(ang))
    put("sin", np.sin(ang))
    tri = np.where(i[None, :] <= i[:, None], 0.0, NEG)
    put("causal", np.concatenate([tri, np.zeros((128, 128)), tri], 1))
    lm = np.zeros((128, LEVELS + 1, 128))
    for l in range(LEVELS):
        h = 1 << l
        s, t = i[:, None], i[None, :]
        lm[:, l] = (s // (2 * h) == t // (2 * h)) & (s % (2 * h) < h) & (t % (2 * h) >= h)
    lm[:, LEVELS] = np.eye(128)
    put("lmask", lm)
    reset = np.ones((128, NT))
    reset[:, 0] = 0
    reset[:, SEQ::DS] = 0
    put("reset", reset)
    k = np.arange(NS)
    nm = np.full((NS, DB, DS), NEG)
    for b in range(DB):
        for t in range(DS):
            nm[(k // DS == b) & (k % DS <= t), b, t] = 0.0
    put("newmask", nm)
    put("later", (i[:, None] > i[None, :]).astype(np.float32))
    put("seqof", (k[:, None] // DS == np.arange(DB)[None, :]).astype(np.float32))
    r = np.arange(DEPTH * BH * DB)
    put("hsel", (np.arange(ROWS)[None, :] // DS == AH + (r[:, None] // DB) % BH).astype(np.float32))
    q = np.arange(DEPTH * DB)
    put("rowsel", ((r[:, None] // (BH * DB) == q[None, :] // DB) & (r[:, None] % DB == q[None, :] % DB)).astype(np.float32))
    put("eps", np.full((128, 1), EPS))
    put("place", np.tile(2.0 ** np.arange(NBLK), (128, 1)))
    return c


ACT_STEPS = 6
DVE_STEPS = 363
DECODE_STEPS = 19


class Chain:

    def __init__(self, eng, sem):
        self.eng, self.sem, self.base, self.n = eng, sem, 0, 0

    def mark(self, ins):
        self.n += 1
        return ins.then_inc(self.sem, 1)

    def catch_up(self):
        self.eng.wait_ge(self.sem, self.base + self.n)

    def link(self, ins):
        self.mark(ins)
        self.catch_up()

    def enter(self, i, steps):
        self._out = (self.base, self.n)
        self.base, self.n = self.base + self.n + i * steps, 0

    def leave(self, trips, steps):
        assert self.n == steps, (self.n, steps)
        self.base, self.n = self._out[0], self._out[1] + trips * steps


def trunk(nc, a, outs):
    ctx = ExitStack()
    with ctx:
        def sb(name, shape, dt=F32, into=ctx):
            return into.enter_context(nc.sbuf_tensor(name, shape, dt))

        def sem(name):
            return ctx.enter_context(nc.semaphore(name))

        X = sb("X", [128, KT_D * NT + 64])
        xt = lambda k: X[:, k * NT:(k + 1) * NT]
        K = sb("K", [128, NC_COLS])
        cst = lambda name: K[:, C[name][0]:C[name][0] + C[name][1]]
        gains = sb("gains", [128, DEPTH * 24 + 8])
        gcur = sb("gcur", [128, 24])
        lbt = sb("lbt", [128, DEPTH, 6])
        lbcur = sb("lbcur", [128, 6])
        gh = sb("gh", [128, DEPTH])
        ghcur = sb("ghcur", [128, 1])
        fb = sb("fb", [BH, DEPTH])
        fbcur = sb("fbcur", [BH, 1])
        pages = sb("pages", [1, DB * NPG], I32)
        brow = [sb(f"brow{n}", [DEPTH * BH * DB, PAST], F32R) for n in range(2)]
        ncn = sb("ncn", [BH, NT + 64])
        tokn = sb("tokn", [NS, BH])
        junk = sb("junk", [128, 1])
        sqsum = sb("sqsum", [128, NT])
        rstd = sb("rstd", [128, NT])
        tmp = [sb(f"tmp{j}", [128, NT]) for j in range(4)]
        raw = [sb(f"raw{s}", [128, 8, 256]) for s in range(2)]
        whi, wlo = [sb("whi0", [128, 8, 256], F32R)], [sb("wlo0", [128, 8, 256], F32R)]
        with ExitStack() as r0:
            whi.append(sb("whi1", [128, 8, 256], F32R, r0))
            wlo.append(sb("wlo1", [128, 8, 256], F32R, r0))
        idle = sb("idle", [128, 2 * 8 * 256])
        with ExitStack() as r1:
            xh = sb("xh", [128, 9, NT], F32R, r1)
            xl = sb("xl", [128, 9, NT], F32R, r1)
        value_pages = sb("value_pages", [128, NPG, AW + BW])
        sb("value_rest", [128, 18 * NT - NPG * (AW + BW)])
        with ExitStack() as r2:
            hh = sb("hh", [128, FT, NT], F32R, r2)
            hl = sb("hl", [128, FT, NT], F32R, r2)
        P = sb("P", [128, 32 * NT + 64])
        pt = lambda n: P[:, n * NT:(n + 1) * NT]
        p3 = lambda n: P[:, n * NT:(n + 3) * NT].rearrange("p (j t) -> p j t", j=3)
        with ExitStack() as r5:
            tokp = sb("tokp", [128, 2, 5 * 384], F32, r5)
        keys_hi = sb("keys_hi", [128, 2, 6, 256], F32R)
        sb("keys_rest", [128, 2 * 5 * 384 - 2 * 6 * 256])
        toks = sb("toks", [128, 5 * 384])
        tok = lambda tt: tokp[:, tt, :] if tt < 2 else toks[:, :]
        tokf = sb("tokf", [128, 3, BH])
        with ExitStack() as r3:
            b = [sb(f"b{i}", [128, 3 * NT], F32, r3) for i in range(5)]
            end_keys_t = sb("end_keys_t", [128, 3, 384], F32, r3)
            states = sb("states", [128, 3, DB, 64], F32, r3)
        with ExitStack() as r4:
            key_pages = sb("key_pages", [128, 4, AW + BW], F32, r4)
            new_row_all = sb("new_row_all", [ROWS, DB, NS], F32, r4)
            weight_rows = sb("weight_rows", [ROWS, 1152], F32, r4)
            weight_cols = sb("weight_cols", [128, 9, ROWS], F32, r4)
            out_rows = sb("out_rows", [ROWS, AW + BW], F32, r4)
            qz = [sb(f"qz{n}", [128, 6, ROWS], F32R, r4) for n in range(2)]
            sel = sb("sel", [DEPTH * BH * DB, ROWS], F32R, r4)
            gate_bias = sb("gate_bias", [ROWS, NBLK + 1], F32, r4)
            gate_sums = sb("gate_sums", [48, 4, NBLK], F32, r4)
            block_max = sb("block_max", [ROWS, NBLK + 1], F32, r4)
            exp_bias = sb("exp_bias", [ROWS, NBLK + 1], F32, r4)
            exp_sums = sb("exp_sums", [ROWS, NBLK + 1], F32, r4)
            row_stats = sb("row_stats", [ROWS, 2], F32, r4)
        q_decayed = tmp[0][:, 0:192].rearrange("p (j t) -> p j t", j=3)
        state_decay = tmp[0][:, 192:216].rearrange("p (j t) -> p j t", j=3)
        a_samples = tmp[1][0:NS, :].rearrange("p (h t) -> p h t", h=CH)
        prompt_state = tmp[3][:, 0:192].rearrange("p (j t) -> p j t", j=3)
        key_halves = [[keys_hi[:, n] for n in range(2)],
               [w[:, :, :].rearrange("p a b -> p (a b)")[:, 0:1536].rearrange("p (j c) -> p j c", j=6) for w in (whi[0], wlo[0])]]
        V_ = lambda i, j: b[i][:, j * NT:(j + 1) * NT]
        VH = [(0, 0, 0), (0, 1, 1), (1, 0, 2), (1, 1, 3), (2, 0, 3), (2, 1, 4)]
        probs = [idle[:, 384 * n:384 * n + 384] for n in range(4)]
        probs_t = [idle[:, 384 * n:384 * n + 384] for n in range(4, 6)]
        prob_stats = idle[:, 2304:2352]
        qb = idle[:, 640:640 + 6 * DB * 16].rearrange("p (j b c) -> p j b c", j=6, b=DB)
        newb = idle[0:NS, 1408:1408 + DB * ROWS].rearrange("p (b c) -> p b c", b=DB)
        new_row = idle[0:ROWS, 0:NS]
        a_blocks = idle[:, 2352:2352 + CH * 256].rearrange("p (h t) -> p h t", h=CH)
        a_cross = idle[:, 0:CH * 128].rearrange("p (h t) -> p h t", h=CH)
        PS = ctx.enter_context(nc.psum_tensor("PS", [128, 8, 512], F32))

        consts_in = sem("consts_in")
        waited = sem("waited")
        small_in = sem("small_in")
        page_column_in = sem("page_column_in")
        tables_in = sem("tables_in")
        x_in = sem("x_in")
        past_logf_in = sem("past_logf_in")
        page_rows_ready = sem("page_rows_ready")
        page_table_in = sem("page_table_in")
        lb_diff, lb_sig = sem("lb_diff"), sem("lb_sig")
        vector_step, scalar_step = sem("vector_step"), sem("scalar_step")
        raw_in = [sem(f"raw_in{s}") for s in range(2)]
        hi_done = [sem(f"hi_done{s}") for s in range(2)]
        split_done = [sem(f"split_done{s}") for s in range(2)]
        w_free = [sem(f"weights_free{s}") for s in range(2)]
        gate_ready, silu_done, up_ready, up_used, h_done = (
            sem(n) for n in ("gate_ready", "silu_done", "up_ready", "up_used", "h_done"))
        acc_ready, acc_used = sem("acc_ready"), sem("acc_used")
        ms_ready, sqsum_ready, rstd_ready, xs_ready, xh_ready, xl_ready, rms_ready = (
            sem(n) for n in ("ms_ready", "sqsum_ready", "rstd_ready", "xs_ready", "xh_ready", "xl_ready", "rms_ready"))
        win_ready, win_used = sem("win_ready"), sem("win_used")
        rot_ready, roped = sem("rot_ready"), sem("roped")
        qf_scaled = sem("qf_scaled")
        z_ready, z_exp, lf_ready = sem("z_ready"), sem("z_ln"), sem("lf_ready")
        rows_turned, rows_copied_dve, rows_copied_act = sem("rows_turned"), sem("rows_copied_dve"), sem("rows_copied_act")
        prompt_scores_ready, prompt_probs_ready, prompt_probs_turned, prompt_probs_copied, prompt_out_ready, prompt_out_copied, prompt_max_ready, prompt_exp_ready, prompt_scores_read = (
            sem(n) for n in ("prompt_scores_ready", "prompt_probs_ready", "prompt_probs_turned", "prompt_probs_copied", "prompt_out_ready", "prompt_out_copied",
                             "prompt_max_ready", "prompt_exp_ready", "prompt_scores_read"))
        rec_own_sums_done = sem("rec_own_sums_done")
        rec_sigmoids_ready, rec_qk_ready, rec_logf_ready = (sem(n) for n in ("rec_sigmoids_ready", "rec_qk_ready", "rec_logf_ready"))
        decay_logs_ready, decays_ready, level_factors_ready, level_products_ready, level_products_taken, cross_products_copied = (sem(n) for n in ("decay_logs_ready", "decays_ready", "level_factors_ready", "level_products_ready", "level_products_taken", "cross_products_copied"))
        end_keys_ready, end_keys_turned, end_keys_copied, rec_out_ready, rec_squares_ready, rec_mean_squares_ready, rec_rstd_ready, rec_out_done = (
            sem(n) for n in ("end_keys_ready", "end_keys_turned", "end_keys_copied", "rec_out_ready", "rec_squares_ready", "rec_mean_squares_ready", "rec_rstd_ready", "rec_out_done"))
        prompt_state_ready, prompt_state_copied, spread_values_ready, state_products_ready, sample_states_done, states_in = (sem(n) for n in ("prompt_state_ready", "prompt_state_copied", "spread_values_ready", "state_products_ready", "sample_states_done", "states_in"))
        k_in = [sem(f"k_in{j}") for j in range(4)]
        v_in = [sem(f"v_in{j}") for j in range(NPG)]
        decode_queries_ready = sem("decode_queries_ready")
        decode_ready, keys_turned, keys_hi_copied, keys_lo_copied, seq_queries_ready, new_scores_ready, new_scores_masked, new_scores_turned = (
            sem(n) for n in ("decode_ready", "keys_turned", "keys_hi_copied", "keys_lo_copied", "seq_queries_ready", "new_scores_ready", "new_scores_masked", "new_scores_turned"))
        exp_bias_ready, weights_ready, values_used, outputs_scaled, outputs_turned = (
            sem(n) for n in ("exp_bias_ready", "weights_ready", "values_used", "outputs_scaled", "outputs_turned"))
        weights_turned, weights_copied_act, weights_copied_dve, value_sums_ready, outputs_copied, block_scores_done = (
            sem(n) for n in ("weights_turned", "weights_copied_act", "weights_copied_dve", "value_sums_ready", "outputs_copied", "block_scores_done"))
        x_turned, gains_turned, past_logf_turned, past_sums_ready, later_pages_ready = (
            sem(n) for n in ("x_turned", "gains_turned", "past_logf_turned", "past_sums_ready", "later_pages_ready"))
        past_sums_copied, past_sums_turned = sem("past_sums_copied"), sem("past_sums_turned")
        out_hi_ready, out_lo_ready = sem("out_hi_ready"), sem("out_lo_ready")
        y_turned, y_copied, f_out = sem("y_turned"), sem("y_copied"), sem("y_out")
        out_tok, out_st = sem("out_tok"), sem("out_state")

        block = ctx.enter_context(nc.Block())
        SMALL = DEPTH * 9 + 1

        wg = [a["ffn1_w_gate"], a["ffn2_w_gate"]]
        wu = [a["ffn1_w_up"], a["ffn2_w_up"]]
        wd = [a["ffn1_w_down"], a["ffn2_w_down"]]
        gu_v = lambda w: w.rearrange("l (k p) n -> p (l k) n", p=128)

        def tile_done(eng, j, first_ready, n, s, use):
            if j == 0:
                eng.wait_ge(first_ready, n + 1)
            else:
                eng.wait_ge(w_free[s], use + 2)

        def settle(eng):
            eng.sem_inc(waited, 1)

        @block.sync
        def _(sp):
            def fill(s, use, parts):
                sp.wait_ge(split_done[s], use + 1)
                for n, (dst, src) in enumerate(parts):
                    ins = sp.dma_start(dst, src)
                    ins.then_inc(raw_in[s], 16 if len(parts) == 2 else 32)

            def gu_chunk(f, L, i):
                u = L * USES + OFF[f"ffn{f + 1}"] + i
                for s, w in ((0, wg[f]), (1, wu[f])):
                    fill(s, u, [(raw[s][:, :, :], gu_v(w)[:, ds(L * 8, 8), ds(i * 256, 256)])])

            def down_chunks(f, L):
                wdv = wd[f].rearrange("l (k p) n -> p (l k) n", p=128)
                with sp.Fori(0, 2) as m:
                    for n in range(6):
                        dp, kk = divmod(n, 3)
                        nk = 8 if kk < 2 else FT - 16
                        fill(n % 2, L * USES + OFF[f"down{f + 1}"] + m * 3 + n // 2,
                             [(raw[n % 2][:, 0:nk, :], wdv[:, ds(L * FT + kk * 8, nk), ds(m * 512 + dp * 256, 256)])])

            def wout_chunks(L, m):
                u = L * USES + OFF["wout"] + m
                rows = lambda r0, n: a["w_out"][ds(L, 1), r0:r0 + n, ds(m * 256, 256)]
                fill(0, u, [(raw[0][:, 0:5, :], rows(0, 640).rearrange("l (k p) n -> p (l k) n", p=128)),
                            (raw[0][64:128, 5, :], rows(640, 64).rearrange("l p n -> (l p) n"))])
                fill(1, u, [(raw[1][:, 0:2, :], rows(704, 256).rearrange("l (k p) n -> p (l k) n", p=128)),
                            (raw[1][64:128, 2, :], rows(960, 64).rearrange("l p n -> (l p) n"))])

            sp.dma_start(K[:, 0:512], a["consts"][:, 0:512]).then_inc(consts_in, 16)
            sp.dma_start(pages[:, :], a["page_table"].rearrange("(o b) n -> o (b n)", o=1)).then_inc(page_table_in, 16)
            xtok = [raw[0].rearrange("p a b -> p (a b)")[:, 0:1024], raw[0].rearrange("p a b -> p (a b)")[:, 1024:2048],
                    raw[1].rearrange("p a b -> p (a b)")[:, 0:1024]]
            xp = a["x_prompt"].rearrange("b (n p) d -> (b n) p d", p=128)
            for n in range(2):
                sp.dma_start(xtok[n], xp[n]).then_inc(x_in, 16)
            sp.dma_start(xtok[2][0:NS, :], a["x_sample"].rearrange("b t d -> (b t) d")).then_inc(x_in, 16)
            sp.dma_start(K[:, 512:], a["consts"][:, 512:]).then_inc(tables_in, 16)
            sp.wait_ge(page_table_in, 16)
            gu_chunk(0, 0, 0)
            with sp.Fori(0, DEPTH) as L:
                with sp.Fori(1, GU) as i:
                    gu_chunk(0, L, i)
                down_chunks(0, L)
                winv = a["w_in"].rearrange("l (k p) n -> p (l k) n", p=128)
                for c in range(WIN_CHUNKS):
                    s = c % 2
                    fill(s, L * USES + OFF["win"] + c // 2,
                         [(raw[s][:, :, 128 * j:128 * j + 128],
                           winv[:, ds(L * 8, 8), TILES[2 * c + j]:TILES[2 * c + j] + 128]) for j in range(2)])
                wout_chunks(L, 0)
                for j in range(3):
                    if j == 0:
                        sp.wait_ge(win_used, L * 32 + 36)
                    hs = [0, 2, 3][j]
                    sp.dma_start(states[:, j, :, :],
                                 a["state_hgrn"][ds(L, 1), :, hs:hs + 2, :, :].rearrange("l b h d e -> (l h d) b e")
                                 ).then_inc(states_in, 16)
                sp.wait_ge(rows_copied_dve, L * 9 + 9)
                sp.wait_ge(rows_copied_act, L * 7 + 7)
                for g, (op, os, w) in enumerate((("moba_k_prompt", "moba_k_sample", AW), ("moba_v_prompt", "moba_v_sample", AW),
                                                 ("fox_k_prompt", "fox_k_sample", BW), ("fox_v_prompt", "fox_v_sample", BW))):
                    for c0, n, t0 in ((0, 384, 0),) if w == AW else ((0, 256, 0), (256, 64, 320)):
                        pv = outs[op].rearrange("l b (n p) h d -> p (l b n) (h d)", p=128)
                        sv = outs[os].rearrange("l b t h d -> l (b t) (h d)")
                        sp.dma_start(pv[:, ds(L * 2, 2), c0:c0 + n], tokp[:, 0:2, g * 384 + t0:g * 384 + t0 + n]).then_inc(out_tok, 16)
                        sp.dma_start(sv[ds(L, 1), :, c0:c0 + n].rearrange("l t c -> (l t) c"),
                                     toks[0:NS, g * 384 + t0:g * 384 + t0 + n]).then_inc(out_tok, 16)
                sp.dma_start(outs["fox_logf_prompt"].rearrange("l b (n p) h -> p (l b n) h", p=128)[:, ds(L * 2, 2), :],
                             tokf[:, 0:2, :]).then_inc(out_tok, 16)
                sp.dma_start(outs["fox_logf_sample"].rearrange("l b t h -> l (b t) h")[ds(L, 1), :, :].rearrange("l t h -> (l t) h"),
                             tokf[0:NS, 2, :]).then_inc(out_tok, 16)
                sp.wait_ge(prompt_state_copied, L + 1)
                sp.wait_ge(sample_states_done, L * 3 + 3)
                for j, (hs, p0) in enumerate(((0, 0), (2, 0), (4, 64))):
                    nh = 2 - p0 // 64
                    sp.dma_start(outs["hgrn_state_prompt"][ds(L, 1), 0, hs:hs + nh, :, :].rearrange("l h d e -> (l h d) e"),
                                 prompt_state[p0:128, j, :]).then_inc(out_st, 16)
                    sp.dma_start(outs["hgrn_state_sample"][ds(L, 1), :, hs:hs + nh, :, :].rearrange("l b h d e -> (l h d) b e"),
                                 states[p0:128, j, :, :]).then_inc(out_st, 16)
                sp.wait_ge(out_st, L * 96 + 96)
                kmv = a["cache_moba_k"].rearrange("l n p h d -> p (l n) (h d)")
                kfv = a["cache_fox_k"].rearrange("l n p h d -> p (l n) (h d)")
                sp.wait_ge(rec_out_done, L + 1)
                settle(sp)
                with sp.Fori(0, DB) as q:
                    for pg in range(NPG):
                        s = pg % 4
                        sp.wait_ge(keys_turned, (L * DB + q) * NPG + pg + 1)
                        page = sp.value_load(pages[0:1, ds(q * NPG + pg, 1)], min_val=0, max_val=NPOOL - 1)
                        sp.dma_start(key_pages[:, s, 0:AW], kmv[:, ds(page + L * NPOOL, 1), :].rearrange("p a c -> p (a c)")).then_inc(k_in[s], 16)
                        sp.dma_start(key_pages[:, s, AW:AW + BW], kfv[:, ds(page + L * NPOOL, 1), :].rearrange("p a c -> p (a c)")).then_inc(k_in[s], 16)
                with sp.Fori(1, 4) as m:
                    wout_chunks(L, m)
                with sp.Fori(0, GU) as i:
                    gu_chunk(1, L, i)
                down_chunks(1, L)
                nl = L * -1 + 1
                for s, w in ((0, wg[0]), (1, wu[0])):
                    fill(s, L * USES + USES, [(raw[s][:, :, :], gu_v(w)[:, ds(nl * 8, 8), 0:256])])
            for n in range(3):
                sp.wait_ge(y_copied, 2 * (n + 1))
                rows = 128 if n < 2 else NS
                dst = outs["y_prompt"].rearrange("b (n p) d -> (b n) p d", p=128)[n] if n < 2 else \
                    outs["y_sample"].rearrange("b t d -> (b t) d")
                sp.dma_start(dst, P[0:rows, n * 1024:(n + 1) * 1024]).then_inc(f_out, 16)
            sp.wait_ge(f_out, 48)
            sp.wait_ge(out_tok, 14 * 16 * DEPTH)
            sp.wait_ge(out_st, 6 * 16 * DEPTH)
            for s in range(2):
                sp.wait_ge(raw_in[s], 32 * (DEPTH * USES + 1))

        @block.gpsimd
        def _(pool):
            pool.dma_start(value_pages[0:DB * NPG, 1, 0:1].bitcast(I32), a["page_table"].rearrange("b (n o) -> (b n) o", o=1)).then_inc(page_column_in, 16)
            lfv = a["cache_fox_logf"].rearrange("l n p h -> (l n) (p h)")
            pool.wait_ge(page_rows_ready, DEPTH)
            for l in range(DEPTH):
                pool.indirect_dma_start(
                    value_pages[0:DB * NPG, 2 + l, 0:PAGE * BH], None, lfv,
                    bass.IndirectOffsetOnAxis(ap=value_pages[0:DB * NPG, 1, 2 + l:3 + l].bitcast(U32), axis=0)).then_inc(past_logf_in, 16)
            pool.wait_ge(page_table_in, 16)
            vmv = a["cache_moba_v"].rearrange("l n p h d -> p (l n) (h d)")
            vfv = a["cache_fox_v"].rearrange("l n p h d -> p (l n) (h d)")
            with pool.Fori(0, DEPTH) as L:
                pool.wait_ge(win_used, L * 32 + 36)
                settle(pool)
                with pool.Fori(0, DB) as q:
                    for pg in range(NPG):
                        pool.wait_ge(values_used, (L * DB + q) * NPG + pg + 1)
                        page = pool.value_load(pages[0:1, ds(q * NPG + pg, 1)], min_val=0, max_val=NPOOL - 1)
                        pool.dma_start(value_pages[:, pg, 0:AW], vmv[:, ds(page + L * NPOOL, 1), :].rearrange("p a c -> p (a c)")).then_inc(v_in[pg], 16)
                        pool.dma_start(value_pages[:, pg, AW:AW + BW], vfv[:, ds(page + L * NPOOL, 1), :].rearrange("p a c -> p (a c)")).then_inc(v_in[pg], 16)

        @block.scalar
        def _(act):
            ch = Chain(act, scalar_step)

            def hi(s, use, nk=8):
                act.wait_ge(raw_in[s], (use + 1) * 32)
                act.wait_ge(w_free[s], use + 1)
                act.activation(whi[s][:, 0:nk, :], raw[s][:, 0:nk, :], ACT.Copy).then_inc(hi_done[s], 1)

            def norm(w):
                ch.link(act.activation(junk[:, :], cst("eps"), ACT.Sqrt))
                act.wait_ge(ms_ready, w + 1)
                act.activation(rstd[:, :], PS[:, 7, 0:NT], ACT.Sqrt, bias=cst("eps"), scale=1.0 / D).then_inc(rms_ready, 1)

            def scaled(w):
                for k in range(KT_D):
                    act.wait_ge(xs_ready, w * KT_D + k + 1)
                    act.activation(xh[:, k, :], tmp[k % 4][:, :], ACT.Copy).then_inc(xh_ready, 1)

            def ffn(f, L):
                u0 = L * USES + OFF[f"ffn{f + 1}"]
                with act.Fori(0, GU) as i:
                    hi(1, u0 + i)
                    for j in range(2):
                        n = L * 2 * FT + f * FT + i * 2 + j
                        tile_done(act, j, gate_ready, L * 2 * GU + f * GU + i, 0, u0 + i)
                        act.wait_ge(up_used, n + 1)
                        act.activation(tmp[j][:, :], PS[:, j, 0:NT], ACT.Silu).then_inc(silu_done, 1)
                    hi(0, u0 + i + 1)
                u0 = L * USES + OFF[f"down{f + 1}"]
                with act.Fori(0, 2) as m:
                    for n in range(6):
                        hi((n + 1) % 2, u0 + m * 3 + (n + 1) // 2)

            grow = value_pages[:, 0, 0:128]
            n = 0
            with nc.allow_non_contiguous_dma(reason="small parameters"):
                for l in range(DEPTH):
                    for w, name in enumerate(("norm_ffn1_g", "norm_mix_g", "norm_ffn2_g")):
                        r = l * 24 + w * 8
                        act.dma_start(grow[r:r + 8, :], a[name][l].rearrange("(k p) -> k p", p=128)).then_inc(small_in, 16)
                        n += 1
                    for j in range(3):
                        act.dma_start(lbt[:, l, j:j + 1], a["hgrn_lb_logits"][l, _THIRD[j]:_THIRD[j] + 128].rearrange("(p o) -> p o", o=1)).then_inc(small_in, 16)
                        n += 1
                    for hf in range(2):
                        act.dma_start(gh[64 * hf:64 * hf + 64, l:l + 1], a["hgrn_norm_g"][l].rearrange("(p o) -> p o", o=1)).then_inc(small_in, 16)
                        n += 1
                    act.dma_start(fb[:, l:l + 1], a["fox_f_bias"][l].rearrange("(p o) -> p o", o=1)).then_inc(small_in, 16)
                    n += 1
                act.dma_start(grow[DEPTH * 24:DEPTH * 24 + 8, :], a["norm_final_g"].rearrange("(k p) -> k p", p=128)).then_inc(small_in, 16)
                n += 1
            assert n == SMALL
            act.wait_ge(consts_in, 16)
            act.activation(tmp[0][:, 0:1], K[:, 0:1], ACT.Silu).then_inc(silu_done, 1)
            act.activation(tmp[0][:, 1:2], K[:, 0:1], ACT.Silu).then_inc(silu_done, 1)
            act.wait_ge(lb_diff, 1)
            act.activation(lbt[:, 1, 0:3], lbt[:, 1, 0:3], ACT.Sigmoid).then_inc(lb_sig, 1)
            hi(0, 0)
            with act.Fori(0, DEPTH) as L:
                ch.base, ch.n = L * ACT_STEPS, 0
                norm(L * 3)
                scaled(L * 3)
                ffn(0, L)
                hi(1, L * USES + OFF["win"])
                scaled(L * 3 + 1)
                norm(L * 3 + 1)
                with act.Fori(0, WIN - 1) as i:
                    hi(0, L * USES + OFF["win"] + i + 1)
                    hi(1, L * USES + OFF["win"] + i + 1)
                act.wait_ge(win_used, L * 32 + 36)
                act.activation(p3(T["qf"]), p3(T["qf"]), ACT.Copy, scale=SCALE).then_inc(qf_scaled, 1)
                act.activation(b[1][:, :].rearrange("p (j t) -> p j t", j=3), p3(T["qc"]), ACT.Sigmoid).then_inc(rec_sigmoids_ready, 1)
                act.activation(b[2][:, :].rearrange("p (j t) -> p j t", j=3), p3(T["gc"]), ACT.Sigmoid).then_inc(rec_sigmoids_ready, 1)
                ch.link(act.activation(b[3][:, :].rearrange("p (j t) -> p j t", j=3), p3(T["fc"]), ACT.Sigmoid))
                act.activation(p3(T["fc"]), p3(T["fc"]), ACT.Sigmoid, scale=-1.0).then_inc(rec_sigmoids_ready, 1)
                act.wait_ge(z_ready, L * 2 + 1)
                act.activation(tmp[2][0:BH, :], tmp[1][0:BH, :], ACT.Exp, scale=-1.0).then_inc(z_exp, 1)
                act.wait_ge(z_ready, L * 2 + 2)
                act.activation(tmp[1][0:BH, :], tmp[2][0:BH, :], ACT.Ln).then_inc(z_exp, 1)
                for j in range(3):
                    act.activation(b[0][:, j * NT:(j + 1) * NT], b[3][:, j * NT:(j + 1) * NT], ACT.Ln,
                                   bias=lbcur[:, j:j + 1], scale=lbcur[:, 3 + j:4 + j]).then_inc(rec_logf_ready, 1)
                for n in range(1, 15, 2):
                    g, tt = divmod(n, 3)
                    r = 128 if tt < 2 else NS
                    act.wait_ge(rows_turned, L * 16 + n + 1)
                    act.activation(tok(tt)[0:r, g * 384:(g + 1) * 384], PS[0:r, 4 + n % 4, 0:384], ACT.Copy).then_inc(rows_copied_act, 1)
                for h in range(NH + 2):
                    if h < NH:
                        for t in range(2):
                            act.wait_ge(prompt_max_ready, L * 2 * NH + 2 * h + t + 1)
                            c0, c1 = ((0, 128), (128, 384))[t]
                            act.activation(probs[h % 4][:, c0:c1], probs[h % 4][:, c0:c1], ACT.Exp,
                                           bias=prob_stats[:, 4 * (h % 4) + t:4 * (h % 4) + t + 1],
                                           accum_out=prob_stats[:, 16 + 4 * (h % 4) + t:17 + 4 * (h % 4) + t]).then_inc(prompt_exp_ready, 1)
                    if h >= 2:
                        n = h - 2
                        act.wait_ge(prompt_probs_turned, L * NH + n + 1)
                        if n >= 2:
                            act.wait_ge(prompt_out_ready, L * NH + n - 1)
                        act.activation(probs_t[n % 2], PS[:, 2 + n % 2, 0:384], ACT.Copy).then_inc(prompt_probs_copied, 1)
                for l in range(LEVELS + 1):
                    act.wait_ge(decay_logs_ready, L * 9 + l + 1)
                    h, d3 = 1 << l, b[3][:, :].rearrange("p (j t) -> p j t", j=3)
                    v = d3.rearrange("p j (s c) -> p (j s) c", c=2 * h) if l < 3 else d3[:, :, 0:SEQ].rearrange("p j (s c) -> p j s c", c=2 * h)
                    act.activation(v[..., h:2 * h], v[..., h:2 * h], ACT.Exp).then_inc(decays_ready, 1)
                    act.activation(v[..., 0:h], v[..., 0:h], ACT.Exp, scale=-1.0).then_inc(decays_ready, 1)
                cum3 = b[2][:, :].rearrange("p (j t) -> p j t", j=3)
                act.activation(q_decayed[:, :, :], cum3[:, :, SEQ:NT], ACT.Exp).then_inc(decays_ready, 1)
                act.activation(state_decay[:, :, :], cum3[:, :, SEQ + DS - 1:NT:DS], ACT.Exp).then_inc(decays_ready, 1)
                act.wait_ge(decay_logs_ready, L * 9 + 9)
                act.activation(b[3][:, :], b[3][:, :], ACT.Exp, scale=-1.0).then_inc(decays_ready, 1)
                act.wait_ge(level_products_ready, L * 9 + 9)
                act.activation(a_cross[:, 0:2, :], PS[:, 0, 0:256].rearrange("p (h t) -> p h t", h=2), ACT.Copy).then_inc(cross_products_copied, 1)
                act.activation(a_cross[:, 2:5, :], PS[:, 1, 0:384].rearrange("p (h t) -> p h t", h=3), ACT.Copy).then_inc(cross_products_copied, 1)
                act.wait_ge(rec_out_ready, L + 1)
                act.wait_ge(end_keys_ready, L + 1)
                act.activation(b[4][:, :].rearrange("p (j t) -> p j t", j=3), PS[:, 0:3, 0:NT], ACT.Square).then_inc(rec_squares_ready, 1)
                ch.link(act.activation(junk[:, :], cst("eps"), ACT.Ln))
                act.wait_ge(rec_mean_squares_ready, L + 1)
                ch.link(act.activation(b[3][:, :].rearrange("p (j t) -> p j t", j=3), PS[:, 4:7, 0:NT], ACT.Ln, bias=cst("eps"), scale=1.0 / HD))
                act.activation(b[3][:, :], b[3][:, :], ACT.Exp, scale=-0.5).then_inc(rec_rstd_ready, 1)
                act.wait_ge(decode_ready, L + 1)

                def keys(Q, pg):
                    act.wait_ge(keys_turned, Q * NPG + pg + 5)
                    act.wait_ge(block_scores_done, Q * 4 + pg // 2 + 1)
                    act.activation(key_halves[0][pg // 2 % 2][:, :, 128 * (pg % 2):128 * (pg % 2) + 128].rearrange("p (a j) c -> p a j c", a=2),
                                   PS[:, 2 * (pg % 2):2 * (pg % 2) + 2, 0:384].rearrange("p a (j c) -> p a j c", j=3), ACT.Copy).then_inc(keys_hi_copied, 1)

                def weights(Q):
                    act.wait_ge(exp_bias_ready, Q + 1)
                    for n in range(NBLK + 1):
                        src = PS[0:ROWS, 4 + n // 2, 256 * (n % 2):256 * (n % 2) + 256] if n < NBLK else new_row[:, :]
                        act.activation(weight_rows[:, 256 * n:256 * n + (256 if n < NBLK else NS)], src, ACT.Exp,
                                       bias=exp_bias[:, n:n + 1], accum_out=exp_sums[:, n:n + 1]).then_inc(weights_ready, 1)

                def turned(Q):
                    act.wait_ge(weights_turned, Q * 2 + 2)
                    act.wait_ge(value_sums_ready, Q + 1)
                    act.activation(weight_cols[:, 5:9, :], PS[:, 1, 0:352].rearrange("p (g c) -> p g c", g=4), ACT.Copy).then_inc(weights_copied_act, 1)

                def step(Q, softmax):
                    keys(Q, 0)
                    keys(Q, 1)
                    if softmax:
                        weights(Q - 1)
                    for pg in range(2, NPG):
                        keys(Q, pg)
                    if softmax:
                        turned(Q - 1)

                step(L * DB, False)
                with act.Fori(1, DB) as q:
                    step(L * DB + q, True)
                weights(L * DB + DB - 1)
                turned(L * DB + DB - 1)
                act.wait_ge(block_scores_done, (L * DB + DB) * 4 + 2)
                hi(0, L * USES + OFF["wout"], 6)
                act.wait_ge(outputs_copied, L * 11 * DB + 11 * DB + 4)
                act.wait_ge(rec_out_done, L + 1)
                act.wait_ge(prompt_out_copied, L * 6 + 6)
                for k in range(9):
                    r = slice(64, 128) if k in (5, 8) else slice(0, 128)
                    act.activation(xh[r, k, :], pt(OUT_T[k])[r, :], ACT.Copy).then_inc(out_hi_ready, 1)
                with act.Fori(0, 2) as m:
                    for dp in range(2):
                        hi(1, L * USES + OFF["wout"] + m * 2 + dp, 3)
                        hi(0, L * USES + OFF["wout"] + m * 2 + dp + 1, 6 if dp == 0 else 8)
                norm(L * 3 + 2)
                scaled(L * 3 + 2)
                ffn(1, L)
                assert ch.n == ACT_STEPS, ch.n
            ch.base, ch.n = DEPTH * ACT_STEPS, 0
            norm(DEPTH * 3)

        @block.vector
        def _(dve):
            ch = Chain(dve, vector_step)
            link = ch.link
            V = lambda i: b[i][:, :].rearrange("p (j t) -> p j t", j=3)

            def give(s, n=1):
                dve.sem_inc(s, n)

            def lo(s, use, nk=8):
                dve.wait_ge(hi_done[s], use + 1)
                dve.tensor_tensor(wlo[s][:, 0:nk, :], raw[s][:, 0:nk, :], whi[s][:, 0:nk, :].bitcast(F32), ALU.subtract).then_inc(split_done[s], 1)

            def norm(w):
                dve.wait_ge(rms_ready, w + 1)
                dve.reciprocal(rstd[:, :], rstd[:, :]).then_inc(rstd_ready, 1)

            def low(w, k):
                dve.wait_ge(xh_ready, w * KT_D + k + 1)
                dve.tensor_tensor(xl[:, k, :], tmp[k % 4][:, :], xh[:, k, :].bitcast(F32), ALU.subtract).then_inc(xl_ready, 1)

            def scaled(w, which):
                if which != 1:
                    dve.wait_ge(rstd_ready, w + 1)
                for k in range(KT_D):
                    if k >= 3:
                        low(w, k - 3)
                    if k >= 4:
                        dve.wait_ge(xl_ready, w * KT_D + k - 3)
                    gain = gcur[:, which * 8 + k:which * 8 + k + 1]
                    if which != 1:
                        ins = dve.scalar_tensor_tensor(tmp[k % 4][:, :], xt(k), gain, rstd[:, :], ALU.mult, ALU.mult)
                    else:
                        ins = dve.tensor_scalar(tmp[k % 4][:, :], xt(k), gain, None, ALU.mult)
                    ins.then_inc(xs_ready, 1)
                for k in range(KT_D - 3, KT_D):
                    low(w, k)

            def accumulate(n0, half, at, bank, scale, s, use):
                for j in range(2):
                    tile_done(dve, j, acc_ready, half, s, use)
                    xs = X[:, ds(at + j * NT, NT)]
                    dve.scalar_tensor_tensor(xs, PS[:, bank + j, 0:NT], scale, xs, ALU.mult, ALU.add).then_inc(acc_used, 1)
                    dve.wait_ge(acc_used, n0 + j + 5)
                    link(dve.tensor_tensor(tmp[2][:, :], xs, xs, ALU.mult))
                    link(dve.tensor_tensor(sqsum[:, :], sqsum[:, :], tmp[2][:, :], ALU.add))

            def ffn(f, L):
                u0 = L * USES + OFF[f"ffn{f + 1}"]
                if f == 1:
                    dve.wait_ge(out_tok, L * 14 * 16 + 14 * 16)
                settle(dve)
                with dve.Fori(0, GU) as i:
                    ch.enter(i, 2)
                    lo(1, u0 + i)
                    lo(0, u0 + i + 1)
                    for j in range(2):
                        n = L * 2 * FT + f * FT + i * 2 + j
                        tile_done(dve, j, up_ready, L * 2 * GU + f * GU + i, 1, u0 + i)
                        dve.wait_ge(silu_done, n + 3)
                        dve.tensor_tensor(tmp[2 + j][:, :], tmp[j][:, :], PS[:, 2 + j, 0:NT], ALU.mult).then_inc(up_used, 1)
                        dve.wait_ge(up_used, n + 3)
                        hs, ls = hh[:, ds(i * 2 + j, 1), :], hl[:, ds(i * 2 + j, 1), :]
                        t = tmp[2 + j][:, :].rearrange("p (o t) -> p o t", o=1)
                        link(dve.tensor_scalar(hs, t, 1.0, None, ALU.mult))
                        dve.tensor_tensor(ls, t, hs.bitcast(F32), ALU.subtract).then_inc(h_done, 1)
                    ch.leave(GU, 2)
                link(dve.memset(sqsum[:, :], 0.0))
                settle(dve)
                u0 = L * USES + OFF[f"down{f + 1}"]
                with dve.Fori(0, 2) as m:
                    ch.enter(m, 8)
                    for n in range(6):
                        lo((n + 1) % 2, u0 + m * 3 + (n + 1) // 2)
                        if n % 3 == 2:
                            dp = n // 3
                            accumulate(L * 24 + f * 16 + m * 4 + 2 * dp, L * 12 + f * 8 + m * 2 + dp,
                                       m * (4 * NT) + dp * 2 * NT, 4 + 2 * dp, 0.5, n % 2, u0 + m * 3 + n // 2)
                    ch.leave(2, 8)
                give(sqsum_ready)

            for s, n in ((w_free[0], 1), (w_free[1], 1), (up_used, 2), (acc_used, 4), (outputs_copied, 4), (value_sums_ready, 1),
                         (win_used, 4), (block_scores_done, 2), (keys_hi_copied, 2), (keys_lo_copied, 2),
                         (keys_turned, 4), (values_used, NPG), (outputs_turned, 1)):
                give(s, n)
            link(dve.memset(X[:, KT_D * NT:], 0.0))
            link(dve.memset(P[:, 32 * NT:], 0.0))
            link(dve.memset(ncn[:, :], 0.0))
            dve.wait_ge(page_column_in, 16)
            for l in range(DEPTH):
                dve.tensor_scalar(value_pages[0:DB * NPG, 1, 2 + l:3 + l].bitcast(I32), value_pages[0:DB * NPG, 1, 0:1].bitcast(I32),
                                  float(l * NPOOL), None, ALU.add).then_inc(page_rows_ready, 1)
            for n in range(6):
                tt, hf = divmod(n, 2)
                r = 128 if tt < 2 else NS
                dve.wait_ge(x_turned, n + 1)
                link(dve.tensor_copy(
                    X[:, 4 * hf * NT:(4 * hf + 4) * NT].rearrange("p (k t) -> p k t", k=4)[:, :, tt * 128:tt * 128 + r],
                    PS[:, n, :].rearrange("p (k t) -> p k t", k=4)[:, :, 0:r]))
            give(split_done[0]); give(split_done[1])
            dve.wait_ge(small_in, 16 * SMALL)
            dve.tensor_tensor(lbt[:, 1, 0:3], lbt[:, 1, 0:3], lbt[:, 0, 0:3], ALU.subtract).then_inc(lb_diff, 1)
            dve.wait_ge(lb_sig, 1)
            link(dve.memset(lbt[:, 0, 0:3], 0.0))
            link(dve.tensor_scalar(lbt[:, :, 3:6], lbt[:, :, 0:3], -1.0, 1.0, ALU.mult, ALU.add))
            dve.wait_ge(tables_in, 16)
            dve.wait_ge(gains_turned, 1)
            link(dve.tensor_copy(gains[:, :], PS[:, 6, 0:DEPTH * 24 + 8]))
            link(dve.memset(sqsum[:, :], 0.0))
            for k in range(KT_D):
                link(dve.tensor_tensor(tmp[2][:, :], xt(k), xt(k), ALU.mult))
                link(dve.tensor_tensor(sqsum[:, :], sqsum[:, :], tmp[2][:, :], ALU.add))
            give(sqsum_ready)
            G = DB * NPG
            lft, later = tok(0)[:, 0:640], tok(1)[:, 0:640]
            l4 = lambda x: x.rearrange("p (l h b g) -> p (l h b) g", l=DEPTH, h=BH, b=DB)
            for l in range(DEPTH):
                dve.wait_ge(past_logf_turned, l + 1)
                link(dve.tensor_copy(lft[:, l * 320:(l + 1) * 320], PS[:, l, 0:320]))
            link(dve.memset(later[:, :], 0.0))
            for pg in range(NPG - 2, -1, -1):
                link(dve.tensor_tensor(l4(later)[:, :, pg:pg + 1], l4(later)[:, :, pg + 1:pg + 2], l4(lft)[:, :, pg + 1:pg + 2], ALU.add))
            give(later_pages_ready)
            for l in range(DEPTH):
                dve.wait_ge(past_sums_ready, l + 1)
                link(dve.tensor_copy(tok(2)[:, l * 320:(l + 1) * 320], PS[:, 2 + l, 0:320]))
            give(past_sums_copied)
            dve.wait_ge(past_sums_turned, 1)
            bh_, bl_ = (x[:, :].rearrange("p (a c) -> p a c", a=2) for x in brow)
            link(dve.tensor_scalar(bh_, PS[0:DEPTH * BH * DB, 0:2, :], 1.0, None, ALU.mult))
            link(dve.tensor_tensor(bl_, PS[0:DEPTH * BH * DB, 0:2, :], bh_.bitcast(F32), ALU.subtract))
            lo(0, 0)
            start_steps = ch.n
            with dve.Fori(0, DEPTH) as L:
                ch.base, ch.n = L * DVE_STEPS + start_steps, 0
                link(dve.tensor_scalar(gcur[:, :], gains[:, ds(L * 24, 24)], 1.0, None, ALU.mult))
                link(dve.tensor_scalar(lbcur[:, :].rearrange("p (o c) -> p o c", o=1), lbt[:, ds(L, 1), :], 1.0, None, ALU.mult))
                link(dve.tensor_scalar(ghcur[:, :], gh[:, ds(L, 1)], 1.0, None, ALU.mult))
                link(dve.tensor_scalar(fbcur[:, :], fb[:, ds(L, 1)], 1.0, None, ALU.mult))
                norm(L * 3)
                scaled(L * 3, 0)
                ffn(0, L)
                scaled(L * 3 + 1, 1)
                lo(1, L * USES + OFF["win"])
                norm(L * 3 + 1)
                dve.wait_ge(rstd_ready, L * 3 + 2)
                settle(dve)

                def projected(i, more):
                    u = L * USES + OFF["win"] + i
                    for c in range(2):
                        for j in range(2):
                            n = 2 * c + j
                            tile_done(dve, j, win_ready, L * 16 + 2 * i + c, c, u)
                            dve.tensor_tensor(P[:, ds(i * (4 * NT) + n * NT, NT)], PS[:, n, 0:NT], rstd[:, :], ALU.mult).then_inc(win_used, 1)
                        if more:
                            lo(c, u + 1)

                with dve.Fori(0, WIN - 1) as i:
                    projected(i, True)
                projected(WIN - 1, False)
                dve.wait_ge(win_used, L * 32 + 36)
                for n in range(6):
                    sc = SCALE if n < 3 else 1.0
                    dve.wait_ge(rot_ready, L * 6 + n + 1)
                    t1, t2 = tmp[2 * (n % 2)], tmp[2 * (n % 2) + 1]
                    link(dve.scalar_tensor_tensor(t1[:, :], pt(n), sc, cst("cos"), ALU.mult, ALU.mult))
                    link(dve.scalar_tensor_tensor(t2[:, :], PS[:, 4 + n % 2, 0:NT], sc, cst("sin"), ALU.mult, ALU.mult))
                    dve.tensor_tensor(pt(n), t1[:, :], t2[:, :], ALU.add).then_inc(roped, 1)
                z, e1, e2 = (tmp[j][0:BH, :] for j in range(3))
                link(dve.tensor_scalar(z, pt(T["ff"])[0:BH, :], fbcur[:, 0:1], None, ALU.add))
                dve.scalar_tensor_tensor(e1, z, -1.0, z, ALU.mult, ALU.max).then_inc(z_ready, 1)
                dve.wait_ge(z_exp, L * 2 + 1)
                dve.tensor_scalar(e2, e2, 1.0, None, ALU.add).then_inc(z_ready, 1)
                dve.wait_ge(z_exp, L * 2 + 2)
                link(dve.scalar_tensor_tensor(pt(T["ff"])[0:BH, :], z, 0.0, e1, ALU.min, ALU.subtract))
                dve.tensor_tensor_scan(ncn[:, 0:NT], cst("reset")[0:BH, :], pt(T["ff"])[0:BH, :], 0.0, ALU.mult, ALU.subtract).then_inc(lf_ready, 1)
                for n in range(0, 15, 2):
                    g, tt = divmod(n, 3)
                    r = 128 if tt < 2 else NS
                    dve.wait_ge(rows_turned, L * 16 + n + 1)
                    dve.tensor_copy(tok(tt)[0:r, g * 384:(g + 1) * 384], PS[0:r, 4 + n % 4, 0:384]).then_inc(rows_copied_dve, 1)
                dve.wait_ge(rows_turned, L * 16 + 16)
                link(dve.tensor_copy(tokf[:, :, :], PS[:, 0, 0:24].rearrange("p (t c) -> p t c", t=3)[:, :, 0:BH]))
                dve.tensor_copy(tokn[:, :], PS[0:NS, 0, 24:24 + BH]).then_inc(rows_copied_dve, 1)
                q3, g3, k3 = p3(T["qc"]), p3(T["gc"]), p3(T["fc"])
                for h in range(NH + 4):
                    if h == 2:
                        dve.wait_ge(rec_sigmoids_ready, L * 3 + 3)
                        dve.wait_ge(rec_logf_ready, L * 3 + 3)
                        link(dve.tensor_tensor(q3, q3, V(1), ALU.mult))
                    elif h == 3:
                        link(dve.tensor_tensor(g3, g3, V(2), ALU.mult))
                    elif h in (4, 5, 6):
                        t = pt(T["fc"] + h - 4)
                        ch.mark(dve.tensor_scalar(t, t, lbcur[:, h - 1:h], None, ALU.mult))
                        ch.mark(dve.tensor_tensor_scan(V(2)[:, h - 4, :], cst("reset"), V(0)[:, h - 4, :], 0.0, ALU.mult, ALU.add))
                    elif h == 7:
                        ch.mark(dve.memset(a_blocks[:, :, :], 0.0))
                        ch.mark(dve.memset(a_samples[:, :, :], 0.0))
                        ch.catch_up()
                        give(rec_qk_ready)
                    if h < NH:
                        c = probs[h % 4]
                        dve.wait_ge(prompt_scores_ready, L * NH + h + 1)
                        if h >= 4:
                            dve.wait_ge(prompt_probs_turned, L * NH + h - 3)
                        dve.tensor_tensor(c, PS[:, h % 2, 0:384], cst("causal"), ALU.add).then_inc(prompt_scores_read, 1)
                        dve.wait_ge(prompt_scores_read, L * NH + h + 1)
                        x = prob_stats[:, 4 * (h % 4):4 * (h % 4) + 2]
                        dve.tensor_reduce(x[:, 0:1], c[:, 0:128], AX.X, ALU.max, negate=True).then_inc(prompt_max_ready, 1)
                        dve.tensor_reduce(x[:, 1:2], c[:, 128:384], AX.X, ALU.max, negate=True).then_inc(prompt_max_ready, 1)
                    if 1 <= h <= NH:
                        n = h - 1
                        c = probs[n % 4]
                        x = prob_stats[:, 16 + 4 * (n % 4):16 + 4 * (n % 4) + 2]
                        dve.wait_ge(prompt_exp_ready, L * 2 * NH + 2 * n + 2)
                        link(dve.reciprocal(x, x))
                        dve.tensor_scalar(c[:, 0:128], c[:, 0:128], x[:, 0:1], None, ALU.mult).then_inc(prompt_probs_ready, 1)
                        dve.tensor_scalar(c[:, 128:384], c[:, 128:384], x[:, 1:2], None, ALU.mult).then_inc(prompt_probs_ready, 1)
                    if h >= 4 and (h - 4) in (1, 3, 5, 7, 9, 10):
                        pr = (1, 3, 5, 7, 9, 10).index(h - 4)
                        r = slice(0, 128) if pr < 5 else slice(64, 128)
                        dve.wait_ge(prompt_out_ready, L * NH + h - 3)
                        dve.tensor_copy(pt(OUT_T[pr])[r, 0:SEQ], PS[r, 4 + pr % 2, 0:SEQ]).then_inc(prompt_out_copied, 1)
                lm = cst("lmask").rearrange("p (l t) -> p l t", l=LEVELS + 1).bitcast(I32)

                def take(n, mask):
                    dve.wait_ge(level_products_ready, L * 9 + n + 1)
                    settle(dve)
                    bk = 4 * (n % 2)
                    for g in range(3):
                        nh = 2 if g < 2 else 1
                        ch.mark(dve.copy_predicated(
                            a_blocks[:, 2 * g:2 * g + nh, :].rearrange("p h (u t) -> p (h u) t", u=2),
                            lm[:, mask:mask + 1, :].to_broadcast([128, 2 * nh, 128]),
                            PS[:, bk + g, 0:256 * nh].rearrange("p (h t) -> p h t", t=128)))
                    if mask == LEVELS or mask < 3:
                        for a0, a1, g, c in ((0, 2, 3, 0), (2, 5, 2, 256)):
                            ch.mark(dve.copy_predicated(
                                a_samples[:, a0:a1, :], lm[0:NS, mask:mask + 1, 0:NS].to_broadcast([NS, a1 - a0, NS]),
                                PS[0:NS, bk + g, c:c + (a1 - a0) * NS].rearrange("p (h t) -> p h t", t=NS)))
                    ch.catch_up()
                    give(level_products_taken)

                for l in range(LEVELS + 1):
                    h = 1 << l
                    if l < 3:
                        seg = lambda x: x.rearrange("p j (s c) -> p (j s) c", c=2 * h)
                        every = lambda x: x
                    else:
                        seg = lambda x: x.rearrange("p j (s c) -> p j s c", c=2 * h)
                        every = lambda x: x[:, :, 0:SEQ]
                    dv, cv, qv, kv, gv = (seg(every(x)) for x in (V(3), V(2), q3, k3, V(4 if l % 2 == 0 else 0)))
                    dve.tensor_tensor(dv, cv, cv[..., h - 1:h].to_broadcast(list(dv.shape)), ALU.subtract).then_inc(decay_logs_ready, 1)
                    dve.wait_ge(decays_ready, L * 19 + 2 * l + 2)
                    ch.mark(dve.tensor_tensor(gv[..., h:2 * h], dv[..., h:2 * h], qv[..., h:2 * h], ALU.mult))
                    ch.mark(dve.tensor_tensor(gv[..., 0:h], dv[..., 0:h], kv[..., 0:h], ALU.mult))
                    ch.catch_up()
                    give(level_factors_ready)
                    if l >= 1:
                        take(l, l - 1)
                    else:
                        take(0, LEVELS)
                link(dve.tensor_tensor(V(3)[:, :, 0:SEQ], V(2)[:, :, 0:SEQ], V(2)[:, :, SEQ - 1:SEQ].to_broadcast([128, 3, SEQ]), ALU.subtract))
                for j in range(3):
                    v = lambda x: x[:, j, SEQ:NT].rearrange("p (b t) -> p b t", t=DS)
                    link(dve.tensor_tensor(v(V(3)), v(V(2)), v(V(2))[:, :, DS - 1:DS].to_broadcast([128, DB, DS]), ALU.subtract))
                give(decay_logs_ready)
                dve.wait_ge(decays_ready, L * 19 + 17)
                link(dve.tensor_tensor(q_decayed[:, :, :], q_decayed[:, :, :], q3[:, :, SEQ:NT], ALU.mult))
                dve.wait_ge(decays_ready, L * 19 + 19)
                link(dve.tensor_tensor(V(1), V(3), k3, ALU.mult))
                give(end_keys_ready)
                for tt in range(3):
                    r = 128 if tt < 2 else NS
                    dve.wait_ge(end_keys_turned, L * 3 + tt + 1)
                    dve.tensor_copy(end_keys_t[0:r, tt, :], PS[0:r, 4 + tt, 0:384]).then_inc(end_keys_copied, 1)
                link(dve.memset(qb[:, :, :, :], 0.0))
                dve.wait_ge(qf_scaled, L + 1)
                for t0, p0, n, hf in ((T["qa"], 0, 3, 0), (T["qa"], 0, 3, 1), (T["qf"], 3, 2, 0), (T["qf"], 3, 3, 1)):
                    r = slice(64 * hf, 64 * hf + 64)
                    src = P[r, t0 * NT:(t0 + n) * NT].rearrange("p (j t) -> p j t", j=n)[:, :, SEQ:NT].rearrange("p j (b t) -> p j b t", t=DS)
                    ch.mark(dve.tensor_copy(qb[r, p0:p0 + n, :, 8 * hf:8 * hf + 8], src))
                nm = cst("newmask")[0:NS, :].rearrange("p (b o t) -> p b o t", b=DB, o=1)
                ch.mark(dve.tensor_copy(newb[:, :, 0:8 * AH].rearrange("p b (h t) -> p b h t", t=DS), nm.to_broadcast([NS, DB, AH, DS])))
                ch.mark(dve.tensor_tensor(newb[:, :, 8 * AH:].rearrange("p b (h t) -> p b h t", t=DS), nm.to_broadcast([NS, DB, BH, DS]),
                                          tokn[:, :].rearrange("p (a h o) -> p a h o", a=1, o=1).to_broadcast([NS, DB, BH, DS]), ALU.add))
                ch.catch_up()
                give(decode_queries_ready)
                vx = [b[0][0:NS, 0:512], P[0:NS, T["qc"] * NT:T["qc"] * NT + 512]]
                dve.wait_ge(rec_out_ready, L + 1)
                for e in range(CH):
                    if e >= 2:
                        dve.wait_ge(state_products_ready, L * CH + e - 1)
                    dve.tensor_tensor(vx[e % 2].rearrange("p (b e) -> p b e", b=DB),
                                      toks[0:NS, 4 * 384 + HCOL[e]:4 * 384 + HCOL[e] + 64].rearrange("p (o e) -> p o e", o=1).to_broadcast([NS, DB, 64]),
                                      cst("seqof")[0:NS, :].rearrange("p (b o) -> p b o", o=1).to_broadcast([NS, DB, 64]),
                                      ALU.mult).then_inc(spread_values_ready, 1)
                dve.wait_ge(prompt_state_ready, L + 1)
                link(dve.tensor_copy(prompt_state[:, 0:2, :], PS[:, 7, 0:128].rearrange("p (j e) -> p j e", j=2)))
                dve.tensor_copy(prompt_state[64:128, 2, :], PS[64:128, 7, 128:192]).then_inc(prompt_state_copied, 1)
                dve.wait_ge(state_products_ready, L * CH + CH)
                for j in range(3):
                    r = slice(0, 128) if j < 2 else slice(64, 128)
                    n = 128 if j < 2 else 64
                    link(dve.tensor_tensor(states[r, j, :, :], states[r, j, :, :],
                                           state_decay[r, j, :].rearrange("p (b o) -> p b o", o=1).to_broadcast([n, DB, 64]), ALU.mult))
                    dve.tensor_tensor(states[r, j, :, :], states[r, j, :, :], PS[r, 4 + j, :].rearrange("p (b e) -> p b e", b=DB), ALU.add).then_inc(sample_states_done, 1)
                dve.wait_ge(rec_rstd_ready, L + 1)
                for j in range(3):
                    link(dve.scalar_tensor_tensor(V(4)[:, j, :], PS[:, j, 0:NT], ghcur[:, 0:1], V(3)[:, j, :], ALU.mult, ALU.mult))
                dve.tensor_tensor(p3(T["ic"]), V(4), g3, ALU.mult).then_inc(rec_out_done, 1)
                qzd, qzl = (z[:, :, :].rearrange("p j c -> p (j c)")[:, 0:5 * (ROWS + 16)].rearrange("p (j c) -> p j c", j=5)[:, :, 0:16] for z in qz)
                dve.wait_ge(rec_out_done, L + 1)
                dve.wait_ge(new_scores_ready, L + 1)
                nbv = newb[:, :, 0:64].rearrange("p b (j c) -> p j b c", j=4)
                link(dve.tensor_tensor(nbv, nbv, PS[0:NS, 4, :].rearrange("p (j b c) -> p j b c", j=4, b=DB), ALU.add))
                for c0, lo_ in ((64, 0), (80, 8)):
                    nbv = newb[:, :, c0:c0 + 16 - lo_]
                    link(dve.tensor_tensor(nbv, nbv, PS[0:NS, 5, 8 * (c0 - 64):8 * (c0 - 64) + 128].rearrange("p (b c) -> p b c", b=DB)[:, :, lo_:16], ALU.add))
                give(new_scores_masked)
                dve.wait_ge(out_st, L * 96 + 96)
                dve.wait_ge(out_tok, L * 14 * 16 + 14 * 16)
                ch.mark(dve.memset(gate_bias[:, :], 0.0))
                ch.mark(dve.memset(weight_rows[:, 1088:1152], 0.0))
                for z in qz:
                    ch.mark(dve.tensor_scalar(z[:, :, :].rearrange("p j c -> p (j c)"), K[:, 0:6 * ROWS], 0.0, None, ALU.mult))
                ch.catch_up()
                dve.wait_ge(new_scores_turned, L + 1)
                link(dve.tensor_copy(new_row_all[:, :, :], PS[0:ROWS, 6, :].rearrange("p (b c) -> p b c", b=DB)))
                give(decode_ready)

                def queries(Q, q):
                    dve.wait_ge(block_scores_done, Q * 4 + 2)
                    q5 = qb[:, 0:5, ds(q, 1), :].rearrange("p j o c -> p j (o c)")
                    last5, z5 = qb[:, 5, ds(q, 1), 8:16], [z[:, 5, 80:88].rearrange("p (o c) -> p o c", o=1) for z in qz]
                    ch.mark(dve.tensor_scalar(qzd, q5, 1.0, None, ALU.mult))
                    ch.mark(dve.tensor_scalar(z5[0], last5, 1.0, None, ALU.mult))
                    ch.catch_up()
                    ch.mark(dve.tensor_tensor(qzl, q5, qzd.bitcast(F32), ALU.subtract))
                    ch.mark(dve.tensor_tensor(z5[1], last5, z5[0].bitcast(F32), ALU.subtract))
                    ch.mark(dve.tensor_tensor(sel[:, :], cst("hsel")[0:DEPTH * BH * DB, :],
                                              cst("rowsel")[0:DEPTH * BH * DB, ds(Q, 1)].to_broadcast([DEPTH * BH * DB, ROWS]), ALU.mult))
                    ch.catch_up()
                    give(seq_queries_ready)

                def keys(Q, pg):
                    dve.wait_ge(keys_hi_copied, Q * NPG + pg + 3)
                    kh, kl = (x[pg // 2 % 2][:, :, 128 * (pg % 2):128 * (pg % 2) + 128].rearrange("p (a j) c -> p a j c", a=2) for x in key_halves)
                    dve.tensor_tensor(kl, PS[:, 2 * (pg % 2):2 * (pg % 2) + 2, 0:384].rearrange("p a (j c) -> p a j c", j=3),
                                      kh.bitcast(F32), ALU.subtract).then_inc(keys_lo_copied, 1)

                def block_sums(Q, q):
                    dve.wait_ge(block_scores_done, Q * 4 + 6)
                    rows = PS[0:ROWS, 4:6, :].rearrange("p a (n c) -> p (a n) c", n=2)
                    ch.mark(dve.tensor_reduce(gate_sums[:, 0, :], rows[0:48], AX.X, ALU.add))
                    ch.mark(dve.tensor_reduce(block_max[:, 0:NBLK], rows, AX.X, ALU.max))
                    link(dve.tensor_scalar(new_row[:, :].rearrange("p (o c) -> p o c", o=1), new_row_all[:, ds(q, 1), :], 1.0, None, ALU.mult))
                    link(dve.tensor_reduce(block_max[:, NBLK:NBLK + 1], new_row[:, :], AX.X, ALU.max))

                def gates(Q):
                    link(dve.tensor_reduce(gate_sums[:, 1, 0:1], gate_sums[:, 0, :], AX.X, ALU.min))
                    link(dve.scalar_tensor_tensor(gate_sums[:, 2, :], gate_sums[:, 0, :], gate_sums[:, 1, 0:1], cst("place")[0:48, :], ALU.is_equal, ALU.mult))
                    link(dve.tensor_reduce(gate_sums[:, 3, 0:1], gate_sums[:, 2, :], AX.X, ALU.max))
                    link(dve.tensor_scalar(gate_bias[0:48, 0:NBLK], gate_sums[:, 2, :], gate_sums[:, 3, 0:1], NEG, ALU.is_equal, ALU.mult))
                    link(dve.tensor_tensor(block_max[:, :], block_max[:, :], gate_bias[:, :], ALU.add))
                    link(dve.tensor_reduce(row_stats[:, 0:1], block_max[:, :], AX.X, ALU.max, negate=True))
                    dve.tensor_scalar(exp_bias[:, :], gate_bias[:, :], row_stats[:, 0:1], None, ALU.add).then_inc(exp_bias_ready, 1)

                def norms(Q):
                    dve.wait_ge(weights_ready, Q * 5 + 5)
                    link(dve.tensor_reduce(row_stats[:, 1:2], exp_sums[:, :], AX.X, ALU.add))
                    link(dve.reciprocal(row_stats[:, 1:2], row_stats[:, 1:2]))

                def turned(Q):
                    dve.wait_ge(weights_turned, Q * 2 + 1)
                    dve.wait_ge(value_sums_ready, Q + 1)
                    dve.tensor_copy(weight_cols[:, 0:5, :], PS[:, 0, 0:440].rearrange("p (g c) -> p g c", g=5)).then_inc(weights_copied_dve, 1)

                def scale_outputs(Q):
                    dve.wait_ge(value_sums_ready, Q + 2)
                    dve.wait_ge(outputs_turned, Q + 1)
                    ch.mark(dve.tensor_scalar(out_rows[:, 0:AW], PS[0:ROWS, 6, 0:AW], row_stats[:, 1:2], None, ALU.mult))
                    ch.mark(dve.tensor_scalar(out_rows[:, AW:AW + BW], PS[0:ROWS, 7, 0:BW], row_stats[:, 1:2], None, ALU.mult))
                    ch.catch_up()
                    give(outputs_scaled)

                def outputs(Q, q):
                    dve.wait_ge(outputs_turned, Q + 2)
                    for r0, t0, p0, n in ((0, T["va"], 0, 3), (64, T["va"], 0, 3), (0, T["vf"], 3, 2), (64, T["vf"], 3, 2), (64, T["vf"] + 2, 5, 1)):
                        r = slice(r0, r0 + 64)
                        if p0 < 5:
                            src = [PS[r, 6, 104 * (p0 + k) + r0 // 8:104 * (p0 + k) + r0 // 8 + 8] for k in range(n)]
                        else:
                            src = [PS[r, 7, 80:88]]
                        for k in range(n):
                            dst = P[r, ds(q * DS + (t0 + k) * NT + SEQ, DS)]
                            dve.tensor_scalar(dst, src[k], 1.0, None, ALU.mult).then_inc(outputs_copied, 1)

                def step(Q, q, softmax, products):
                    queries(Q, q)
                    if softmax:
                        block_sums(Q - 1, q - 1)
                        gates(Q - 1)
                    keys(Q, 0)
                    keys(Q, 1)
                    if products:
                        scale_outputs(Q - 2)
                    keys(Q, 2)
                    keys(Q, 3)
                    if products:
                        outputs(Q - 2, q - 2)
                    if softmax:
                        norms(Q - 1)
                    for pg in range(4, NPG):
                        keys(Q, pg)
                    if softmax:
                        turned(Q - 1)

                step(L * DB, 0, False, False)
                step(L * DB + 1, 1, True, False)
                settle(dve)
                with dve.Fori(2, DB) as q:
                    ch.enter(q - 2, DECODE_STEPS)
                    step(L * DB + q, q, True, True)
                    ch.leave(DB - 2, DECODE_STEPS)
                Q = L * DB + DB - 1
                block_sums(Q, DB - 1)
                gates(Q)
                scale_outputs(Q - 1)
                outputs(Q - 1, DB - 2)
                norms(Q)
                turned(Q)
                scale_outputs(Q)
                outputs(Q, DB - 1)
                lo(0, L * USES + OFF["wout"], 6)
                for k in range(9):
                    r = slice(64, 128) if k in (5, 8) else slice(0, 128)
                    dve.wait_ge(out_hi_ready, L * 9 + k + 1)
                    dve.tensor_tensor(xl[r, k, :], pt(OUT_T[k])[r, :], xh[r, k, :].bitcast(F32), ALU.subtract).then_inc(out_lo_ready, 1)
                link(dve.memset(sqsum[:, :], 0.0))
                settle(dve)
                with dve.Fori(0, 2) as m:
                    ch.enter(m, 8)
                    for dp in range(2):
                        u = L * USES + OFF["wout"] + m * 2 + dp
                        lo(1, u, 3)
                        lo(0, u + 1, 6 if dp == 0 else 8)
                        accumulate(L * 24 + 8 + m * 4 + 2 * dp, L * 12 + 4 + m * 2 + dp, m * (4 * NT) + dp * 2 * NT, 4 + 2 * dp, 1.0, 1, u)
                    ch.leave(2, 8)
                give(sqsum_ready)
                norm(L * 3 + 2)
                scaled(L * 3 + 2, 2)
                ffn(1, L)
                assert ch.n == DVE_STEPS, ch.n
            ch.base, ch.n = DEPTH * DVE_STEPS + start_steps, 0
            norm(DEPTH * 3)
            dve.wait_ge(rstd_ready, DEPTH * 3 + 1)
            for k in range(KT_D):
                ins = dve.scalar_tensor_tensor(xt(k), xt(k), gains[:, DEPTH * 24 + k:DEPTH * 24 + k + 1], rstd[:, :], ALU.mult, ALU.mult)
                ins.then_inc(xs_ready, 1)
            for n in range(6):
                tt, hf = divmod(n, 2)
                r = 128 if tt < 2 else NS
                dve.wait_ge(y_turned, n + 1)
                dve.tensor_copy(P[0:r, tt * 1024 + hf * 512:tt * 1024 + hf * 512 + 512], PS[0:r, n, :]).then_inc(y_copied, 1)

        @block.tensor
        def _(te):
            ident = cst("ident")

            def dense(out, wslot, cols, rhs, ktiles, start, stop, x_ready=None):
                hs, ls = rhs
                last = None
                for n, (kt, at, r) in enumerate(ktiles):
                    if x_ready is not None:
                        te.wait_ge(x_ready[0], x_ready[1] + n + 1)
                    for m, (w, x) in enumerate(((whi, hs), (wlo, hs), (whi, ls))):
                        last = te.matmul(out, w[wslot][r, kt, cols], x[r, at, :],
                                         start=start and n == 0 and m == 0, stop=stop and n == len(ktiles) - 1 and m == 2)
                return last

            ALLR = slice(0, 128)

            def norm(w):
                te.wait_ge(sqsum_ready, w + 1)
                te.matmul(PS[:, 7, 0:NT], cst("ones"), sqsum[:, :], start=True, stop=True).then_inc(ms_ready, 1)

            def chunk(s, use):
                te.wait_ge(split_done[s], use + 2)

            def ffn(f, L, w):
                settle(te)
                u0 = L * USES + OFF[f"ffn{f + 1}"]
                kts = [(k, k, ALLR) for k in range(KT_D)]
                with te.Fori(0, GU) as i:
                    n0 = L * 2 * FT + f * FT + i * 2
                    for s in range(2):
                        chunk(s, u0 + i)
                        for j in range(2):
                            te.wait_ge(silu_done if s == 0 else up_used, n0 + j + 1)
                            dense(PS[:, 2 * s + j, 0:NT], s, slice(128 * j, 128 * j + 128), (xh, xl), kts, True, True,
                                  (xl_ready, w * KT_D) if s == 0 and j == 0 else None).then_inc(w_free[s] if j else (gate_ready, up_ready)[s], 1)
                settle(te)
                u0 = L * USES + OFF[f"down{f + 1}"]
                with te.Fori(0, 2) as m:
                    for n in range(6):
                        dp, kk = divmod(n, 3)
                        if n < 3:
                            te.wait_ge(h_done, L * 2 * FT + f * FT + min(8 * kk + 8, FT))
                        chunk(n % 2, u0 + m * 3 + n // 2)
                        kts = [(k, kk * 8 + k, ALLR) for k in range(8 if kk < 2 else FT - 16)]
                        for j in range(2):
                            a0 = L * 24 + f * 16 + m * 4 + 2 * dp + j
                            if kk == 0:
                                te.wait_ge(acc_used, a0 + 1)
                            last = dense(PS[:, 4 + 2 * dp + j, 0:NT], n % 2, slice(128 * j, 128 * j + 128), (hh, hl), kts, kk == 0, kk == 2)
                            if j == 1:
                                last.then_inc(w_free[n % 2], 1)
                            elif kk == 2:
                                last.then_inc(acc_ready, 1)

            te.wait_ge(consts_in, 16)
            te.wait_ge(x_in, 48)
            xtok = [raw[0].rearrange("p a b -> p (a b)")[:, 0:1024], raw[0].rearrange("p a b -> p (a b)")[:, 1024:2048],
                    raw[1].rearrange("p a b -> p (a b)")[:, 0:1024]]
            for n in range(6):
                tt, hf = divmod(n, 2)
                r = 128 if tt < 2 else NS
                for k in range(4):
                    last = te.transpose(PS[:, n, 128 * k:128 * k + r], xtok[tt][0:r, (4 * hf + k) * 128:(4 * hf + k + 1) * 128], ident[0:r, 0:r])
                last.then_inc(x_turned, 1)
            te.wait_ge(small_in, 16 * SMALL)
            n = DEPTH * 24 + 8
            te.transpose(PS[:, 6, 0:n], value_pages[0:n, 0, 0:128], ident[0:n, 0:n]).then_inc(gains_turned, 1)
            te.wait_ge(past_logf_in, 32)
            te.wait_ge(sqsum_ready, 1)
            G = DB * NPG
            for l in range(DEPTH):
                for h in range(BH):
                    last = te.transpose(PS[:, l, h * G:(h + 1) * G], value_pages[0:G, 2 + l, 0:PAGE * BH].rearrange("p (k h) -> p h k", h=BH)[:, h, :], ident[0:G, 0:G])
                last.then_inc(past_logf_turned, 1)
            te.wait_ge(tables_in, 16)
            te.wait_ge(later_pages_ready, 1)
            for l in range(DEPTH):
                te.matmul(PS[:, 2 + l, 0:320], cst("later"), tok(0)[:, l * 320:(l + 1) * 320], start=True, stop=False)
                te.matmul(PS[:, 2 + l, 0:320], cst("ones"), tok(1)[:, l * 320:(l + 1) * 320], start=False, stop=True).then_inc(past_sums_ready, 1)
            te.wait_ge(past_sums_copied, 1)
            n = DEPTH * BH * DB
            for g in range(NPG):
                last = te.transpose(PS[0:n, g // 4, 128 * (g % 4):128 * (g % 4) + 128],
                                    tok(2)[:, 0:640].rearrange("p (r g) -> p g r", g=NPG)[:, g, :], ident)
            last.then_inc(past_sums_turned, 1)
            with te.Fori(0, DEPTH) as L:
                norm(L * 3)
                ffn(0, L, L * 3)
                norm(L * 3 + 1)
                with te.Fori(0, WIN) as i:
                    for s in range(2):
                        chunk(s, L * USES + OFF["win"] + i)
                        for j in range(2):
                            te.wait_ge(win_used, L * 32 + i * 4 + 2 * s + j + 1)
                            dense(PS[:, 2 * s + j, 0:NT], s, slice(128 * j, 128 * j + 128), (xh, xl),
                                  [(k, k, ALLR) for k in range(KT_D)], True, True,
                                  (xl_ready, (L * 3 + 1) * KT_D) if s == 0 and j == 0 else None).then_inc(w_free[s] if j else win_ready, 1)
                te.wait_ge(win_used, L * 32 + 36)
                for n in range(6):
                    if n >= 2:
                        te.wait_ge(roped, L * 6 + n - 1)
                    te.matmul(PS[:, 4 + n % 2, 0:NT], cst("perm"), pt(n), start=True, stop=True).then_inc(rot_ready, 1)
                te.wait_ge(roped, L * 6 + 6)
                for n in range(15):
                    g, tt = divmod(n, 3)
                    t0 = T[("ka", "va", "kf", "vf", "ic")[g]]
                    if n >= 4:
                        te.wait_ge(rows_copied_act if n % 2 else rows_copied_dve, L * (7 if n % 2 else 9) + n // 2 - 1)
                    for j in range(3):
                        at = (t0 + j) * NT + tt * 128
                        last = te.transpose(PS[:, 4 + n % 4, 128 * j:128 * j + 128], P[:, at:at + 128], ident)
                    last.then_inc(rows_turned, 1)
                te.wait_ge(lf_ready, L + 1)
                settle(te)
                for tt in range(3):
                    at = T["ff"] * NT + tt * 128
                    te.transpose(PS[:, 0, 8 * tt:8 * tt + BH], P[0:BH, at:at + 128], ident[0:BH, 0:BH])
                te.transpose(PS[:, 0, 24:24 + BH], ncn[:, SEQ:SEQ + 128], ident[0:BH, 0:BH]).then_inc(rows_turned, 1)
                te.wait_ge(rows_copied_dve, L * 9 + 9)
                te.wait_ge(rows_copied_act, L * 7 + 7)
                te.wait_ge(qf_scaled, L + 1)
                for h in range(NH + 3):
                    if h < NH:
                        moba = h < AH
                        j, hf = (h // 2, h % 2) if moba else HEADS5[h - AH]
                        r = slice(64 * hf, 64 * hf + 64)
                        qt, kt = pt((T["qa"] if moba else T["qf"]) + j), pt((T["ka"] if moba else T["kf"]) + j)
                        if h >= 2:
                            te.wait_ge(prompt_scores_read, L * NH + h - 1)
                        for t in range(2):
                            out = PS[:, h % 2, 128 * t:128 * t + 128 * (t + 1)]
                            last = te.matmul(out, qt[r, 128 * t:128 * t + 128], kt[r, 0:128 * (t + 1)], start=True, stop=moba)
                            if not moba:
                                e = h - AH
                                last = te.matmul(out, ident[0:BH, e:e + 1].to_broadcast([BH, 128]), ncn[:, 0:128 * (t + 1)], start=False, stop=True)
                        last.then_inc(prompt_scores_ready, 1)
                    if 2 <= h <= NH + 1:
                        n = h - 2
                        te.wait_ge(prompt_probs_ready, L * 2 * NH + 2 * n + 2)
                        if n >= 2:
                            te.wait_ge(prompt_probs_copied, L * NH + n - 1)
                        for t in range(3):
                            last = te.transpose(PS[:, 2 + n % 2, 128 * t:128 * t + 128], probs[n % 4][:, 128 * t:128 * t + 128], ident)
                        last.then_inc(prompt_probs_turned, 1)
                    if h >= 3:
                        n = h - 3
                        moba = n < AH
                        e = n if moba else n - AH
                        pr = n // 2 if n < 10 else 5
                        hf = n % 2 if n < 10 else 1
                        te.wait_ge(prompt_probs_copied, L * NH + n + 1)
                        if pr >= 2 and (n % 2 == 0):
                            te.wait_ge(prompt_out_copied, L * 6 + pr - 1)
                        settle(te)
                        g, c0 = (1, 64 * e) if moba else (3, HCOL[e])
                        out = PS[64 * hf:64 * hf + 64, 4 + pr % 2, 0:SEQ]
                        te.matmul(out, tok(0)[:, g * 384 + c0:g * 384 + c0 + 64], probs_t[n % 2][:, 0:256], start=True, stop=True)
                        te.matmul(out[:, 128:256], tok(1)[:, g * 384 + c0:g * 384 + c0 + 64], probs_t[n % 2][:, 256:384], start=False, stop=True,
                                  skip_group_check=True).then_inc(prompt_out_ready, 1)
                te.wait_ge(rec_qk_ready, L + 1)
                te.wait_ge(prompt_out_copied, L * 6 + 6)
                for n in range(9):
                    if n >= 2:
                        te.wait_ge(level_products_taken, L * 8 + n - 1)
                    if n >= 1:
                        te.wait_ge(level_factors_ready, L * 8 + n)
                    settle(te)
                    bk = 4 * (n % 2)
                    for at, h in enumerate(ORD):
                        j, hf = HEADS5[h]
                        r = slice(64 * hf, 64 * hf + 64)
                        if n == 0:
                            kk, qq = pt(T["fc"] + j), pt(T["qc"] + j)
                        else:
                            kk = qq = V_(4 if n % 2 == 1 else 0, j)
                        if n < 8:
                            for t in range(2):
                                c = 256 * (at % 2) + 128 * t
                                last = te.matmul(PS[:, bk + at // 2, c:c + 128],
                                                 kk[r, 128 * t:128 * t + 128], qq[r, 128 * t:128 * t + 128], start=True, stop=True)
                            if n < 4:
                                c = NS * at if at < 2 else 256 + NS * (at - 2)
                                last = te.matmul(PS[0:NS, bk + (3 if at < 2 else 2), c:c + NS], kk[r, SEQ:NT], qq[r, SEQ:NT], start=True, stop=True)
                        else:
                            c = 128 * (at if at < 2 else at - 2)
                            last = te.matmul(PS[:, bk + (0 if at < 2 else 1), c:c + 128], kk[r, 0:128], qq[r, 128:256], start=True, stop=True)
                    last.then_inc(level_products_ready, 1)
                te.wait_ge(end_keys_ready, L + 1)
                te.wait_ge(level_products_taken, L * 8 + 8)
                for tt in range(2):
                    for j in range(3):
                        last = te.transpose(PS[:, 4 + tt, 128 * j:128 * j + 128], V_(1, j)[:, 128 * tt:128 * tt + 128], ident)
                    last.then_inc(end_keys_turned, 1)
                for j in range(3):
                    last = te.matmul(PS[0:NS, 6, 128 * j:128 * j + 128], V_(1, j)[:, SEQ:NT], ident, start=True, stop=True)
                last.then_inc(end_keys_turned, 1)
                te.wait_ge(cross_products_copied, L * 2 + 2)
                te.wait_ge(states_in, L * 48 + 48)
                for j, hf, h in VH:
                    r = slice(64 * hf, 64 * hf + 64)
                    c = 4 * 384 + 128 * j + 64 * hf
                    o, at = PS[r, j, :], ORD.index(h)
                    te.matmul(o[:, 0:128], tok(0)[:, c:c + 64], a_blocks[:, at, 0:128], start=True, stop=True)
                    te.matmul(o[:, 128:256], tok(0)[:, c:c + 64], a_cross[:, at, :], start=True, stop=False)
                    te.matmul(o[:, 128:256], tok(1)[:, c:c + 64], a_blocks[:, at, 128:256], start=False, stop=True)
                    last = te.matmul(o[:, 256:320], toks[0:NS, c:c + 64], a_samples[:, at, :], start=True, stop=False, skip_group_check=True)
                last.then_inc(rec_own_sums_done, 1)
                te.wait_ge(rec_own_sums_done, L + 1)
                settle(te)
                for j, hf, h in VH:
                    r = slice(64 * hf, 64 * hf + 64)
                    o = PS[r, j, :]
                    for q in range(DB):
                        last = te.matmul(o[:, 256 + 8 * q:264 + 8 * q], states[r, j, q, :], q_decayed[r, j, 8 * q:8 * q + 8], start=False, stop=q == DB - 1, skip_group_check=True)
                last.then_inc(rec_out_ready, 1)
                te.wait_ge(end_keys_copied, L * 3 + 3)
                settle(te)
                for e, (j, hf) in enumerate(HEADS5):
                    r = slice(64 * hf, 64 * hf + 64)
                    for tt in range(2):
                        last = te.matmul(PS[r, 7, 64 * j:64 * j + 64], end_keys_t[:, tt, HCOL[e]:HCOL[e] + 64], tok(tt)[:, 4 * 384 + HCOL[e]:4 * 384 + HCOL[e] + 64],
                                         start=tt == 0, stop=tt == 1)
                last.then_inc(prompt_state_ready, 1)
                for e, (j, hf) in enumerate(HEADS5):
                    r = slice(64 * hf, 64 * hf + 64)
                    te.wait_ge(spread_values_ready, L * CH + e + 1)
                    settle(te)
                    vx = [b[0][0:NS, 0:512], P[0:NS, T["qc"] * NT:T["qc"] * NT + 512]][e % 2]
                    te.matmul(PS[r, 4 + j, :], end_keys_t[0:NS, 2, HCOL[e]:HCOL[e] + 64], vx, start=True, stop=True).then_inc(state_products_ready, 1)
                te.wait_ge(rec_squares_ready, L + 1)
                te.wait_ge(sample_states_done, L * 3 + 3)
                for j in range(3):
                    last = te.matmul(PS[:, 4 + j, 0:NT], cst("blk"), V_(4, j), start=True, stop=True)
                last.then_inc(rec_mean_squares_ready, 1)
                te.wait_ge(decode_queries_ready, L + 1)
                te.wait_ge(rec_rstd_ready, L + 1)
                settle(te)
                for pr in range(6):
                    t = pt((T["ka"] if pr < 3 else T["kf"]) + pr % 3)[:, SEQ:NT]
                    last = te.matmul(PS[0:NS, 4 + pr // 4, 128 * (pr % 4):128 * (pr % 4) + 128], t,
                                     qb[:, pr, :, :].rearrange("p b c -> p (b c)"), start=True, stop=True)
                last.then_inc(new_scores_ready, 1)
                te.wait_ge(new_scores_masked, L + 1)
                settle(te)
                for b_ in range(DB):
                    last = te.transpose(PS[0:ROWS, 6, 64 * b_:64 * b_ + 64], newb[:, b_, :], ident[0:NS, 0:NS])
                last.then_inc(new_scores_turned, 1)
                te.wait_ge(decode_ready, L + 1)
                settle(te)
                PAIRS = (0, 128, 256, AW, AW + 128, AW + 192)

                def turn_page(Q, pg):
                    s = pg % 4
                    te.wait_ge(k_in[s], (Q * 2 + pg // 4) * 32 + 32)
                    te.wait_ge(keys_hi_copied, Q * NPG + pg + 1)
                    te.wait_ge(keys_lo_copied, Q * NPG + pg + 1)
                    for j, c in enumerate(PAIRS):
                        last = te.transpose(PS[:, 2 * (pg % 2) + j // 3, 128 * (j % 3):128 * (j % 3) + 128], key_pages[:, s, c:c + 128], ident)
                    last.then_inc(keys_turned, 1)

                def block_scores(Q, n, softmax):
                    if n == 0:
                        te.wait_ge(seq_queries_ready, Q + 1)
                        if softmax:
                            te.wait_ge(weights_ready, Q * 5)
                    te.wait_ge(keys_hi_copied, Q * NPG + 2 * n + 4)
                    te.wait_ge(keys_lo_copied, Q * NPG + 2 * n + 4)
                    o = PS[0:ROWS, 4 + n // 2, 256 * (n % 2):256 * (n % 2) + 256]
                    for m in range(2):
                        te.matmul(o, sel[:, :], brow[m][:, 256 * n:256 * n + 256], start=m == 0, stop=False)
                    for pr in range(6):
                        for m, (zq, k) in enumerate(((0, 0), (1, 0), (0, 1))):
                            last = te.matmul(o, qz[zq][:, pr, :], key_halves[k][n % 2][:, pr, :], start=False, stop=pr == 5 and m == 2)
                    last.then_inc(block_scores_done, 1)

                def turn_weights(Q):
                    te.wait_ge(weights_ready, Q * 5 + 5)
                    for g in range(9):
                        last = te.transpose(PS[:, g // 5, 88 * (g % 5):88 * (g % 5) + 88], weight_rows[:, 128 * g:128 * g + 128], ident[0:ROWS, 0:ROWS])
                        if g in (4, 8):
                            last.then_inc(weights_turned, 1)

                def values(Q):
                    te.wait_ge(weights_copied_act, Q + 1)
                    te.wait_ge(weights_copied_dve, Q + 1)
                    te.wait_ge(outputs_copied, Q * 11 + 4)
                    for g in range(NPG):
                        te.wait_ge(v_in[g], Q * 32 + 32)
                        te.matmul(PS[0:ROWS, 6, 0:AW], weight_cols[:, g, :], value_pages[:, g, 0:AW], start=g == 0, stop=False, skip_group_check=True)
                        te.matmul(PS[0:ROWS, 7, 0:BW], weight_cols[:, g, :], value_pages[:, g, AW:AW + BW], start=g == 0, stop=False, skip_group_check=True
                                  ).then_inc(values_used, 1)
                    p, v = weight_cols[0:NS, NPG, :], toks[0:NS, :]
                    te.matmul(PS[0:ROWS, 6, 0:AW], p, v[:, 384:384 + AW], start=False, stop=True, skip_group_check=True)
                    te.matmul(PS[0:ROWS, 7, 0:256], p, v[:, 3 * 384:3 * 384 + 256], start=False, stop=True, skip_group_check=True)
                    te.matmul(PS[0:ROWS, 7, 256:320], p, v[:, 3 * 384 + 320:3 * 384 + 384], start=False, stop=True, skip_group_check=True
                              ).then_inc(value_sums_ready, 1)

                def turn_outputs(Q):
                    te.wait_ge(outputs_scaled, Q + 1)
                    for pr, c in enumerate(PAIRS):
                        last = te.transpose(PS[:, 6 + pr // 5, 88 * (pr % 5):88 * (pr % 5) + 88], out_rows[:, c:c + 128], ident[0:ROWS, 0:ROWS])
                    last.then_inc(outputs_turned, 1)

                def step(Q, softmax, products):
                    if products:
                        te.wait_ge(weights_copied_act, Q - 1)
                        te.wait_ge(weights_copied_dve, Q - 1)
                    turn_page(Q, 0)
                    turn_page(Q, 1)
                    if products:
                        values(Q - 2)
                    turn_page(Q, 2)
                    turn_page(Q, 3)
                    block_scores(Q, 0, softmax)
                    if products:
                        turn_outputs(Q - 2)
                    for n in range(1, 4):
                        if n < 3:
                            turn_page(Q, 2 * n + 2)
                            turn_page(Q, 2 * n + 3)
                        block_scores(Q, n, softmax)
                        if n == 2 and softmax:
                            te.wait_ge(keys_hi_copied, Q * NPG + 9)
                            te.wait_ge(keys_lo_copied, Q * NPG + 9)
                            turn_weights(Q - 1)

                step(L * DB, False, False)
                step(L * DB + 1, True, False)
                with te.Fori(2, DB) as q:
                    step(L * DB + q, True, True)
                Q = L * DB + DB - 1
                values(Q - 1)
                turn_outputs(Q - 1)
                turn_weights(Q)
                values(Q)
                turn_outputs(Q)
                settle(te)
                with te.Fori(0, 2) as m:
                    for dp in range(2):
                        for s in range(2):
                            chunk(s, L * USES + OFF["wout"] + m * 2 + dp)
                            if s == 0:
                                kts = [(k, k, ALLR) for k in range(5)] + [(5, 5, slice(64, 128))]
                            else:
                                kts = [(0, 6, ALLR), (1, 7, ALLR), (2, 8, slice(64, 128))]
                            for j in range(2):
                                if s == 0:
                                    te.wait_ge(acc_used, L * 24 + 8 + m * 4 + 2 * dp + j + 1)
                                last = dense(PS[:, 4 + 2 * dp + j, 0:NT], s, slice(128 * j, 128 * j + 128), (xh, xl), kts, s == 0, s == 1,
                                             (out_lo_ready, L * 9 + 6 * s) if dp == 0 and j == 0 else None)
                                if j == 1:
                                    last.then_inc(w_free[s], 1)
                                elif s == 1:
                                    last.then_inc(acc_ready, 1)
                norm(L * 3 + 2)
                ffn(1, L, L * 3 + 2)
            norm(DEPTH * 3)
            te.wait_ge(xs_ready, DEPTH * 3 * KT_D + KT_D)
            for n in range(6):
                tt, hf = divmod(n, 2)
                for k in range(4):
                    at = (4 * hf + k) * NT + tt * 128
                    last = te.transpose(PS[:, n, 128 * k:128 * k + 128], X[:, at:at + 128], ident)
                last.then_inc(y_turned, 1)


INS = ["x_prompt", "x_sample", "cache_moba_k", "cache_moba_v", "cache_fox_k", "cache_fox_v", "cache_fox_logf", "state_hgrn",
       "page_table", "norm_ffn1_g", "ffn1_w_gate", "ffn1_w_up", "ffn1_w_down", "norm_mix_g", "w_in", "fox_f_bias",
       "hgrn_lb_logits", "hgrn_norm_g", "w_out", "norm_ffn2_g", "ffn2_w_gate", "ffn2_w_up", "ffn2_w_down", "norm_final_g"]
OUTS = [("y_prompt", (1, SEQ, D)), ("y_sample", (DB, DS, D)),
        ("moba_k_prompt", (DEPTH, 1, SEQ, AH, HD)), ("moba_v_prompt", (DEPTH, 1, SEQ, AH, HD)),
        ("fox_k_prompt", (DEPTH, 1, SEQ, BH, HD)), ("fox_v_prompt", (DEPTH, 1, SEQ, BH, HD)),
        ("fox_logf_prompt", (DEPTH, 1, SEQ, BH)), ("hgrn_state_prompt", (DEPTH, 1, CH, HD, HD)),
        ("moba_k_sample", (DEPTH, DB, DS, AH, HD)), ("moba_v_sample", (DEPTH, DB, DS, AH, HD)),
        ("fox_k_sample", (DEPTH, DB, DS, BH, HD)), ("fox_v_sample", (DEPTH, DB, DS, BH, HD)),
        ("fox_logf_sample", (DEPTH, DB, DS, BH)), ("hgrn_state_sample", (DEPTH, DB, CH, HD, HD))]


def kernel(**inputs):
    import concourse.bacc as bacc
    from concourse.bass_utils import run_bass_kernel_spmd

    nc = bacc.Bacc("TRN2", target_bir_lowering=False, num_devices=1)
    arrays, a = {}, {}
    for name in INS + ["consts"]:
        v = constants() if name == "consts" else np.ascontiguousarray(inputs[name])
        arrays["in_" + name] = v
        a[name] = nc.dram_tensor("in_" + name, v.shape, mybir.dt.from_np(v.dtype), kind="ExternalInput").ap()
    outs = {n: nc.dram_tensor("out_" + n, s, F32, kind="ExternalOutput").ap() for n, s in OUTS}
    trunk(nc, a, outs)
    r = run_bass_kernel_spmd(nc, [arrays], core_ids=[0])
    return tuple(r.results[0]["out_" + n] for n, _ in OUTS)
```
